# Optimizing a Trainium2 kernel written in Bass

```python
import math
import jax, jax.numpy as jnp
from jax import lax
import numpy as np

D_MODEL = 1024
BATCH = 1
SEQ = 256
DEPTH = 1

LRU_W = 256
LRU_BLOCKS = 4
LRU_BLOCK_W = LRU_W // LRU_BLOCKS
LRU_C = 8.0
CONV_W = 4
MLSTM_HEADS = 4
MLSTM_HEAD_DIM = 64
MLSTM_W = MLSTM_HEADS * MLSTM_HEAD_DIM
MLSTM_CHUNK = 64
SB_HEADS = 4
SB_HEAD_DIM = 64
SB_W = SB_HEADS * SB_HEAD_DIM
SB_BLOCK = 128
FF = ((8 * D_MODEL // 3 + 255) // 256) * 256
EPS = 1e-6

SPLIT_SIZES = (LRU_W, LRU_W, 2 * MLSTM_W, MLSTM_W, MLSTM_W, MLSTM_HEADS, MLSTM_HEADS,
               SB_W, SB_W, SB_W, D_MODEL, D_MODEL, D_MODEL)
IN_COLS = sum(SPLIT_SIZES)


def rmsnorm(x, g):
    xf = x.astype(jnp.float32)
    y = xf * lax.rsqrt(jnp.mean(xf * xf, axis=-1, keepdims=True) + EPS)
    return (y * g.astype(jnp.float32)).astype(x.dtype)

def causal_dwconv(x, w):
    K, C = w.shape
    return lax.conv_general_dilated(
        x, w.astype(x.dtype)[:, None, :], window_strides=(1,), padding=[(K - 1, 0)],
        dimension_numbers=("NWC", "WIO", "NWC"), feature_group_count=C)

def to_heads(t, n_heads):
    B, S, W = t.shape
    return t.reshape(B, S, n_heads, W // n_heads).transpose(0, 2, 1, 3)

def from_heads(t):
    B, H, S, d = t.shape
    return t.transpose(0, 2, 1, 3).reshape(B, S, H * d)

def rg_lru(xb, wa, ba, wx, bx, lam):
    B, S, W = xb.shape
    xf = xb.astype(jnp.float32)
    xh = xf.reshape(B, S, LRU_BLOCKS, LRU_BLOCK_W)
    r = jax.nn.sigmoid(jnp.einsum('bsgi,gij->bsgj', xh, wa.astype(jnp.float32)).reshape(B, S, W)
                       + ba.astype(jnp.float32))
    i = jax.nn.sigmoid(jnp.einsum('bsgi,gij->bsgj', xh, wx.astype(jnp.float32)).reshape(B, S, W)
                       + bx.astype(jnp.float32))
    log_a = -LRU_C * r * jax.nn.softplus(-lam.astype(jnp.float32))
    a = jnp.exp(log_a)
    u = jnp.sqrt(-jnp.expm1(2.0 * log_a)) * (i * xf)

    def combine(left, right):
        a1, b1 = left
        a2, b2 = right
        return a1 * a2, a2 * b1 + b2

    _, h = lax.associative_scan(combine, (a, u), axis=1)
    return h.astype(xb.dtype)

def mlstm_chunkwise(q, k, v, i_pre, f_pre):
    B, H, S, dk = q.shape
    dv = v.shape[-1]
    L = MLSTM_CHUNK
    nc = S // L
    out_dtype = v.dtype
    q = q.astype(jnp.float32)
    k = k.astype(jnp.float32) * (dk ** -0.5)
    v = v.astype(jnp.float32)
    logi = i_pre.astype(jnp.float32)
    logf = jax.nn.log_sigmoid(f_pre.astype(jnp.float32))

    def chunks(t):
        return jnp.moveaxis(t.reshape((B, H, nc, L) + t.shape[3:]), 2, 0)

    tril = jnp.tril(jnp.ones((L, L), dtype=bool))

    def step(carry, inp):
        C, n, m = carry
        qc, kc, vc, ic, fc = inp
        b = jnp.cumsum(fc, axis=-1)
        D = jnp.where(tril, b[..., :, None] - b[..., None, :] + ic[..., None, :], -jnp.inf)
        m_inter = b + m[..., None]
        m_t = jnp.maximum(jnp.max(D, axis=-1), m_inter)
        P = jnp.exp(D - m_t[..., None]) * jnp.einsum('bhtk,bhsk->bhts', qc, kc)
        decay = jnp.exp(m_inter - m_t)
        num = (jnp.einsum('bhts,bhsv->bhtv', P, vc)
               + decay[..., None] * jnp.einsum('bhvk,bhtk->bhtv', C, qc))
        den = jnp.sum(P, axis=-1) + decay * jnp.einsum('bhk,bhtk->bht', n, qc)
        h = num / jnp.maximum(jnp.abs(den), jnp.exp(-m_t))[..., None]
        bL = b[..., -1]
        g = bL[..., None] - b + ic
        m_new = jnp.maximum(bL + m, jnp.max(g, axis=-1))
        wts = jnp.exp(g - m_new[..., None])
        carry_decay = jnp.exp(bL + m - m_new)
        C = carry_decay[..., None, None] * C + jnp.einsum('bhs,bhsv,bhsk->bhvk', wts, vc, kc)
        n = carry_decay[..., None] * n + jnp.einsum('bhs,bhsk->bhk', wts, kc)
        return (C, n, m_new), h

    init = (jnp.zeros((B, H, dv, dk), jnp.float32), jnp.zeros((B, H, dk), jnp.float32),
            jnp.zeros((B, H), jnp.float32))
    _, hs = lax.scan(step, init, (chunks(q), chunks(k), chunks(v), chunks(logi), chunks(logf)))
    return jnp.moveaxis(hs, 0, 2).reshape(B, H, S, dv).astype(out_dtype)

def stick_breaking_attention(q, k, v):
    B, H, S, d = q.shape
    nb = S // SB_BLOCK
    scale = 1.0 / math.sqrt(d)
    loc = jnp.arange(SB_BLOCK)
    diag_mask = loc[None, :] < loc[:, None]
    outs = []
    for bi in range(nb):
        nk = bi + 1
        lk_len = nk * SB_BLOCK
        qblk = q[:, :, bi * SB_BLOCK:(bi + 1) * SB_BLOCK]
        kk = k[:, :, :lk_len]
        vv = v[:, :, :lk_len]
        z = jnp.einsum('bhqd,bhsd->bhqs', qblk, kk).astype(jnp.float32) * scale
        causal = jnp.concatenate(
            [jnp.ones((SB_BLOCK, lk_len - SB_BLOCK), dtype=bool), diag_mask], axis=1)
        log_keep = jnp.where(causal, jax.nn.log_sigmoid(-z), 0.0)
        intra = lax.cumsum(log_keep.reshape(B, H, SB_BLOCK, nk, SB_BLOCK), axis=4, reverse=True)
        bsum = intra[..., 0]
        inter = lax.cumsum(bsum, axis=3, reverse=True) - bsum
        R = (intra + inter[..., None]).reshape(B, H, SB_BLOCK, lk_len)
        A = jnp.where(causal, jnp.exp(z + R), 0.0)
        outs.append(jnp.einsum('bhqs,bhsd->bhqd', A.astype(v.dtype), vv))
    return jnp.concatenate(outs, axis=2)

def first_inputs(seed: int = 0) -> dict:
    key = jax.random.key(seed)
    ks = jax.random.split(key, 24)
    f32 = jnp.float32
    D = D_MODEL

    def nrm(k, shape, fan_in):
        return jax.random.normal(k, shape, f32) * (fan_in ** -0.5)

    a0 = jax.random.uniform(ks[8], (DEPTH, LRU_W), f32, 0.9, 0.999)
    s0 = a0 ** (1.0 / LRU_C)
    lru_lambda = jnp.log(s0) - jnp.log1p(-s0)
    fg_b = (jnp.linspace(3.0, 6.0, MLSTM_HEADS, dtype=f32)[None, :]
            + 0.1 * jax.random.normal(ks[11], (DEPTH, MLSTM_HEADS), f32))
    return {
        "x": jax.random.normal(ks[0], (BATCH, SEQ, D), f32),
        "norm_mix_g": 1.0 + 0.02 * jax.random.normal(ks[1], (DEPTH, D), f32),
        "w_in": nrm(ks[2], (DEPTH, D, IN_COLS), D),
        "conv_lru_w": nrm(ks[3], (DEPTH, CONV_W, LRU_W), CONV_W),
        "lru_wa": nrm(ks[4], (DEPTH, LRU_BLOCKS, LRU_BLOCK_W, LRU_BLOCK_W), LRU_BLOCK_W),
        "lru_ba": 0.02 * jax.random.normal(ks[5], (DEPTH, LRU_W), f32),
        "lru_wx": nrm(ks[6], (DEPTH, LRU_BLOCKS, LRU_BLOCK_W, LRU_BLOCK_W), LRU_BLOCK_W),
        "lru_bx": 0.02 * jax.random.normal(ks[7], (DEPTH, LRU_W), f32),
        "lru_lambda": lru_lambda,
        "conv_mlstm_w": nrm(ks[9], (DEPTH, CONV_W, 2 * MLSTM_W), CONV_W),
        "mlstm_ig_b": 0.1 * jax.random.normal(ks[10], (DEPTH, MLSTM_HEADS), f32),
        "mlstm_fg_b": fg_b,
        "w_out_lru": nrm(ks[12], (DEPTH, LRU_W, D), LRU_W),
        "w_out_mlstm": nrm(ks[13], (DEPTH, MLSTM_W, D), MLSTM_W),
        "w_out_sb": nrm(ks[14], (DEPTH, SB_W, D), SB_W),
        "w_o": nrm(ks[15], (DEPTH, D, D), D),
        "norm_ffn_g": 1.0 + 0.02 * jax.random.normal(ks[16], (DEPTH, D), f32),
        "w_ffn_in": nrm(ks[17], (DEPTH, D, 2 * FF), D),
        "w_ffn_out": nrm(ks[18], (DEPTH, FF, D), FF),
        "final_norm_g": 1.0 + 0.02 * jax.random.normal(ks[19], (D,), f32),
    }

def first_block(x, norm_mix_g, w_in, conv_lru_w, lru_wa, lru_ba, lru_wx, lru_bx, lru_lambda,
              conv_mlstm_w, mlstm_ig_b, mlstm_fg_b, w_out_lru, w_out_mlstm, w_out_sb, w_o,
              norm_ffn_g, w_ffn_in, w_ffn_out, final_norm_g):
    split_points = np.cumsum(SPLIT_SIZES)[:-1].tolist()
    for l in range(DEPTH):
        h = rmsnorm(x, norm_mix_g[l])
        proj = h @ w_in[l]
        (lru_x, lru_gate, m_qk, m_v, m_o, m_i, m_f,
         s_q, s_k, s_v, g_a, g_b, g_c) = jnp.split(proj, split_points, axis=-1)

        xa = causal_dwconv(lru_x, conv_lru_w[l])
        ya = rg_lru(xa, lru_wa[l], lru_ba[l], lru_wx[l], lru_bx[l], lru_lambda[l])
        ya = (ya * jax.nn.gelu(lru_gate)) @ w_out_lru[l]

        qk = jax.nn.silu(causal_dwconv(m_qk, conv_mlstm_w[l]))
        mq, mk = jnp.split(qk, 2, axis=-1)
        i_pre = (m_i + mlstm_ig_b[l]).transpose(0, 2, 1)
        f_pre = (m_f + mlstm_fg_b[l]).transpose(0, 2, 1)
        hb = mlstm_chunkwise(to_heads(mq, MLSTM_HEADS), to_heads(mk, MLSTM_HEADS),
                             to_heads(m_v, MLSTM_HEADS), i_pre, f_pre)
        yb = (jax.nn.sigmoid(m_o) * from_heads(hb)) @ w_out_mlstm[l]

        hc = stick_breaking_attention(to_heads(s_q, SB_HEADS), to_heads(s_k, SB_HEADS),
                                      to_heads(s_v, SB_HEADS))
        yc = from_heads(hc) @ w_out_sb[l]

        merged = (jax.nn.sigmoid(g_a) * ya + jax.nn.sigmoid(g_b) * yb
                  + jax.nn.sigmoid(g_c) * yc)
        x = x + merged @ w_o[l]

        hf = rmsnorm(x, norm_ffn_g[l])
        gate, up = jnp.split(hf @ w_ffn_in[l], 2, axis=-1)
        x = x + (jax.nn.silu(gate) * up) @ w_ffn_out[l]
    return rmsnorm(x, final_norm_g)


MIX_WIDTH = D_MODEL
HEAD_DIM = 64
A_WIDTH = D_MODEL // 4
B_WIDTH = D_MODEL // 2
C_WIDTH = D_MODEL // 4
A_HEADS = A_WIDTH // HEAD_DIM
B_HEADS = B_WIDTH // HEAD_DIM
C_GROUPS = C_WIDTH // HEAD_DIM
IN_COLS_2 = 2 * A_WIDTH + 3 * B_WIDTH + 2 * C_WIDTH
CHUNK = 128
MOBA_BLOCK = 256
MOBA_TOPK = 3
Q_BLK = 64
CONV_WIDTH = 31
MEM_LEN = 256
X_HEADS = 4
X_HEAD_DIM = D_MODEL // X_HEADS
D_FF = 4 * D_MODEL


def rms_norm(x, g):
    xf = x.astype(jnp.float32)
    y = xf * lax.rsqrt(jnp.mean(xf * xf, axis=-1, keepdims=True) + EPS)
    return (y * g.astype(jnp.float32)).astype(x.dtype)

def layer_norm(x, g, b):
    xf = x.astype(jnp.float32)
    mu = jnp.mean(xf, axis=-1, keepdims=True)
    xc = xf - mu
    var = jnp.mean(xc * xc, axis=-1, keepdims=True)
    y = xc * lax.rsqrt(var + EPS) * g.astype(jnp.float32) + b.astype(jnp.float32)
    return y.astype(x.dtype)

def alibi_slopes(n_heads):
    return 2.0 ** (-8.0 * jnp.arange(1, n_heads + 1, dtype=jnp.float32) / n_heads)

def spatial_gating(z, ln_g, ln_b, w_s, b_s):
    Bn, S, _ = z.shape
    u, v = jnp.split(z, 2, axis=-1)
    v = layer_norm(v, ln_g, ln_b)
    v = v.reshape(Bn, S // CHUNK, CHUNK, A_HEADS, HEAD_DIM)
    causal = jnp.tril(jnp.ones((CHUNK, CHUNK), dtype=w_s.dtype))
    w = (w_s * causal[None]).astype(v.dtype)
    mixed = jnp.einsum('hts,bcshd->bcthd', w, v) + b_s.T.astype(v.dtype)[None, None, :, :, None]
    return u * mixed.reshape(Bn, S, A_WIDTH)

def moba_attention(q, k, v):
    Bn, H, S, Dh = q.shape
    s_pad = -(-S // MOBA_BLOCK) * MOBA_BLOCK
    pad = ((0, 0), (0, 0), (0, s_pad - S), (0, 0))
    q, k, v = jnp.pad(q, pad), jnp.pad(k, pad), jnp.pad(v, pad)
    nb = s_pad // MOBA_BLOCK
    kk = min(MOBA_TOPK, nb)
    n_q = s_pad // Q_BLK
    scale = Dh ** -0.5
    slopes = alibi_slopes(H)
    kb = k.reshape(Bn, H, nb, MOBA_BLOCK, Dh)
    vb = v.reshape(Bn, H, nb, MOBA_BLOCK, Dh)
    kmean = jnp.mean(kb.astype(jnp.float32), axis=3)
    qc = q.reshape(Bn, H, n_q, Q_BLK, Dh).transpose(2, 0, 1, 3, 4)
    bi = jnp.arange(Bn)[:, None, None, None]
    hi = jnp.arange(H)[None, :, None, None]
    offs = jnp.arange(MOBA_BLOCK)

    def one_block(args):
        qi, ci = args
        t = ci * Q_BLK + jnp.arange(Q_BLK)
        own = (ci * Q_BLK) // MOBA_BLOCK
        gate = jnp.einsum('bhqd,bhnd->bhqn', qi.astype(jnp.float32), kmean)
        gate = jnp.where(jnp.arange(nb) < own, gate, -jnp.inf)
        _, idx = lax.top_k(gate, kk)
        valid = idx < own
        ksel = kb[bi, hi, idx]
        vsel = vb[bi, hi, idx]
        s_past = jnp.einsum('bhqd,bhqkld->bhqkl', qi, ksel).astype(jnp.float32) * scale
        kpos = idx[..., None] * MOBA_BLOCK + offs
        dist = (t[None, None, :, None, None] - kpos).astype(jnp.float32)
        s_past = jnp.where(valid[..., None], s_past - slopes[None, :, None, None, None] * dist, -jnp.inf)
        k_own = lax.dynamic_index_in_dim(kb, own, axis=2, keepdims=False)
        v_own = lax.dynamic_index_in_dim(vb, own, axis=2, keepdims=False)
        s_own = jnp.einsum('bhqd,bhld->bhql', qi, k_own).astype(jnp.float32) * scale
        kpos_own = own * MOBA_BLOCK + offs
        dist_own = (t[:, None] - kpos_own[None, :]).astype(jnp.float32)
        s_own = jnp.where((dist_own >= 0)[None, None],
                          s_own - slopes[None, :, None, None] * dist_own[None, None], -jnp.inf)
        s_all = jnp.concatenate([s_past.reshape(Bn, H, Q_BLK, kk * MOBA_BLOCK), s_own], axis=-1)
        p = jax.nn.softmax(s_all, axis=-1).astype(v.dtype)
        p_past = p[..., :kk * MOBA_BLOCK].reshape(Bn, H, Q_BLK, kk, MOBA_BLOCK)
        p_own = p[..., kk * MOBA_BLOCK:]
        return (jnp.einsum('bhqkl,bhqkld->bhqd', p_past, vsel)
                + jnp.einsum('bhql,bhld->bhqd', p_own, v_own))

    out = lax.map(one_block, (qc, jnp.arange(n_q, dtype=jnp.int32)))
    out = out.transpose(1, 0, 3, 2, 4).reshape(Bn, s_pad, H * Dh)
    return out[:, :S]

def conformer_conv(z, w_dw, b_dw, gn_g, gn_b):
    Bn, S, _ = z.shape
    a, g = jnp.split(z, 2, axis=-1)
    y = a * jax.nn.sigmoid(g)
    rhs = w_dw.astype(y.dtype)[:, None, :]
    y = lax.conv_general_dilated(y, rhs, window_strides=(1,), padding=[(CONV_WIDTH - 1, 0)],
                                 dimension_numbers=('NWC', 'WIO', 'NWC'),
                                 feature_group_count=C_WIDTH)
    y = y + b_dw.astype(y.dtype)
    y = y.reshape(Bn, S, C_GROUPS, HEAD_DIM)
    y = layer_norm(y, gn_g.reshape(C_GROUPS, HEAD_DIM), gn_b.reshape(C_GROUPS, HEAD_DIM))
    return jax.nn.silu(y.reshape(Bn, S, C_WIDTH))

def memory_cross_attention(h, m, w_q, w_kv, w_o):
    Bn, S, _ = h.shape
    M = m.shape[1]
    q = (h @ w_q).reshape(Bn, S, X_HEADS, X_HEAD_DIM)
    k, v = jnp.split(m @ w_kv, 2, axis=-1)
    k = k.reshape(Bn, M, X_HEADS, X_HEAD_DIM)
    v = v.reshape(Bn, M, X_HEADS, X_HEAD_DIM)
    s = jnp.einsum('bshd,bmhd->bhsm', q, k).astype(jnp.float32) * (X_HEAD_DIM ** -0.5)
    p = jax.nn.softmax(s, axis=-1).astype(v.dtype)
    o = jnp.einsum('bhsm,bmhd->bshd', p, v).reshape(Bn, S, D_MODEL)
    return o @ w_o

def second_inputs(seed: int = 0) -> dict:
    key = jax.random.key(seed)
    ks = jax.random.split(key, 24)
    f32 = jnp.float32
    L = DEPTH

    def nrm(k, shape, scale):
        return jax.random.normal(k, shape, f32) * scale

    def gain(k, shape):
        return 1.0 + 0.05 * jax.random.normal(k, shape, f32)

    return {
        "x": nrm(ks[0], (BATCH, SEQ, D_MODEL), 1.0),
        "mem": nrm(ks[1], (BATCH, MEM_LEN, D_MODEL), 1.0),
        "pre_mix_g": gain(ks[2], (L, D_MODEL)),
        "w_in": nrm(ks[3], (L, D_MODEL, IN_COLS_2), D_MODEL ** -0.5),
        "gate_ln_g": gain(ks[4], (L, A_WIDTH)),
        "gate_ln_b": nrm(ks[5], (L, A_WIDTH), 0.02),
        "w_s": nrm(ks[6], (L, A_HEADS, CHUNK, CHUNK), CHUNK ** -0.5),
        "b_s": nrm(ks[7], (L, A_HEADS, CHUNK), 0.02),
        "w_dw": nrm(ks[8], (L, CONV_WIDTH, C_WIDTH), CONV_WIDTH ** -0.5),
        "b_dw": nrm(ks[9], (L, C_WIDTH), 0.02),
        "conv_gn_g": gain(ks[10], (L, C_WIDTH)),
        "conv_gn_b": nrm(ks[11], (L, C_WIDTH), 0.02),
        "w_out": nrm(ks[12], (L, MIX_WIDTH, D_MODEL), MIX_WIDTH ** -0.5),
        "post_mix_g": gain(ks[13], (L, D_MODEL)),
        "pre_x_g": gain(ks[14], (L, D_MODEL)),
        "mem_g": gain(ks[15], (L, D_MODEL)),
        "w_xq": nrm(ks[16], (L, D_MODEL, D_MODEL), D_MODEL ** -0.5),
        "w_xkv": nrm(ks[17], (L, D_MODEL, 2 * D_MODEL), D_MODEL ** -0.5),
        "w_xo": nrm(ks[18], (L, D_MODEL, D_MODEL), D_MODEL ** -0.5),
        "post_x_g": gain(ks[19], (L, D_MODEL)),
        "pre_ffn_g": gain(ks[20], (L, D_MODEL)),
        "w_ff1": nrm(ks[21], (L, D_MODEL, D_FF), D_MODEL ** -0.5),
        "w_ff2": nrm(ks[22], (L, D_FF, D_MODEL), D_FF ** -0.5),
        "post_ffn_g": gain(ks[23], (L, D_MODEL)),
    }

def second_block(x, mem, pre_mix_g, w_in, gate_ln_g, gate_ln_b, w_s, b_s, w_dw, b_dw,
              conv_gn_g, conv_gn_b, w_out, post_mix_g, pre_x_g, mem_g, w_xq, w_xkv,
              w_xo, post_x_g, pre_ffn_g, w_ff1, w_ff2, post_ffn_g):
    Bn, S, _ = x.shape
    split_a = 2 * A_WIDTH
    split_b = split_a + 3 * B_WIDTH
    for l in range(DEPTH):
        h = rms_norm(x, pre_mix_g[l])
        z = h @ w_in[l]
        za, zb, zc = z[..., :split_a], z[..., split_a:split_b], z[..., split_b:]
        ya = spatial_gating(jax.nn.gelu(za, approximate=False),
                            gate_ln_g[l], gate_ln_b[l], w_s[l], b_s[l])
        q, k, v = jnp.split(zb, 3, axis=-1)
        q, k, v = (a.reshape(Bn, S, B_HEADS, HEAD_DIM).transpose(0, 2, 1, 3) for a in (q, k, v))
        yb = moba_attention(q, k, v)
        yc = conformer_conv(zc, w_dw[l], b_dw[l], conv_gn_g[l], conv_gn_b[l])
        y = jnp.concatenate([ya, yb, yc], axis=-1) @ w_out[l]
        x = x + rms_norm(y, post_mix_g[l])
        h = rms_norm(x, pre_x_g[l])
        m = rms_norm(mem, mem_g[l])
        x = x + rms_norm(memory_cross_attention(h, m, w_xq[l], w_xkv[l], w_xo[l]), post_x_g[l])
        h = rms_norm(x, pre_ffn_g[l])
        f = jnp.square(jax.nn.relu(h @ w_ff1[l])) @ w_ff2[l]
        x = x + rms_norm(f, post_ffn_g[l])
    return x


def setup_inputs(seed=0):
    out = dict(first_inputs(seed))
    for name, value in second_inputs(seed + 1).items():
        if name != "x":
            out[name + "_2"] = value
    return out


def reference(
    x, norm_mix_g, w_in, conv_lru_w, lru_wa, lru_ba, lru_wx, lru_bx, lru_lambda, conv_mlstm_w,
    mlstm_ig_b, mlstm_fg_b, w_out_lru, w_out_mlstm, w_out_sb, w_o, norm_ffn_g, w_ffn_in,
    w_ffn_out, final_norm_g, mem_2, pre_mix_g_2, w_in_2, gate_ln_g_2, gate_ln_b_2, w_s_2, b_s_2,
    w_dw_2, b_dw_2, conv_gn_g_2, conv_gn_b_2, w_out_2, post_mix_g_2, pre_x_g_2, mem_g_2, w_xq_2,
    w_xkv_2, w_xo_2, post_x_g_2, pre_ffn_g_2, w_ff1_2, w_ff2_2, post_ffn_g_2,
):
    x = first_block(
        x, norm_mix_g, w_in, conv_lru_w, lru_wa, lru_ba, lru_wx, lru_bx, lru_lambda,
        conv_mlstm_w, mlstm_ig_b, mlstm_fg_b, w_out_lru, w_out_mlstm, w_out_sb, w_o, norm_ffn_g,
        w_ffn_in, w_ffn_out, final_norm_g,
    )
    return second_block(
        x, mem_2, pre_mix_g_2, w_in_2, gate_ln_g_2, gate_ln_b_2, w_s_2, b_s_2, w_dw_2, b_dw_2,
        conv_gn_g_2, conv_gn_b_2, w_out_2, post_mix_g_2, pre_x_g_2, mem_g_2, w_xq_2, w_xkv_2,
        w_xo_2, post_x_g_2, pre_ffn_g_2, w_ff1_2, w_ff2_2, post_ffn_g_2,
    )


_drawn_inputs = setup_inputs


def setup_inputs(seed=0):
    import zlib

    import numpy as np

    out = dict(_drawn_inputs(seed))
    spreads = {}
    factors = {'norm_mix_g': 3.277,
     'lru_ba': 8.0,
     'lru_bx': 8.0,
     'mlstm_ig_b': 8.0,
     'norm_ffn_g': 3.388,
     'gate_ln_g_2': 3.015,
     'gate_ln_b_2': 7.552,
     'b_s_2': 5.675,
     'b_dw_2': 2.877,
     'conv_gn_b_2': 5.012}
    for name, (base, spread) in spreads.items():
        noise = np.random.default_rng([zlib.crc32(name.encode()), seed]).standard_normal(out[name].shape)
        drawn = base * np.exp(spread * noise) if base else spread * noise
        out[name] = __import__('jax').numpy.asarray(drawn.astype(out[name].dtype))
    for name, factor in factors.items():
        out[name] = (out[name] * factor).astype(out[name].dtype)
    return out
```

```python
from contextlib import ExitStack
import math

import concourse.bass as bass
from concourse import mybir

P = 128
T = 256
TT = T // P
D = 1024
KD = D // P
F1 = 2816
F2 = 4096
NB = 512
EPS = 1e-6
RAW = 3
SPLIT = 3
ARENA = 18700
LEAD = 2
GROUP = 2048
DIAG = 3 * P

F32 = mybir.dt.float32
F32R = mybir.dt.float32r
ALU = mybir.AluOpType
ACT = mybir.ActivationFunctionType
AX = mybir.AxisListType

VEC_A = [("norm_mix_g", 8), ("norm_ffn_g", 8), ("pre_mix_g_2", 8), ("mem_g_2", 8), ("pre_x_g_2", 8),
         ("pre_ffn_g_2", 8), ("lru_ba", 2), ("lru_bx", 2), ("lru_lambda", 2), ("conv_lru_w", 8),
         ("conv_mlstm_w", 16), ("b_dw_2", 2), ("conv_gn_g_2", 2), ("conv_gn_b_2", 2), ("b_s_2", 4)]
VEC_OFF = {}
_n = 0
for _name, _rows in VEC_A:
    VEC_OFF[_name] = _n
    _n += _rows
VEC_ROWS = _n
DW_TAPS = 31
DW_ROWS = 2 * DW_TAPS


def plan_weights(w):
    groups, chunks = [], {}

    def add(key, src, row0, kts, cols, view):
        ids = []
        per = GROUP // view
        for k in range(0, kts, per):
            nk = min(per, kts - k)
            dmas = [(src, row0 + k * P, nk, d, c, n) for d, c, n in cols]
            groups.append((dmas, view, nk, max(d + n for d, _, n in cols)))
            ids.append((len(groups) - 1, list(range(k, k + nk))))
        chunks[key] = ids

    win = w["w_in"]
    for key, cols in (("lru", [(0, 0, 512)]), ("qk", [(0, 512, 512)]), ("ifsv", [(0, 1536, 8), (8, 2056, 256)]),
                      ("vo", [(0, 1024, 512)]), ("sqk", [(0, 1544, 512)])):
        add(key, win, 0, KD, cols, NB)
    for c in range(6):
        add(("gate", c), win, 0, KD, [(0, 2312 + c * NB, NB)], NB)
    for b, name in enumerate(("w_out_lru", "w_out_mlstm", "w_out_sb")):
        add(("branch", b), w[name], 0, 2, [(0, 0, D)], D)
    for c in range(2):
        add(("wo", c), w["w_o"], 0, KD, [(0, c * NB, NB)], NB)
    n1 = F1 // 256
    for c in range(n1 + 1):
        if c < n1:
            add(("up1", c), w["w_ffn_in"], 0, KD, [(0, c * 256, 256), (256, F1 + c * 256, 256)], NB)
        if c >= 1:
            add(("down1", c - 1), w["w_ffn_out"], (c - 1) * 256, 2, [(0, 0, D)], D)
    for key, c in (("za", 0), ("q2", 512), ("k2", 1024), ("zc", 2048), ("v2", 1536)):
        add(key, w["w_in_2"], 0, KD, [(0, c, NB)], NB)
    for c in range(4):
        add(("kv", c), w["w_xkv_2"], 0, KD, [(0, c * NB, NB)], NB)
    for c in range(2):
        add(("mixout", c), w["w_out_2"], 0, KD, [(0, c * NB, NB)], NB)
    for c in range(2):
        add(("xq", c), w["w_xq_2"], 0, KD, [(0, c * NB, NB)], NB)
    for c in range(2):
        add(("xo", c), w["w_xo_2"], 0, KD, [(0, c * NB, NB)], NB)
    n2 = F2 // NB
    for c in range(n2 + 1):
        if c < n2:
            add(("up2", c), w["w_ff1_2"], 0, KD, [(0, c * NB, NB)], NB)
        if c >= 1:
            add(("down2", c - 1), w["w_ff2_2"], (c - 1) * NB, 4, [(0, 0, D)], D)
    return groups, chunks


class Semaphores:

    def __init__(self, new):
        self.act_h = new("act_h")
        self.act_hl = new("act_hl")
        self.act_step = new("act_step")
        self.bias_in = new("bias_in")
        self.cols = new("cols")
        self.cols_turned = new("cols_turned")
        self.consts = new("consts")
        self.conv_done = new("conv_done")
        self.dist = new("dist")
        self.dve_step = new("dve_step")
        self.dw_in = new("dw_in")
        self.exp_m = new("exp_m")
        self.gate_in = new("gate_in")
        self.gate_w = new("gate_w")
        self.gn_mean = new("gn_mean")
        self.gn_sd = new("gn_sd")
        self.gn_sq = new("gn_sq")
        self.gn_t = new("gn_t")
        self.gn_var = new("gn_var")
        self.gn_z = new("gn_z")
        self.hid_a = new("hid_a")
        self.hid_h = new("hid_h")
        self.hid_hl = new("hid_hl")
        self.hid_t = new("hid_t")
        self.ident = new("ident")
        self.if_rows = new("if_rows")
        self.if_turned = new("if_turned")
        self.ifsv_in = new("ifsv_in")
        self.kv_in = new("kv_in")
        self.lam_e = new("lam_e")
        self.ln_in = new("ln_in")
        self.ln_rstd = new("ln_rstd")
        self.ln_stat = new("ln_stat")
        self.log_f = new("log_f")
        self.low_by_dve = new("low_by_dve")
        self.low_by_pool = new("low_by_pool")
        self.lru_cols = new("lru_cols")
        self.lru_conv = new("lru_conv")
        self.lru_gelu = new("lru_gelu")
        self.lru_in = new("lru_in")
        self.lru_sqrt = new("lru_sqrt")
        self.lru_t = new("lru_t")
        self.lru_tg = new("lru_tg")
        self.lru_z = new("lru_z")
        self.m_bc = new("m_bc")
        self.m_conv = new("m_conv")
        self.m_e = new("m_e")
        self.m_e_masked = new("m_e_masked")
        self.m_p = new("m_p")
        self.m_qk = new("m_qk")
        self.m_s = new("m_s")
        self.m_stab = new("m_stab")
        self.m_tanh = new("m_tanh")
        self.m_turned = new("m_turned")
        self.m_y = new("m_y")
        self.m_yb = new("m_yb")
        self.mem_in = new("mem_in")
        self.merge = new("merge")
        self.merged = new("merged")
        self.mixed = new("mixed")
        self.mo_max = new("mo_max")
        self.mo_n = new("mo_n")
        self.mo_o = new("mo_o")
        self.mo_p = new("mo_p")
        self.mo_s = new("mo_s")
        self.mo_sc = new("mo_sc")
        self.mo_t = new("mo_t")
        self.mo_turned = new("mo_turned")
        self.pool_step = new("pool_step")
        self.post_read = new("post_read")
        self.post_sum = new("post_sum")
        self.qk2_in = new("qk2_in")
        self.qk_in = new("qk_in")
        self.row_in = new("row_in")
        self.rstd = new("rstd")
        self.sb_a = new("sb_a")
        self.sb_a_masked = new("sb_a_masked")
        self.sb_ln = new("sb_ln")
        self.sb_masked = new("sb_masked")
        self.sb_o = new("sb_o")
        self.sb_sp = new("sb_sp")
        self.sb_sum = new("sb_sum")
        self.sb_z = new("sb_z")
        self.sqk_in = new("sqk_in")
        self.stored = new("stored")
        self.sumsq = new("sumsq")
        self.turned = new("turned")
        self.v2_in = new("v2_in")
        self.vec_in = new("vec_in")
        self.vec_out = new("vec_out")
        self.vec_turned = new("vec_turned")
        self.vn = new("vn")
        self.vo_in = new("vo_in")
        self.w_high = new("w_high")
        self.w_used = new("w_used")
        self.ws_in = new("ws_in")
        self.ws_masked = new("ws_masked")
        self.ws_out = new("ws_out")
        self.ws_turned = new("ws_turned")
        self.x_in = new("x_in")
        self.x_max = new("x_max")
        self.x_n = new("x_n")
        self.x_o = new("x_o")
        self.x_p = new("x_p")
        self.x_ready = new("x_ready")
        self.x_s = new("x_s")
        self.x_t = new("x_t")
        self.x_turned = new("x_turned")
        self.xn = new("xn")
        self.xq_in = new("xq_in")
        self.y_a = new("y_a")
        self.y_b = new("y_b")
        self.y_c = new("y_c")
        self.ya2 = new("ya2")
        self.ya2_tok = new("ya2_tok")
        self.ya2_turned = new("ya2_turned")
        self.yb2 = new("yb2")
        self.yc2 = new("yc2")
        self.za_in = new("za_in")
        self.zc_in = new("zc_in")
        self.zc_t = new("zc_t")


def two_blocks(nc, w, out):
    groups, chunks = plan_weights(w)
    n_groups = len(groups)
    ctx = ExitStack()
    with ctx:
        def sb(name, shape, dt=F32):
            return ctx.enter_context(nc.sbuf_tensor(name, shape, dt))

        raw = [sb(f"raw{s}", [P, GROUP]) for s in range(RAW)]
        high = [sb(f"high{s}", [P, GROUP], F32R) for s in range(SPLIT)]
        low = [sb(f"low{s}", [P, GROUP], F32R) for s in range(SPLIT)]
        act_h = sb("act_h", [P, KD, T], F32R)
        act_l = sb("act_l", [P, KD, T], F32R)
        hid_h = [sb(f"hid_h{i}", [P, 4, T], F32R) for i in range(2)]
        hid_l = [sb(f"hid_l{i}", [P, 4, T], F32R) for i in range(2)]
        x = sb("x", [P, TT, D])
        xn = sb("xn", [P, TT, D])
        row_g = sb("row_g", [P, D])
        vec_rows = sb("vec_rows", [P, P])
        dw_rows = sb("dw_rows", [P, P])
        vec = sb("vec", [P, VEC_ROWS])
        dw = sb("dw", [P, DW_ROWS])
        ident = sb("ident", [P, P])
        block_mean = sb("block_mean", [P, P])
        if_bias = sb("if_bias", [4, 2])
        neg_half = sb("neg_half", [P, 4])
        sums = sb("sums", [P, 32])
        var = sb("var", [P, 32])
        rstd = sb("rstd", [P, 32])
        tiny = sb("tiny", [P, 40])
        neg_max = sb("neg_max", [P, 16])
        soft = sb("soft", [P, 16])

        arena = sb("arena", [P, ARENA])
        top = [0]

        def carve(*shape):
            size = math.prod(shape)
            a = arena[:, top[0]:top[0] + size]
            top[0] += size
            assert top[0] <= ARENA, top[0]
            if len(shape) == 2:
                a = a.rearrange("p (a b) -> p a b", a=shape[0])
            if len(shape) == 3:
                a = a.rearrange("p (a b c) -> p a b c", a=shape[0], b=shape[1])
            return a

        y = carve(6, T)
        gates = carve(TT, 3 * D)
        m_v = carve(TT, 4, 65)
        m_o = carve(TT, T)
        s_q = carve(2, T)
        s_k = carve(2, T)
        s_v = carve(TT, T)
        if_tok = carve(TT, 8)
        cols = carve(2, TT, 4)
        m_e = carve(4, DIAG)
        m_tmp = carve(TT, T)
        rows = carve(6, T)
        neg_tri = carve(P)
        neg_one = carve(P)
        head_row = carve(4, P)
        gate_w = [carve(2, P), carve(2, P)]
        ones4 = carve(T)
        era = top[0]
        lru_x = carve(2, T + 3)
        lru_g = carve(2, T)
        m_x = carve(4, T + 3)
        m_qk = carve(4, T)
        top1 = top[0]
        top[0] = era
        sb_a = carve(4, DIAG)
        top[0] = max(top[0], top1)
        l_r, l_i, l_u, l_a = (gates[:, :, 2 * D + i * T:2 * D + (i + 1) * T] for i in range(4))
        l_s, xa = (gates[:, :, D + NB + i * T:D + NB + (i + 1) * T] for i in range(2))
        top[0] = 0
        h_act = carve(2 * T)
        h_tmp = carve(2 * T)
        h_val = carve(2 * T)
        top[0] = 0
        y2 = carve(8, T)
        spatial_w = y2[:, 4:6, :].rearrange("p a (b s) -> p (a b) s", b=2)
        spatial_t = y2[:, 6:8, :].rearrange("p a (b s) -> p (a b) s", b=2)
        k_mem = carve(KD, T)
        v_mem = carve(TT, D)
        attn = top[0]
        sc = carve(8, DIAG)
        pt = carve(4, DIAG)
        q2 = carve(4, T)
        k2 = carve(4, T)
        v2 = carve(TT, NB)
        zg = carve(TT, NB)
        vn = carve(TT, T)
        dist = carve(DIAG)
        glu = carve(2, T + DW_TAPS - 1)
        cv = carve(2, T)
        cx = carve(2 * T)
        cs = carve(2 * T)
        ln_g = carve(T)
        ln_b = carve(T)
        top[0] = attn
        x_p = carve(4, TT, T)
        x_pt = carve(4, TT, T)
        x_q = carve(KD, T)

        bank = [ctx.enter_context(nc.psum_tensor(f"bank{i}", [P, NB], F32)) for i in range(8)]

        sem = Semaphores(lambda name: ctx.enter_context(nc.semaphore(name)))
        raw_in = [ctx.enter_context(nc.semaphore(f"raw_in{s}")) for s in range(RAW)]

        def arrived(g):
            return 16 * sum(len(groups[i][0]) for i in range(g % RAW, g + 1, RAW))

        def low_sem(g):
            return sem.low_by_pool if g % 2 else sem.low_by_dve

        def before(g):
            return g // 2 + 1

        def part(tiles, g):
            _, view, nk, width = groups[g]
            return tiles[g % len(tiles)][:, :].rearrange("p (k n) -> p k n", n=view)[:, 0:nk, 0:width]

        def col(name, i=0):
            return vec[:, VEC_OFF[name] + i:VEC_OFF[name] + i + 1]

        def f32(ap):
            return ap.bitcast(F32)

        def flat(ap):
            return ap.rearrange("p a b -> p (a b)")

        def in2(ap):
            return ap.rearrange("p (a b) -> p a b", a=2)

        NORM_GAIN = ["norm_mix_g", "norm_ffn_g", "pre_mix_g_2", "mem_g_2", "pre_x_g_2", "pre_ffn_g_2"]
        X_READY_END = 4 + 4 + 2 + 3 * TT
        FINAL, POST = 6, 7
        SQRT_2_PI = math.sqrt(2 / math.pi)
        block = ctx.enter_context(nc.Block())

        class Count:

            def __init__(self):
                self.steps, self.counts, self.used, self.pairs = 0, {}, 0, 0

            def seen(self, name, n=1):
                self.counts[name] = self.counts.get(name, 0) + n
                return self.counts[name]

            def step(self):
                self.steps += 1
                return self.steps

            def pair(self, back=0):
                i = 2 * ((self.pairs - 1 - back) % 2)
                return bank[i], bank[i + 1]

            def groups_of(self, key, mode):
                for g, kts in chunks[key]:
                    yield g, kts
                    self.used += 1
                self.pairs += {"W": 2, "F": 0}.get(mode, 1)

        @block.sync
        def _(sp):
            for g, (dmas, view, nk, width) in enumerate(groups):
                if g >= RAW:
                    sp.wait_ge(low_sem(g - RAW), before(g - RAW))
                tile = part(raw, g)
                for src, row, n, d, c, cw in dmas:
                    sp.dma_start(tile[:, 0:n, d:d + cw],
                                 src[row:row + n * P, c:c + cw].rearrange("(k p) n -> p k n", p=P))\
                      .then_inc(raw_in[g % RAW], 16)
            for t in range(TT):
                sp.wait_ge(sem.x_ready, X_READY_END - TT + 1 + t)
                sp.dma_start(out[t * P:(t + 1) * P, :], x[:, t, :]).then_inc(sem.stored, 16)
            sp.wait_ge(sem.stored, 16 * TT)

        @block.gpsimd
        def _(pool):
            me = Count()
            split = [0]

            def split_low(upto):
                while split[0] < min(upto, n_groups):
                    g = split[0]
                    split[0] += 1
                    if g % 2 == 0:
                        continue
                    pool.wait_ge(sem.w_high, g + 1)
                    if g >= SPLIT:
                        pool.wait_ge(sem.w_used, g - SPLIT + 1)
                    pool.tensor_tensor(part(low, g), part(raw, g), f32(part(high, g)), ALU.subtract)\
                        .then_inc(sem.low_by_pool, 1)

            def rsqrt(dst, src, scale, done):
                n = src.shape[-1]
                pool.tensor_scalar(src, src, scale, EPS, ALU.mult, ALU.add).then_inc(sem.pool_step, 1)
                pool.wait_ge(sem.pool_step, me.step())
                pool.tensor_tensor(dst, src, neg_half[:, 0:n], ALU.pow).then_inc(done, 1)

            def setup():
                pool.memset(ident[:, :], 0.0).then_inc(sem.pool_step, 1)
                pool.wait_ge(sem.pool_step, me.step())
                pool.affine_select(out=ident[:, :], in_=ident[:, :], compare_op=ALU.not_equal, fill=1.0, base=0,
                                   pattern=[[-1, P]], channel_multiplier=1).then_inc(sem.ident, 1)
                pool.memset(gate_w[0], 0.0)
                pool.memset(neg_half[:, :], -0.5)
                pool.memset(gate_w[1], 0.0).then_inc(sem.pool_step, 1)
                pool.wait_ge(sem.pool_step, me.step())
                for i, name in enumerate(("lru_wa", "lru_wx")):
                    for g in range(4):
                        q = 64 * (g % 2)
                        pool.dma_start(gate_w[i][q:q + 64, g // 2, q:q + 64], w[name][g]).then_inc(sem.gate_w, 16)
                split_low(LEAD)
                pool.memset(neg_tri, -1.0).then_inc(sem.pool_step, 1)
                pool.wait_ge(sem.pool_step, me.step())
                pool.affine_select(out=neg_tri, in_=neg_tri, compare_op=ALU.is_ge, fill=0.0, base=0,
                                   pattern=[[-1, P]], channel_multiplier=1).then_inc(sem.consts, 1)
                pool.memset(neg_one, -1.0).then_inc(sem.consts, 1)
                pool.memset(head_row[0:4], 0.0).then_inc(sem.pool_step, 1)
                pool.wait_ge(sem.pool_step, me.step())
                pool.affine_select(out=head_row[0:4], in_=head_row[0:4], compare_op=ALU.not_equal, fill=1.0, base=0,
                                   pattern=[[-1, 4], [0, P]], channel_multiplier=1).then_inc(sem.consts, 1)
                pool.memset(block_mean[:, :], 0.0).then_inc(sem.pool_step, 1)
                pool.wait_ge(sem.pool_step, me.step())
                pool.memset(block_mean[0:64, 0:64], 1 / 64).then_inc(sem.consts, 1)
                pool.wait_ge(sem.consts, me.seen("consts", 4))
                pool.memset(block_mean[64:P, 64:P], 1 / 64).then_inc(sem.consts, 1)
                pool.wait_ge(sem.consts, me.seen("consts"))

            def norm(n):
                pool.wait_ge(sem.sumsq, me.seen("sumsq", 2))
                rsqrt(rstd[:, 2 * n:2 * n + 2], sums[:, 2 * n:2 * n + 2], 1 / D, sem.rstd)

            def mlstm_cols():
                pool.wait_ge(sem.m_e, me.seen("m_e", 8))
                for a in (0, 2 * P):
                    part_e = m_e[:, :, a:a + P]
                    pool.affine_select(out=part_e, in_=part_e, compare_op=ALU.is_ge, fill=0.0, base=0,
                                       pattern=[[0, 4], [1, P]], channel_multiplier=-1).then_inc(sem.m_e_masked, 1)

            def strict(done, masked):
                pool.wait_ge(done, 4)
                for a in (0, 2 * P):
                    part_a = sb_a[:, :, a:a + P]
                    pool.affine_select(out=part_a, in_=part_a, compare_op=ALU.is_gt, fill=0.0, base=0,
                                       pattern=[[0, 4], [1, P]], channel_multiplier=-1).then_inc(masked, 1)

            def za_in():
                pool.wait_ge(sem.ws_in, me.seen("ws_in", 16))
                pool.affine_select(out=spatial_w, in_=spatial_w, compare_op=ALU.is_ge, fill=0.0, base=0,
                                   pattern=[[0, 4], [-1, P]], channel_multiplier=1).then_inc(sem.ws_masked, 1)
                pool.iota(dist[:, 0:P], [[1, P]], base=0, channel_multiplier=-1,
                               allow_small_or_imprecise_dtypes=True).then_inc(sem.pool_step, 1)
                pool.wait_ge(sem.pool_step, me.step())
                pool.iota(dist[:, P:DIAG], [[1, 2 * P]], base=-P, channel_multiplier=-1,
                               allow_small_or_imprecise_dtypes=True).then_inc(sem.pool_step, 1)
                pool.wait_ge(sem.pool_step, me.step())
                for a in (0, 2 * P):
                    pool.affine_select(out=dist[:, a:a + P], in_=dist[:, a:a + P], compare_op=ALU.is_ge,
                                       fill=-1e30, base=0, pattern=[[-1, P]], channel_multiplier=1)\
                        .then_inc(sem.dist, 1)
                pool.wait_ge(sem.ln_stat, me.seen("ln_stat", 2))
                rsqrt(rstd[:, 24:26], tiny[:, 17:20:2], 1.0, sem.ln_rstd)

            def post_norm(i):
                pool.wait_ge(sem.post_sum, me.seen("post_sum", 4))
                pool.tensor_tensor(var[:, 0:2], sums[:, 16:20:2], sums[:, 17:20:2], ALU.add).then_inc(sem.pool_step, 1)
                pool.wait_ge(sem.pool_step, me.step())
                rsqrt(rstd[:, 2 * (POST + i):2 * (POST + i) + 2], var[:, 0:2], 1 / D, sem.rstd)

            def ahead_of(key, mode):
                for g, _ in me.groups_of(key, mode):
                    split_low(g + LEAD + 1)

            setup()
            norm(0)
            ahead_of("lru", "C")
            ahead_of("qk", "C")
            ahead_of("ifsv", "T")
            ahead_of("vo", "T")
            ahead_of("sqk", "C")
            mlstm_cols()
            ahead_of(("gate", 0), "T")
            ahead_of(("gate", 1), "T")
            ahead_of(("gate", 2), "T")
            strict(sem.sb_sp, sem.sb_masked)
            ahead_of(("gate", 3), "T")
            strict(sem.sb_a, sem.sb_a_masked)
            ahead_of(("gate", 4), "T")
            ahead_of(("gate", 5), "T")
            for b in range(3):
                ahead_of(("branch", b), "W")
            for c in range(2):
                ahead_of(("wo", c), "T")
            norm(1)
            n1 = F1 // 256
            for c in range(n1 + 1):
                if c < n1:
                    ahead_of(("up1", c), "C")
                if c >= 1:
                    ahead_of(("down1", c - 1), "F")
            norm(FINAL)
            norm(2)
            ahead_of("za", "T")
            za_in()
            ahead_of("q2", "C")
            ahead_of("k2", "C")
            ahead_of("zc", "C")
            ahead_of("v2", "T")
            norm(3)
            ahead_of(("kv", 0), "C")
            ahead_of(("kv", 1), "C")
            ahead_of(("kv", 2), "T")
            ahead_of(("kv", 3), "T")
            for c in range(2):
                ahead_of(("mixout", c), "T")
            post_norm(0)
            norm(4)
            for c in range(2):
                ahead_of(("xq", c), "C")
            for c in range(2):
                ahead_of(("xo", c), "T")
            post_norm(1)
            norm(5)
            n2 = F2 // NB
            for c in range(n2 + 1):
                if c < n2:
                    ahead_of(("up2", c), "C")
                if c >= 1:
                    ahead_of(("down2", c - 1), "F")
            post_norm(2)

        @block.scalar
        def _(act):
            me = Count()
            split = [0]

            def f(dst, src, func, **k):
                return act.activation(dst, src, func, **k)

            def split_high(upto):
                while split[0] < min(upto, n_groups):
                    g = split[0]
                    split[0] += 1
                    act.wait_ge(raw_in[g % RAW], arrived(g))
                    if g >= SPLIT:
                        act.wait_ge(sem.w_used, g - SPLIT + 1)
                    f(part(high, g), part(raw, g), ACT.Copy).then_inc(sem.w_high, 1)

            def setup():
                act.dma_start(x[:, :, :], w["x"].rearrange("(t p) d -> p t d", p=P)).then_inc(sem.x_in, 16)
                for name, n in VEC_A:
                    act.dma_start(vec_rows[VEC_OFF[name]:VEC_OFF[name] + n, :], w[name].rearrange("(r c) -> r c", c=P))\
                       .then_inc(sem.vec_in, 16)
                act.dma_start(dw_rows[0:DW_ROWS, :], w["w_dw_2"].rearrange("(r c) -> r c", c=P))\
                   .then_inc(sem.dw_in, 16)
                for i, name in enumerate(("mlstm_ig_b", "mlstm_fg_b")):
                    act.dma_start(if_bias[:, i:i + 1], w[name].rearrange("(a b) -> a b", b=1)).then_inc(sem.bias_in, 16)
                load_row("final_norm_g")
                split_high(LEAD)

            def load_row(name):
                act.dma_start(row_g[:, :], w[name].partition_broadcast(P)).then_inc(sem.row_in, 16)

            def vectors():
                act.wait_ge(sem.vec_turned, me.seen("vec_turned", 2))
                f(vec[:, :], bank[4][:, 0:VEC_ROWS], ACT.Copy).then_inc(sem.vec_out, 1)
                f(dw[:, :], bank[4][:, P:P + DW_ROWS], ACT.Copy).then_inc(sem.vec_out, 1)
                act.wait_ge(sem.vec_out, me.seen("vec_out", 2))
                lam = vec[:, VEC_OFF["lru_lambda"]:VEC_OFF["lru_lambda"] + 2]
                f(tiny[:, 0:2], lam, ACT.Abs).then_inc(sem.act_step, 1)
                act.wait_ge(sem.act_step, me.step())
                f(tiny[:, 2:4], tiny[:, 0:2], ACT.Exp, scale=-1.0).then_inc(sem.lam_e, 1)

            X_BEFORE = {1: 4, 2: 2, 4: 2, 5: 2}

            def squares(n, src):
                for t in range(TT):
                    k = 2 * n + t
                    f((v_mem if src is xn else xn)[:, t, :], src[:, t, :], ACT.Square, accum_out=sums[:, k:k + 1])\
                        .then_inc(sem.sumsq, 1)

            def norm(n, src):
                if n == 0:
                    act.wait_ge(sem.x_in, me.seen("x_in", 16))
                elif src == "mem":
                    act.dma_start(xn[:, :, :], w["mem_2"].rearrange("(t p) d -> p t d", p=P)).then_inc(sem.mem_in, 16)
                    act.wait_ge(sem.mem_in, me.seen("mem_in", 16))
                else:
                    act.wait_ge(sem.x_ready, me.seen("x_ready", X_BEFORE[n]))
                squares(n, xn if src == "mem" else x)
                if n == 2:
                    load_row("post_mix_g_2")
                    act.dma_start(ln_g, w["gate_ln_g_2"].partition_broadcast(P)).then_inc(sem.ln_in, 16)
                    act.dma_start(ln_b, w["gate_ln_b_2"].partition_broadcast(P)).then_inc(sem.ln_in, 16)
                    act.dma_start(spatial_w, w["w_s_2"].rearrange("h t s -> t h s")).then_inc(sem.ws_in, 16)
                if n == 4:
                    load_row("post_x_g_2")
                if n == 5:
                    load_row("post_ffn_g_2")
                act.wait_ge(sem.w_used, me.used)
                for q in range(4):
                    act.wait_ge(sem.turned, me.seen("turned"))
                    for k in range(2):
                        kt = 2 * q + k
                        ins = f(act_h[:, kt, :], bank[4 + q][:, k * T:(k + 1) * T], ACT.Copy,
                                scale=col(NORM_GAIN[n], kt))
                    ins.then_inc(sem.act_h, 1)

            def final_norm():
                act.wait_ge(sem.x_ready, me.seen("x_ready", 4))
                squares(FINAL, x)

            def copy_pair(d0, d1, done, scale=1.0, func=ACT.Copy):
                act.wait_ge(sem.w_used, me.used)
                b0, b1 = me.pair()
                for d, b in ((d0, b0), (d1, b1)):
                    src = b[:, :]
                    if len(d.shape) == 3:
                        src = src.rearrange("p (a b) -> p a b", a=d.shape[1])
                    f(d, src, func, scale=scale).then_inc(done, 1)


            def gate_in(c):
                if c >= 3:
                    act.wait_ge(sem.y_a, 1)
                copy_pair(gates[:, 0, c * NB:(c + 1) * NB], gates[:, 1, c * NB:(c + 1) * NB], sem.gate_in, 0.5, ACT.Tanh)

            def ifsv_in():
                act.wait_ge(sem.w_used, me.used)
                for t, b in enumerate(me.pair()):
                    f(if_tok[:, t, :], b[:, 0:8], ACT.Copy)
                    f(s_v[:, t, :], b[:, 8:264], ACT.Copy).then_inc(sem.ifsv_in, 1)

            def vo_in():
                act.wait_ge(sem.w_used, me.used)
                for t, b in enumerate(me.pair()):
                    f(m_v[:, t, :, 0:64], b[:, 0:T].rearrange("p (h d) -> p h d", h=4), ACT.Copy)
                    f(m_o[:, t, :], b[:, T:2 * T], ACT.Tanh, scale=0.5).then_inc(sem.vo_in, 1)

            def sqk_in():
                act.wait_ge(sem.w_used, me.used)
                b0, b1 = me.pair()
                f(flat(s_q), b0[:, :], ACT.Copy, scale=0.125).then_inc(sem.sqk_in, 1)
                f(flat(s_k), b1[:, :], ACT.Copy).then_inc(sem.sqk_in, 1)

            def if_rows():
                act.wait_ge(sem.if_rows, me.seen("if_rows"))
                f(rows[0:4, 2, :], rows[0:4, 0, :], ACT.Abs).then_inc(sem.act_step, 1)
                act.wait_ge(sem.act_step, me.step())
                f(rows[0:4, 2, :], rows[0:4, 2, :], ACT.Exp, scale=-1.0).then_inc(sem.act_step, 1)
                act.wait_ge(sem.act_step, me.step())
                f(rows[0:4, 2, :], rows[0:4, 2, :], ACT.Ln, bias=1.0).then_inc(sem.log_f, 1)
                act.wait_ge(sem.m_stab, me.seen("m_stab"))
                f(rows[0:4, 5, :], rows[0:4, 5, :], ACT.Exp, scale=-1.0).then_inc(sem.exp_m, 1)

            def lru_gates():
                act.wait_ge(sem.lru_z, me.seen("lru_z"))
                act.wait_ge(sem.lru_cols, me.seen("lru_cols"))
                for i, (b, dst) in enumerate(((bank[4], l_r), (bank[5], l_i))):
                    for c in range(2):
                        k = 8 + 2 * i + c
                        ins = f(dst[:, c, :], b[:, c * T:(c + 1) * T], ACT.Tanh, scale=0.5, bias=tiny[:, k:k + 1])
                    ins.then_inc(sem.lru_t, 1)
                act.wait_ge(sem.lru_t, me.seen("lru_t"))
                for c in range(2):
                    k = 12 + c
                    ins = f(l_r[:, c, :], l_r[:, c, :], ACT.Tanh, scale=tiny[:, k:k + 1], bias=tiny[:, k:k + 1])
                ins.then_inc(sem.lru_t, 1)
                act.wait_ge(sem.lru_t, me.seen("lru_t", 2))
                f(l_s, l_r, ACT.Sqrt, scale=-4.0).then_inc(sem.lru_sqrt, 1)

            def lru_scan():
                act.wait_ge(sem.lru_gelu, me.seen("lru_gelu"))
                f(xa, xa, ACT.Tanh, scale=SQRT_2_PI).then_inc(sem.lru_tg, 1)

            def mlstm_cols():
                act.wait_ge(sem.cols, me.seen("cols"))
                act.wait_ge(sem.m_bc, me.seen("m_bc", 2))
                for h in range(4):
                    b = bank[4 + h // 2]
                    o = (h % 2) * T
                    f(m_e[:, h, 0:T], b[:, o:o + T], ACT.Exp, scale=-1.0, bias=cols[:, 0, 0, h:h + 1])\
                        .then_inc(sem.m_e, 1)
                    f(m_e[:, h, T:DIAG], b[:, o + P:o + T], ACT.Exp, scale=-1.0, bias=cols[:, 0, 1, h:h + 1])\
                        .then_inc(sem.m_e, 1)

            def mlstm_qk():
                act.wait_ge(sem.m_conv, me.seen("m_conv", 4))
                f(m_x[:, :, 0:T], m_qk, ACT.Tanh, scale=0.5).then_inc(sem.m_tanh, 1)

            def mlstm_turn():
                act.wait_ge(sem.m_turned, me.seen("m_turned"))
                f(flat(y[:, 2:4, :]), bank[4][:, :], ACT.Copy, scale=0.5).then_inc(sem.y_b, 1)

            def sb_scores():
                act.wait_ge(sem.y_a, 1)
                for h in range(4):
                    act.wait_ge(sem.sb_z, me.seen("sb_z"))
                    ins = f(sb_a[:, h, :], bank[4 + h][:, 0:DIAG], ACT.Abs)
                ins.then_inc(sem.act_step, 1)
                act.wait_ge(sem.act_step, me.step())
                f(flat(sb_a), flat(sb_a), ACT.Exp, scale=-1.0).then_inc(sem.act_step, 1)
                act.wait_ge(sem.act_step, me.step())
                f(flat(sb_a), flat(sb_a), ACT.Ln, bias=1.0).then_inc(sem.sb_ln, 1)

            def sb_sums():
                for h in range(4):
                    act.wait_ge(sem.sb_sum, me.seen("sb_sum"))
                    f(sb_a[:, h, :], bank[4 + h][:, 0:DIAG], ACT.Exp).then_inc(sem.sb_a, 1)

            def sb_out():
                act.wait_ge(sem.sb_o, me.seen("sb_o"))
                f(flat(y[:, 4:6, :]), bank[4][:, :], ACT.Copy).then_inc(sem.y_c, 1)

            def split_y(n):
                if n == 6:
                    act.wait_ge(sem.y_a, 1)
                    act.wait_ge(sem.y_b, 1)
                    act.wait_ge(sem.y_c, 1)
                else:
                    act.wait_ge(sem.ya2, 1)
                    act.wait_ge(sem.yb2, 4)
                    act.wait_ge(sem.yc2, 1)
                act.wait_ge(sem.w_used, me.used)
                src = y if n == 6 else y2
                f(flat(act_h[:, 0:n, :]), flat(src[:, 0:n, :]), ACT.Copy).then_inc(sem.act_h, 1)

            def turn_merged():
                act.wait_ge(sem.w_used, me.used)
                for q in range(4):
                    act.wait_ge(sem.turned, me.seen("turned"))
                    f(flat(act_h[:, 2 * q:2 * q + 2, :]), bank[4 + q][:, :], ACT.Copy, scale=0.5)\
                        .then_inc(sem.act_h, 1)

            def hidden1(c):
                act.wait_ge(sem.w_used, me.used)
                b0, _ = me.pair()
                f(h_act, b0[:, :], ACT.Tanh, scale=0.5).then_inc(sem.hid_t, 1)
                act.wait_ge(sem.hid_a, me.seen("hid_a", 1))
                f(flat(hid_h[c % 2][:, 0:2, :]), h_val, ACT.Copy).then_inc(sem.hid_h, 1)

            def hidden2(c):
                act.wait_ge(sem.w_used, me.used)
                for b in range(2):
                    src = me.pair()[b]
                    f(h_act, src[:, :], ACT.Relu).then_inc(sem.hid_t, 1)
                    act.wait_ge(sem.hid_a, me.seen("hid_a", 1))
                    f(flat(hid_h[c % 2][:, 2 * b:2 * b + 2, :]), h_val, ACT.Copy).then_inc(sem.hid_h, 1)

            def za_in():
                copy_pair(zg[:, 0, :], zg[:, 1, :], sem.za_in, 1.0, ACT.Gelu)
                act.wait_ge(sem.ws_turned, me.seen("ws_turned"))
                f(spatial_t, bank[5][:, :].rearrange("p (h t) -> p h t", h=4), ACT.Copy).then_inc(sem.ws_out, 1)

            def qk2_in(i):
                d = (q2, k2)[i]
                copy_pair(d[:, 0:2, :], d[:, 2:4, :], sem.qk2_in, (0.125, 1.0)[i])

            def kv_in(c):
                if c < 2:
                    copy_pair(k_mem[:, 4 * c:4 * c + 2, :], k_mem[:, 4 * c + 2:4 * c + 4, :], sem.kv_in)
                else:
                    a = (c - 2) * NB
                    copy_pair(v_mem[:, 0, a:a + NB], v_mem[:, 1, a:a + NB], sem.kv_in)

            def zc_in():
                act.wait_ge(sem.w_used, me.used)
                f(cs, me.pair()[1][:, :], ACT.Tanh, scale=0.5).then_inc(sem.zc_t, 1)

            def spatial():
                act.wait_ge(sem.ya2_turned, me.seen("ya2_turned"))
                f(flat(y2[:, 0:2, :]), bank[5][:, :], ACT.Copy).then_inc(sem.ya2, 1)

            def moba_turn(i):
                act.wait_ge(sem.mo_max, me.seen("mo_max"))
                for h in range(4 * i, 4 * i + 4):
                    for t, (a, n) in enumerate(((0, P), (P, 2 * P))):
                        k = 8 * t + h
                        ins = f(sc[:, h, a:a + n], sc[:, h, a:a + n], ACT.Exp, bias=neg_max[:, k:k + 1],
                                accum_out=soft[:, k:k + 1])
                    ins.then_inc(sem.mo_p, 1)
                for h in range(4):
                    act.wait_ge(sem.mo_turned, me.seen("mo_turned"))
                    f(pt[:, h, :], bank[4 + h][:, 0:DIAG], ACT.Copy).then_inc(sem.mo_t, 1)
                for c in range(2):
                    act.wait_ge(sem.mo_o, me.seen("mo_o"))
                    f(y2[:, 2 + 2 * i + c, :], bank[4 + c][:, 0:T], ACT.Copy).then_inc(sem.yb2, 1)

            def group_norm():
                act.wait_ge(sem.gn_var, me.seen("gn_var"))
                f(cs, bank[5][:, :], ACT.Sqrt, bias=EPS).then_inc(sem.gn_sd, 1)
                act.wait_ge(sem.gn_z, me.seen("gn_z", 2))
                f(cs, cx, ACT.Tanh, scale=0.5).then_inc(sem.gn_t, 1)

            def square(b, t, c):
                k = 16 + 2 * t + c
                f(xn[:, t, c * NB:(c + 1) * NB], b[:, :], ACT.Square, accum_out=sums[:, k:k + 1])\
                    .then_inc(sem.post_sum, 1)

            def post_in(c):
                act.wait_ge(sem.w_used, me.used)
                for t, b in enumerate(me.pair()):
                    square(b, t, c)

            def post_acc():
                act.wait_ge(sem.w_used, me.used)
                for t in range(TT):
                    for c in range(2):
                        square(bank[4 + 2 * t + c], t, c)

            def x_scores():
                for h in range(4):
                    act.wait_ge(sem.x_max, me.seen("x_max"))
                    for t in range(TT):
                        k = 2 * h + t
                        ins = f(x_p[:, h, t, :], bank[4 + h][:, t * T:(t + 1) * T], ACT.Exp, bias=neg_max[:, k:k + 1],
                                accum_out=soft[:, k:k + 1])
                    ins.then_inc(sem.x_p, 1)
                for h in range(4):
                    act.wait_ge(sem.x_turned, me.seen("x_turned"))
                    f(flat(x_pt[:, h, :, :]), bank[4 + h][:, :], ACT.Copy).then_inc(sem.x_t, 1)

            def x_out():
                act.wait_ge(sem.w_used, me.used)
                for q in range(4):
                    act.wait_ge(sem.x_o, me.seen("x_o"))
                    f(flat(act_h[:, 2 * q:2 * q + 2, :]), bank[4 + q][:, :], ACT.Copy).then_inc(sem.act_h, 1)

            def ahead_of(key, mode):
                for g, _ in me.groups_of(key, mode):
                    split_high(g + LEAD + 1)

            setup()
            vectors()
            norm(0, "x")
            ahead_of("lru", "C")
            copy_pair(lru_x[:, :, 3:], lru_g, sem.lru_in)
            ahead_of("qk", "C")
            copy_pair(m_x[:, 0:2, 3:], m_x[:, 2:4, 3:], sem.qk_in)
            ahead_of("ifsv", "T")
            ifsv_in()
            if_rows()
            ahead_of("vo", "T")
            vo_in()
            lru_gates()
            ahead_of("sqk", "C")
            sqk_in()
            mlstm_cols()
            mlstm_qk()
            ahead_of(("gate", 0), "T")
            gate_in(0)
            ahead_of(("gate", 1), "T")
            gate_in(1)
            lru_scan()
            ahead_of(("gate", 2), "T")
            gate_in(2)
            mlstm_turn()
            sb_scores()
            ahead_of(("gate", 3), "T")
            gate_in(3)
            sb_sums()
            ahead_of(("gate", 4), "T")
            gate_in(4)
            sb_out()
            ahead_of(("gate", 5), "T")
            gate_in(5)
            split_y(6)
            for b in range(3):
                ahead_of(("branch", b), "W")
            turn_merged()
            for c in range(2):
                ahead_of(("wo", c), "T")
            norm(1, "x")
            n1 = F1 // 256
            for c in range(n1 + 1):
                if c < n1:
                    ahead_of(("up1", c), "C")
                    hidden1(c)
                if c >= 1:
                    ahead_of(("down1", c - 1), "F")
            final_norm()
            norm(2, "x")
            ahead_of("za", "T")
            za_in()
            ahead_of("q2", "C")
            qk2_in(0)
            ahead_of("k2", "C")
            qk2_in(1)
            ahead_of("zc", "C")
            zc_in()
            spatial()
            ahead_of("v2", "T")
            copy_pair(v2[:, 0, :], v2[:, 1, :], sem.v2_in)
            norm(3, "mem")
            ahead_of(("kv", 0), "C")
            kv_in(0)
            moba_turn(0)
            ahead_of(("kv", 1), "C")
            kv_in(1)
            moba_turn(1)
            ahead_of(("kv", 2), "T")
            kv_in(2)
            group_norm()
            ahead_of(("kv", 3), "T")
            kv_in(3)
            split_y(8)
            for c in range(2):
                ahead_of(("mixout", c), "T")
                post_in(c)
            norm(4, "x")
            for c in range(2):
                ahead_of(("xq", c), "C")
                copy_pair(x_q[:, 4 * c:4 * c + 2, :], x_q[:, 4 * c + 2:4 * c + 4, :], sem.xq_in, 1 / 16)
            x_scores()
            x_out()
            for c in range(2):
                ahead_of(("xo", c), "T")
                post_in(c)
            norm(5, "x")
            n2 = F2 // NB
            for c in range(n2 + 1):
                if c < n2:
                    ahead_of(("up2", c), "C")
                    hidden2(c)
                if c >= 1:
                    ahead_of(("down2", c - 1), "F")
            post_acc()

        @block.vector
        def _(dve):
            me = Count()
            split = [0]
            stt, ts, tt = dve.scalar_tensor_tensor, dve.tensor_scalar, dve.tensor_tensor
            MUL, ADD, SUB, MAX, MIN = ALU.mult, ALU.add, ALU.subtract, ALU.max, ALU.min

            def split_low(upto):
                while split[0] < min(upto, n_groups):
                    g = split[0]
                    split[0] += 1
                    if g % 2:
                        continue
                    dve.wait_ge(sem.w_high, g + 1)
                    if g >= SPLIT:
                        dve.wait_ge(sem.w_used, g - SPLIT + 1)
                    tt(part(low, g), part(raw, g), f32(part(high, g)), SUB).then_inc(sem.low_by_dve, 1)

            def setup():
                dve.memset(lru_x[:, :, 0:3], 0.0)
                dve.memset(m_x[:, :, 0:3], 0.0)
                dve.memset(m_v[:, :, :, 64:65], 1.0)
                dve.memset(ones4[0:4], 1.0).then_inc(sem.dve_step, 1)
                dve.wait_ge(sem.dve_step, me.step())
                split_low(LEAD)

            def vectors():
                dve.wait_ge(sem.lam_e, me.seen("lam_e"))
                e, s_, p_, q_ = tiny[:, 2:4], tiny[:, 4:6], tiny[:, 6:8], tiny[:, 14:16]
                ts(s_, e, 2.0, None, ADD).then_inc(sem.dve_step, 1)
                dve.wait_ge(sem.dve_step, me.step())
                dve.reciprocal(s_, s_).then_inc(sem.dve_step, 1)
                dve.wait_ge(sem.dve_step, me.step())
                tt(s_, s_, e, MUL).then_inc(sem.dve_step, 1)
                dve.wait_ge(sem.dve_step, me.step())
                tt(p_, s_, s_, MUL).then_inc(sem.dve_step, 1)
                dve.wait_ge(sem.dve_step, me.step())
                ts(q_, p_, 1 / 15, None, MUL).then_inc(sem.dve_step, 1)
                dve.wait_ge(sem.dve_step, me.step())
                for k in (13, 11, 9, 7, 5, 3):
                    stt(q_, q_, 1 / k, p_, ADD, MUL).then_inc(sem.dve_step, 1)
                    dve.wait_ge(sem.dve_step, me.step())
                stt(q_, q_, 1.0, s_, ADD, MUL).then_inc(sem.dve_step, 1)
                dve.wait_ge(sem.dve_step, me.step())
                lam = vec[:, VEC_OFF["lru_lambda"]:VEC_OFF["lru_lambda"] + 2]
                ts(s_, lam, -1.0, 0.0, MUL, MAX).then_inc(sem.dve_step, 1)
                dve.wait_ge(sem.dve_step, me.step())
                stt(s_, q_, 2.0, s_, MUL, ADD).then_inc(sem.dve_step, 1)
                dve.wait_ge(sem.dve_step, me.step())
                ts(tiny[:, 12:14], s_, -2.0, None, MUL)
                k = VEC_OFF["lru_ba"]
                ts(tiny[:, 8:12], vec[:, k:k + 4], 0.5, None, MUL).then_inc(sem.lru_cols, 1)

            def norm(n, src):
                dve.wait_ge(sem.rstd, me.seen("rstd"))
                for t in range(TT):
                    k = 2 * n + t
                    ts(xn[:, t, :], (xn if src == "mem" else x)[:, t, :], rstd[:, k:k + 1], None, MUL)\
                        .then_inc(sem.xn, 1)
                for q in range(4):
                    dve.wait_ge(sem.act_h, me.seen("act_h"))
                    for k in range(2):
                        kt = 2 * q + k
                        ins = stt(act_l[:, kt, :], bank[4 + q][:, k * T:(k + 1) * T], col(NORM_GAIN[n], kt),
                                  f32(act_h[:, kt, :]), MUL, SUB)
                    ins.then_inc(sem.act_hl, 1)

            def final_norm():
                dve.wait_ge(sem.rstd, me.seen("rstd"))
                dve.wait_ge(sem.row_in, me.seen("row_in", 16))
                for t in range(TT):
                    k = 2 * FINAL + t
                    stt(x[:, t, :], x[:, t, :], rstd[:, k:k + 1], row_g[:, :], MUL, MUL).then_inc(sem.x_ready, 1)

            def conv(dst, src, taps, weight, tiles, first, done=None):
                for j in taps:
                    for c in range(tiles):
                        window = src[:, c, j:j + T]
                        if j == first:
                            ins = ts(dst[:, c, :], window, weight(j, c), None, MUL)
                        else:
                            ins = stt(dst[:, c, :], window, weight(j, c), dst[:, c, :], MUL, ADD)
                        if c == tiles - 1 or (done and j == taps[-1]):
                            if done and j == taps[-1]:
                                ins.then_inc(done, 1)
                            else:
                                ins.then_inc(sem.dve_step, 1)
                                dve.wait_ge(sem.dve_step, me.step())

            def lru_conv():
                dve.wait_ge(sem.lru_in, me.seen("lru_in", 2))
                conv(xa, lru_x, range(4), lambda j, c: col("conv_lru_w", 2 * j + c), 2, 0, sem.lru_conv)

            def if_rows():
                dve.wait_ge(sem.if_turned, me.seen("if_turned"))
                dve.wait_ge(sem.bias_in, me.seen("bias_in", 32))
                ts(rows[0:4, 0, :], bank[6][0:4, T:2 * T], if_bias[:, 1:2], None, ADD)
                ts(rows[0:4, 1, :], bank[6][0:4, 0:T], if_bias[:, 0:1], None, ADD).then_inc(sem.if_rows, 1)
                dve.wait_ge(sem.log_f, me.seen("log_f"))
                r = [rows[0:4, i, :] for i in range(6)]
                stt(r[0], r[0], 0.0, r[2], MIN, SUB).then_inc(sem.dve_step, 1)
                dve.wait_ge(sem.dve_step, me.step())
                dve.tensor_tensor_scan(r[3], ones4[0:4], r[0], 0.0, MUL, ADD).then_inc(sem.dve_step, 1)
                dve.wait_ge(sem.dve_step, me.step())
                tt(r[1], r[1], r[3], SUB).then_inc(sem.dve_step, 1)
                dve.wait_ge(sem.dve_step, me.step())
                dve.tensor_tensor_scan(r[4], r[1], r[1], 0.0, MAX, MAX).then_inc(sem.dve_step, 1)
                dve.wait_ge(sem.dve_step, me.step())
                tt(r[5], r[3], r[4], ADD).then_inc(sem.m_stab, 1)

            def mlstm_cols():
                dve.wait_ge(sem.cols_turned, me.seen("cols_turned"))
                dve.tensor_copy(cols.rearrange("p a b c -> p (a b c)"), bank[7][:, 0:16]).then_inc(sem.cols, 1)

            def mlstm_qk():
                dve.wait_ge(sem.qk_in, me.seen("qk_in", 2))
                conv(m_qk, m_x, range(4), lambda j, c: col("conv_mlstm_w", 4 * j + c), 4, 0, sem.m_conv)
                dve.wait_ge(sem.m_tanh, me.seen("m_tanh"))
                stt(m_qk, m_x[:, :, 0:T], 1.0, m_qk, ADD, MUL).then_inc(sem.m_qk, 1)

            def mlstm_scores():
                dve.wait_ge(sem.m_e_masked, me.seen("m_e_masked", 2))
                for h in range(4):
                    dve.wait_ge(sem.m_s, me.seen("m_s"))
                    b = bank[(6, 7, 4, 5)[h]]
                    stt(m_e[:, h, :], b[:, 0:DIAG], 1 / 32, m_e[:, h, :], MUL, MUL).then_inc(sem.m_p, 1)

            def mlstm_out():
                dve.wait_ge(sem.m_y, me.seen("m_y"))
                dve.wait_ge(sem.vo_in, me.seen("vo_in", 2))
                for t in range(TT):
                    b = bank[6 + t][:, 0:260].rearrange("p (h d) -> p h d", h=4)
                    den, neg = tiny[:, 20 + 4 * t:24 + 4 * t], tiny[:, 28:32]
                    dve.tensor_copy(den, b[:, :, 64]).then_inc(sem.dve_step, 1)
                    dve.wait_ge(sem.dve_step, me.step())
                    stt(den, den, -1.0, den, MUL, MAX).then_inc(sem.dve_step, 1)
                    dve.wait_ge(sem.dve_step, me.step())
                    tt(den, den, cols[:, 1, t, :], MAX).then_inc(sem.dve_step, 1)
                    dve.wait_ge(sem.dve_step, me.step())
                    dve.reciprocal(den, den).then_inc(sem.dve_step, 1)
                    dve.wait_ge(sem.dve_step, me.step())
                    out_t = m_tmp[:, t, :].rearrange("p (h d) -> p h d", h=4)
                    tt(out_t, b[:, :, 0:64], den.unsqueeze(2).broadcast_to([P, 4, 64]), MUL).then_inc(sem.dve_step, 1)
                    dve.wait_ge(sem.dve_step, me.step())
                    stt(m_tmp[:, t, :], m_o[:, t, :], 1.0, m_tmp[:, t, :], ADD, MUL).then_inc(sem.m_yb, 1)

            def lru_scan():
                dve.wait_ge(sem.lru_sqrt, me.seen("lru_sqrt"))
                ts(l_u, l_r, -1.0, 1.0, MUL, ADD).then_inc(sem.dve_step, 1)
                dve.wait_ge(sem.dve_step, me.step())
                dve.reciprocal(l_u, l_u).then_inc(sem.dve_step, 1)
                dve.wait_ge(sem.dve_step, me.step())
                stt(l_a, l_r, 1.0, l_u, ADD, MUL)
                stt(l_i, l_i, 1.0, xa, ADD, MUL)
                tt(l_s, l_s, l_u, MUL).then_inc(sem.dve_step, 1)
                dve.wait_ge(sem.dve_step, me.step())
                stt(l_i, l_i, 0.5, l_s, MUL, MUL).then_inc(sem.dve_step, 1)
                dve.wait_ge(sem.dve_step, me.step())
                for c in range(2):
                    dve.tensor_tensor_scan(l_s[:, c, :], l_a[:, c, :], l_i[:, c, :], 0.0, MUL, ADD).then_inc(sem.dve_step, 1)
                    dve.wait_ge(sem.dve_step, me.step())
                tt(xa, lru_g, lru_g, MUL).then_inc(sem.dve_step, 1)
                dve.wait_ge(sem.dve_step, me.step())
                ts(xa, xa, 0.044715, 1.0, MUL, ADD).then_inc(sem.dve_step, 1)
                dve.wait_ge(sem.dve_step, me.step())
                tt(xa, xa, lru_g, MUL).then_inc(sem.lru_gelu, 1)
                dve.wait_ge(sem.lru_tg, me.seen("lru_tg"))
                stt(lru_g, xa, 1.0, lru_g, ADD, MUL).then_inc(sem.dve_step, 1)
                dve.wait_ge(sem.dve_step, me.step())
                stt(y[:, 0:2, :], lru_g, 0.5, l_s, MUL, MUL).then_inc(sem.y_a, 1)

            def sb_scores():
                dve.wait_ge(sem.sb_ln, me.seen("sb_ln"))
                for h in range(4):
                    stt(sb_a[:, h, :], bank[4 + h][:, 0:DIAG], 0.0, sb_a[:, h, :], MAX, ADD).then_inc(sem.sb_sp, 1)

            def split_y(n):
                dve.wait_ge(sem.act_h, me.seen("act_h"))
                src = y if n == 6 else y2
                tt(flat(act_l[:, 0:n, :]), flat(src[:, 0:n, :]), f32(flat(act_h[:, 0:n, :])), SUB)\
                    .then_inc(sem.act_hl, 1)

            def merge(b):
                dve.wait_ge(sem.w_used, me.used)
                for c in range(2):
                    for t in range(TT):
                        src = me.pair(1 - c)[t]
                        g = gates[:, t, b * D + c * NB:b * D + (c + 1) * NB]
                        m = xn[:, t, c * NB:(c + 1) * NB]
                        if b == 0:
                            stt(m, g, 1.0, src[:, :], ADD, MUL).then_inc(sem.merge, 1)
                        else:
                            tmp = (h_act, h_tmp)[t]
                            stt(tmp, g, 1.0, src[:, :], ADD, MUL).then_inc(sem.merge, 1)
                            dve.wait_ge(sem.merge, 4 * b + 2 * c + t + 1)
                            tt(m, m, tmp, ADD).then_inc(sem.merged, 1)

            def low_of_bank(q, scale=1.0):
                dve.wait_ge(sem.act_h, me.seen("act_h"))
                stt(flat(act_l[:, 2 * q:2 * q + 2, :]), bank[4 + q][:, :], scale,
                    f32(flat(act_h[:, 2 * q:2 * q + 2, :])), MUL, SUB).then_inc(sem.act_hl, 1)

            def turn_merged():
                for q in range(4):
                    low_of_bank(q, 0.5)

            def x_out():
                for q in range(4):
                    low_of_bank(q)

            def add_x(c):
                dve.wait_ge(sem.w_used, me.used)
                for t, b in enumerate(me.pair()):
                    o = x[:, t, c * NB:(c + 1) * NB]
                    tt(o, b[:, :], o, ADD).then_inc(sem.x_ready, 1)

            def add_acc():
                dve.wait_ge(sem.w_used, me.used)
                for t in range(TT):
                    for c in range(2):
                        o = x[:, t, c * NB:(c + 1) * NB]
                        tt(o, bank[4 + 2 * t + c][:, :], o, ADD).then_inc(sem.x_ready, 1)

            def hidden1(c):
                dve.wait_ge(sem.hid_t, me.seen("hid_t"))
                b0, b1 = me.pair()
                stt(h_tmp, h_act, 1.0, b0[:, :], ADD, MUL).then_inc(sem.dve_step, 1)
                dve.wait_ge(sem.dve_step, me.step())
                stt(h_val, h_tmp, 0.5, b1[:, :], MUL, MUL).then_inc(sem.hid_a, 1)
                dve.wait_ge(sem.hid_h, me.seen("hid_h"))
                hl = flat(hid_l[c % 2][:, 0:2, :])
                tt(hl, h_val, f32(flat(hid_h[c % 2][:, 0:2, :])), SUB).then_inc(sem.hid_hl, 1)
                dve.wait_ge(sem.hid_hl, me.seen("hid_hl"))

            def hidden2(c):
                for b in range(2):
                    dve.wait_ge(sem.hid_t, me.seen("hid_t"))
                    tt(h_val, h_act, h_act, MUL).then_inc(sem.hid_a, 1)
                    dve.wait_ge(sem.hid_h, me.seen("hid_h"))
                    hl = flat(hid_l[c % 2][:, 2 * b:2 * b + 2, :])
                    tt(hl, h_val, f32(flat(hid_h[c % 2][:, 2 * b:2 * b + 2, :])), SUB).then_inc(sem.hid_hl, 1)
                    dve.wait_ge(sem.hid_hl, me.seen("hid_hl"))

            def za_in():
                dve.wait_ge(sem.za_in, me.seen("za_in", 2))
                for t in range(TT):
                    k = 20 + 6 * t
                    dve.bn_stats(tiny[:, k:k + 6], zg[:, t, T:2 * T]).then_inc(sem.dve_step, 1)
                    dve.wait_ge(sem.dve_step, me.step())
                    dve.bn_aggr(tiny[:, 16 + 2 * t:18 + 2 * t], tiny[:, k:k + 6]).then_inc(sem.ln_stat, 1)
                dve.wait_ge(sem.ln_rstd, me.seen("ln_rstd"))
                dve.wait_ge(sem.ln_in, me.seen("ln_in", 32))
                for t in range(TT):
                    ts(vn[:, t, :], zg[:, t, T:2 * T], tiny[:, 16 + 2 * t:17 + 2 * t], rstd[:, 24 + t:25 + t],
                            SUB, MUL).then_inc(sem.dve_step, 1)
                    dve.wait_ge(sem.dve_step, me.step())
                    tt(vn[:, t, :], vn[:, t, :], ln_g, MUL).then_inc(sem.dve_step, 1)
                    dve.wait_ge(sem.dve_step, me.step())
                    tt(vn[:, t, :], vn[:, t, :], ln_b, ADD).then_inc(sem.vn, 1)

            def spatial():
                dve.wait_ge(sem.mixed, me.seen("mixed"))
                for t in range(TT):
                    for h in range(4):
                        d = slice(h * 64, h * 64 + 64)
                        ins = stt(vn[:, t, d], bank[4][:, t * T + h * 64:t * T + h * 64 + 64], col("b_s_2", h),
                                  zg[:, t, d], ADD, MUL)
                    ins.then_inc(sem.ya2_tok, 1)

            def moba_scores(i):
                if i == 0:
                    dve.wait_ge(sem.dist, me.seen("dist", 2))
                for h in range(4 * i, 4 * i + 4):
                    dve.wait_ge(sem.mo_s, me.seen("mo_s"))
                    stt(sc[:, h, :], dist, 2.0 ** -(h + 1), bank[4 + h % 4][:, 0:DIAG], MUL, ADD)\
                        .then_inc(sem.mo_sc, 1)
                dve.wait_ge(sem.mo_sc, me.seen("mo_sc", 4))
                r = slice(4 * i, 4 * i + 4)
                for t, (a, n) in enumerate(((0, P), (P, 2 * P))):
                    dve.tensor_reduce(neg_max[:, 8 * t + 4 * i:8 * t + 4 * i + 4], sc[:, r, a:a + n], AX.X, MAX,
                                      negate=True).then_inc(sem.mo_max, 1)

            def moba_turn(i):
                dve.wait_ge(sem.mo_p, me.seen("mo_p", 4))
                for t in range(TT):
                    k = 8 * t + 4 * i
                    dve.reciprocal(soft[:, k:k + 4], soft[:, k:k + 4]).then_inc(sem.dve_step, 1)
                    dve.wait_ge(sem.dve_step, me.step())
                for h in range(4 * i, 4 * i + 4):
                    for t, (a, n) in enumerate(((0, P), (P, 2 * P))):
                        k = 8 * t + h
                        ins = ts(sc[:, h, a:a + n], sc[:, h, a:a + n], soft[:, k:k + 1], None, MUL)
                    ins.then_inc(sem.mo_n, 1)

            def zc_in():
                dve.memset(glu[:, :, 0:DW_TAPS - 1], 0.0).then_inc(sem.dve_step, 1)
                dve.wait_ge(sem.dve_step, me.step())
                dve.wait_ge(sem.zc_t, me.seen("zc_t"))
                stt(glu[:, :, DW_TAPS - 1:], in2(cs), 1.0, in2(me.pair()[0][:, :]), ADD, MUL).then_inc(sem.zc_in, 1)
                dve.wait_ge(sem.zc_in, me.seen("zc_in"))

            def conv_dw(i):
                taps = (range(0, 10), range(10, 20), range(20, DW_TAPS))[i]
                conv(cv, glu, taps, lambda j, c: dw[:, 2 * j + c:2 * j + c + 1], 2, 0)

            def group_norm():
                for c in range(2):
                    ts(cv[:, c, :], cv[:, c, :], 0.5, col("b_dw_2", c), MUL, ADD).then_inc(sem.conv_done, 1)
                dve.wait_ge(sem.gn_mean, me.seen("gn_mean"))
                dve.wait_ge(sem.conv_done, me.seen("conv_done", 2))
                tt(cx, flat(cv), bank[4][:, :], SUB).then_inc(sem.dve_step, 1)
                dve.wait_ge(sem.dve_step, me.step())
                tt(cs, cx, cx, MUL).then_inc(sem.gn_sq, 1)
                dve.wait_ge(sem.gn_sd, me.seen("gn_sd"))
                dve.reciprocal(cs, cs).then_inc(sem.dve_step, 1)
                dve.wait_ge(sem.dve_step, me.step())
                tt(cx, cx, cs, MUL).then_inc(sem.dve_step, 1)
                dve.wait_ge(sem.dve_step, me.step())
                for c in range(2):
                    a = cx[:, c * T:(c + 1) * T]
                    ts(a, a, col("conv_gn_g_2", c), col("conv_gn_b_2", c), MUL, ADD).then_inc(sem.gn_z, 1)
                dve.wait_ge(sem.gn_t, me.seen("gn_t"))
                stt(cx, cs, 1.0, cx, ADD, MUL).then_inc(sem.dve_step, 1)
                dve.wait_ge(sem.dve_step, me.step())
                ts(flat(y2[:, 6:8, :]), cx, 0.5, None, MUL).then_inc(sem.yc2, 1)

            def post_norm(i):
                dve.wait_ge(sem.rstd, me.seen("rstd"))
                dve.wait_ge(sem.row_in, me.seen("row_in", 16))
                for t in range(TT):
                    for c in range(2):
                        b = bank[4 + 2 * t + c] if i == 2 else me.pair(1 - c)[t]
                        k = 2 * (POST + i) + t
                        stt(xn[:, t, c * NB:(c + 1) * NB], b[:, :], rstd[:, k:k + 1], row_g[:, c * NB:(c + 1) * NB],
                            MUL, MUL).then_inc(sem.post_read, 1)
                    dve.wait_ge(sem.post_read, me.seen("post_read", 2))
                    tt(x[:, t, :], x[:, t, :], xn[:, t, :], ADD).then_inc(sem.x_ready, 1)

            def x_scores():
                for h in range(4):
                    dve.wait_ge(sem.x_s, me.seen("x_s"))
                    dve.tensor_reduce(neg_max[:, 2 * h:2 * h + 2], in2(bank[4 + h][:, :]), AX.X, MAX, negate=True)\
                        .then_inc(sem.x_max, 1)
                for h in range(4):
                    dve.wait_ge(sem.x_p, me.seen("x_p"))
                    dve.reciprocal(soft[:, 2 * h:2 * h + 2], soft[:, 2 * h:2 * h + 2]).then_inc(sem.dve_step, 1)
                    dve.wait_ge(sem.dve_step, me.step())
                    for t in range(TT):
                        ins = ts(x_p[:, h, t, :], x_p[:, h, t, :], soft[:, 2 * h + t:2 * h + t + 1], None, MUL)
                    ins.then_inc(sem.x_n, 1)

            def ahead_of(key, mode):
                for g, _ in me.groups_of(key, mode):
                    split_low(g + LEAD + 1)

            setup()
            vectors()
            norm(0, "x")
            ahead_of("lru", "C")
            lru_conv()
            ahead_of("qk", "C")
            ahead_of("ifsv", "T")
            if_rows()
            ahead_of("vo", "T")
            ahead_of("sqk", "C")
            mlstm_cols()
            mlstm_qk()
            ahead_of(("gate", 0), "T")
            mlstm_scores()
            ahead_of(("gate", 1), "T")
            mlstm_out()
            lru_scan()
            ahead_of(("gate", 2), "T")
            sb_scores()
            ahead_of(("gate", 3), "T")
            ahead_of(("gate", 4), "T")
            ahead_of(("gate", 5), "T")
            split_y(6)
            for b in range(3):
                ahead_of(("branch", b), "W")
                merge(b)
            turn_merged()
            for c in range(2):
                ahead_of(("wo", c), "T")
                add_x(c)
            norm(1, "x")
            n1 = F1 // 256
            for c in range(n1 + 1):
                if c < n1:
                    ahead_of(("up1", c), "C")
                    hidden1(c)
                if c >= 1:
                    ahead_of(("down1", c - 1), "F")
            add_acc()
            final_norm()
            norm(2, "x")
            ahead_of("za", "T")
            za_in()
            ahead_of("q2", "C")
            ahead_of("k2", "C")
            moba_scores(0)
            ahead_of("zc", "C")
            zc_in()
            spatial()
            ahead_of("v2", "T")
            moba_scores(1)
            norm(3, "mem")
            conv_dw(0)
            ahead_of(("kv", 0), "C")
            moba_turn(0)
            conv_dw(1)
            ahead_of(("kv", 1), "C")
            moba_turn(1)
            conv_dw(2)
            ahead_of(("kv", 2), "T")
            group_norm()
            ahead_of(("kv", 3), "T")
            split_y(8)
            for c in range(2):
                ahead_of(("mixout", c), "T")
            post_norm(0)
            norm(4, "x")
            for c in range(2):
                ahead_of(("xq", c), "C")
            x_scores()
            x_out()
            for c in range(2):
                ahead_of(("xo", c), "T")
            post_norm(1)
            norm(5, "x")
            n2 = F2 // NB
            for c in range(n2 + 1):
                if c < n2:
                    ahead_of(("up2", c), "C")
                    hidden2(c)
                if c >= 1:
                    ahead_of(("down2", c - 1), "F")
            post_norm(2)

        @block.tensor
        def _(pe):
            me = Count()

            def mm(dst, lhs, rhs, start=True, stop=True, loose=True):
                return pe.matmul(dst, lhs, rhs, start=start, stop=stop, skip_group_check=loose)

            def mm3(dst, lhs_h, lhs_l, rhs_h, rhs_l, start, stop):
                mm(dst, lhs_l, rhs_h, start, False)
                mm(dst, lhs_h, rhs_l, False, False)
                return mm(dst, lhs_h, rhs_h, False, stop)

            def products(key, mode, *a):
                parity = me.pairs % 2
                if mode == "F":
                    c, nk, first, last = a
                width = a[0] if mode == "T" and a else NB
                ids = chunks[key]
                n_kt = sum(len(kts) for _, kts in ids)
                for g, kts in me.groups_of(key, mode):
                    pe.wait_ge(low_sem(g), before(g))
                    wh, wl = part(high, g), part(low, g)
                    for j, kt in enumerate(kts):
                        s0, s1 = kt == 0, kt == n_kt - 1
                        if mode == "T":
                            for t in range(TT):
                                tok = slice(t * P, (t + 1) * P)
                                ins = mm3(bank[2 * parity + t][:, 0:width], act_h[:, kt, tok], act_l[:, kt, tok],
                                          wh[:, j, 0:width], wl[:, j, 0:width], s0, s1)
                        elif mode == "C":
                            for i in range(4):
                                ch = slice(i * P, (i + 1) * P)
                                o = (i % 2) * T
                                ins = mm3(bank[2 * parity + i // 2][:, o:o + T], wh[:, j, ch], wl[:, j, ch],
                                          act_h[:, kt, :], act_l[:, kt, :], s0 and o == 0, s1)
                        elif mode == "W":
                            for c in range(2):
                                for t in range(TT):
                                    tok = slice(t * P, (t + 1) * P)
                                    k = 2 * a[0] + kt
                                    ins = mm3(bank[2 * ((parity + c) % 2) + t][:, :], act_h[:, k, tok],
                                              act_l[:, k, tok], wh[:, j, c * NB:(c + 1) * NB],
                                              wl[:, j, c * NB:(c + 1) * NB], s0, s1)
                        else:
                            for t in range(TT):
                                tok = slice(t * P, (t + 1) * P)
                                for n in range(2):
                                    ins = mm3(bank[4 + 2 * t + n][:, :], hid_h[c % 2][:, kt, tok],
                                              hid_l[c % 2][:, kt, tok], wh[:, j, n * NB:(n + 1) * NB],
                                              wl[:, j, n * NB:(n + 1) * NB], s0 and first, s1 and last)
                    ins.then_inc(sem.w_used, 1)

            def turn(dst, src):
                n = src.shape[0]
                return pe.transpose(dst, src, ident[0:n, 0:n])

            def vectors():
                pe.wait_ge(sem.ident, me.seen("ident"))
                pe.wait_ge(sem.vec_in, me.seen("vec_in", 16 * len(VEC_A)))
                turn(bank[4][:, 0:VEC_ROWS], vec_rows[0:VEC_ROWS, :]).then_inc(sem.vec_turned, 1)
                pe.wait_ge(sem.dw_in, me.seen("dw_in", 16))
                turn(bank[4][:, P:P + DW_ROWS], dw_rows[0:DW_ROWS, :]).then_inc(sem.vec_turned, 1)
                pe.wait_ge(sem.vec_out, me.seen("vec_out", 2))

            def turn_x():
                for q in range(4):
                    for k in range(2):
                        for t in range(TT):
                            kt = 2 * q + k
                            ins = turn(bank[4 + q][:, k * T + t * P:k * T + (t + 1) * P], xn[:, t, kt * P:(kt + 1) * P])
                    ins.then_inc(sem.turned, 1)
                pe.wait_ge(sem.act_hl, me.seen("act_hl", 4))

            def norm():
                pe.wait_ge(sem.xn, me.seen("xn", 2))
                turn_x()


            def if_rows():
                pe.wait_ge(sem.ifsv_in, 2)
                for k in range(2):
                    for t in range(TT):
                        ins = turn(bank[6][0:4, k * T + t * P:k * T + (t + 1) * P], if_tok[:, t, 4 * k:4 * k + 4])
                ins.then_inc(sem.if_turned, 1)

            def lru_gates():
                pe.wait_ge(sem.lru_conv, me.seen("lru_conv", 2))
                pe.wait_ge(sem.gate_w, me.seen("gate_w", 16 * 8))
                for i in range(2):
                    for c in range(2):
                        ins = mm(bank[4 + i][:, c * T:(c + 1) * T], gate_w[i][:, c, :], xa[:, c, :])
                ins.then_inc(sem.lru_z, 1)

            def mlstm_cols():
                pe.wait_ge(sem.exp_m, me.seen("exp_m"))
                for k, r in enumerate((1, 5)):
                    for t in range(TT):
                        o = 8 * k + 4 * t
                        ins = turn(bank[7][:, o:o + 4], rows[0:4, r, t * P:(t + 1) * P])
                ins.then_inc(sem.cols_turned, 1)
                pe.wait_ge(sem.consts, me.seen("consts", 5))
                pe.wait_ge(sem.lru_t, 2)
                for h in range(4):
                    ins = mm(bank[4 + h // 2][:, (h % 2) * T:(h % 2 + 1) * T], head_row[0:4, h, :], rows[0:4, 4, :])
                    if h % 2:
                        ins.then_inc(sem.m_bc, 1)

            def scores(dst, q, k, h):
                p_ = slice(64 * (h % 2), 64 * (h % 2) + 64)
                mm(dst[:, 0:T], k[p_, h // 2, 0:P], q[p_, h // 2, :])
                return mm(dst[:, T:DIAG], k[p_, h // 2, P:T], q[p_, h // 2, P:T], start=False)

            def mlstm_scores():
                pe.wait_ge(sem.m_qk, me.seen("m_qk"))
                pe.wait_ge(sem.m_e, me.seen("m_e", 8))
                pe.wait_ge(sem.cols, me.seen("cols"))
                for h in range(4):
                    scores(bank[(6, 7, 4, 5)[h]], m_qk[:, 0:2, :], m_qk[:, 2:4, :], h).then_inc(sem.m_s, 1)

            def mlstm_out():
                pe.wait_ge(sem.m_p, me.seen("m_p", 4))
                pe.wait_ge(sem.vo_in, 2)
                for h in range(4):
                    o = slice(65 * h, 65 * h + 65)
                    mm(bank[6][:, o], m_e[:, h, 0:P], m_v[:, 0, h, :], start=h == 0)
                    mm(bank[7][:, o], m_e[:, h, P:T], m_v[:, 0, h, :], start=h == 0, stop=False)
                    ins = mm(bank[7][:, o], m_e[:, h, T:DIAG], m_v[:, 1, h, :], start=False)
                ins.then_inc(sem.m_y, 1)

            def turn_256(dst, src):
                for c in range(2):
                    for t in range(TT):
                        ins = turn(dst[:, c * T + t * P:c * T + (t + 1) * P], src[:, t, c * P:(c + 1) * P])
                return ins

            def mlstm_turn():
                pe.wait_ge(sem.m_yb, me.seen("m_yb", 2))
                turn_256(bank[4], m_tmp).then_inc(sem.m_turned, 1)

            def sb_scores():
                pe.wait_ge(sem.sqk_in, 2)
                pe.wait_ge(sem.y_b, me.seen("y_b"))
                for h in range(4):
                    scores(bank[4 + h], s_q, s_k, h).then_inc(sem.sb_z, 1)

            def sb_sums():
                pe.wait_ge(sem.sb_masked, me.seen("sb_masked", 2))
                pe.wait_ge(sem.sb_sp, me.seen("sb_sp", 4))
                for h in range(4):
                    b, a = bank[4 + h], sb_a[:, h, :]
                    scores(b, s_q, s_k, h)
                    mm(b[:, 0:T], neg_tri, a[:, 0:T], start=False)
                    mm(b[:, P:T], neg_one, a[:, T:DIAG], start=False)
                    mm(b[:, T:DIAG], neg_tri, a[:, T:DIAG], start=False).then_inc(sem.sb_sum, 1)

            def weighted(dst, v, p, h, hh, start):
                q = slice(64 * (h % 2), 64 * (h % 2) + 64)
                d = slice(64 * h, 64 * h + 64)
                mm(dst[q, 0:T], v[:, 0, d], p[:, hh, 0:T], start=start, stop=False)
                return mm(dst[q, P:T], v[:, 1, d], p[:, hh, T:DIAG], start=False)

            def sb_out():
                pe.wait_ge(sem.sb_a_masked, me.seen("sb_a_masked", 2))
                pe.wait_ge(sem.sb_a, me.seen("sb_a", 4))
                for h in (0, 1, 2, 3):
                    ins = weighted(bank[4][:, (h // 2) * T:(h // 2 + 1) * T], s_v, sb_a, h, h, h < 2)
                ins.then_inc(sem.sb_o, 1)

            def turn_merged():
                pe.wait_ge(sem.merged, me.seen("merged", 8))
                pe.wait_ge(sem.y_c, 1)
                turn_x()


            def za_in():
                pe.wait_ge(sem.ws_masked, me.seen("ws_masked"))
                for h in range(4):
                    ins = turn(bank[5][:, h * P:(h + 1) * P], spatial_w[:, h, :])
                ins.then_inc(sem.ws_turned, 1)

            def moba_scores(i):
                pe.wait_ge(sem.qk2_in, 4)
                if i == 0:
                    pe.wait_ge(sem.ws_out, me.seen("ws_out"))
                else:
                    pe.wait_ge(sem.ya2, 1)
                for h in range(4 * i, 4 * i + 4):
                    q = slice(64 * (h % 2), 64 * (h % 2) + 64)
                    b = bank[4 + h % 4]
                    mm(b[:, 0:P], q2[q, h // 2, 0:P], k2[q, h // 2, 0:P])
                    mm(b[:, P:DIAG], q2[q, h // 2, P:T], k2[q, h // 2, :], start=False).then_inc(sem.mo_s, 1)
                pe.wait_ge(sem.mo_sc, me.seen("mo_sc", 4))

            def spatial():
                pe.wait_ge(sem.vn, me.seen("vn", 2))
                for t in range(TT):
                    for h in range(4):
                        o = t * T + h * 64
                        ins = mm(bank[4][:, o:o + 64], spatial_t[:, h, :], vn[:, t, h * 64:h * 64 + 64])
                ins.then_inc(sem.mixed, 1)
                pe.wait_ge(sem.ya2_tok, me.seen("ya2_tok", 2))
                turn_256(bank[5], vn).then_inc(sem.ya2_turned, 1)

            def moba_turn(i):
                pe.wait_ge(sem.v2_in, 2)
                for h in range(4):
                    pe.wait_ge(sem.mo_n, me.seen("mo_n"))
                    for k in range(3):
                        ins = turn(bank[4 + h][:, k * P:(k + 1) * P], sc[:, 4 * i + h, k * P:(k + 1) * P])
                    ins.then_inc(sem.mo_turned, 1)
                pe.wait_ge(sem.mo_t, me.seen("mo_t", 4))
                for c in range(2):
                    for hh in range(2):
                        h = 2 * c + hh
                        ins = weighted(bank[4 + c], v2, pt, 4 * i + h, h, True)
                    ins.then_inc(sem.mo_o, 1)
                pe.wait_ge(sem.yb2, me.seen("yb2", 2))

            def group_norm():
                pe.wait_ge(sem.conv_done, me.seen("conv_done", 2))
                mm(bank[4][:, :], block_mean[:, :], flat(cv)).then_inc(sem.gn_mean, 1)
                pe.wait_ge(sem.gn_sq, me.seen("gn_sq"))
                mm(bank[5][:, :], block_mean[:, :], cs).then_inc(sem.gn_var, 1)

            def x_scores():
                pe.wait_ge(sem.xq_in, 4)
                for h in range(4):
                    for t in range(TT):
                        for k in range(2):
                            ins = mm(bank[4 + h][:, t * T:(t + 1) * T], x_q[:, 2 * h + k, t * P:(t + 1) * P],
                                     k_mem[:, 2 * h + k, :], start=k == 0, stop=k == 1)
                    ins.then_inc(sem.x_s, 1)
                for h in range(4):
                    pe.wait_ge(sem.x_n, me.seen("x_n"))
                    for m in range(2):
                        for t in range(TT):
                            ins = turn(bank[4 + h][:, m * T + t * P:m * T + (t + 1) * P],
                                       x_p[:, h, t, m * P:(m + 1) * P])
                    ins.then_inc(sem.x_turned, 1)

            def x_out():
                pe.wait_ge(sem.x_t, me.seen("x_t", 4))
                for h in range(4):
                    for c in range(2):
                        for m in range(2):
                            ch = slice((2 * h + c) * P, (2 * h + c + 1) * P)
                            ins = mm(bank[4 + h][:, c * T:(c + 1) * T], v_mem[:, m, ch], x_pt[:, h, m, :],
                                     start=m == 0, stop=m == 1)
                    ins.then_inc(sem.x_o, 1)
                pe.wait_ge(sem.act_hl, me.seen("act_hl", 4))

            vectors()
            norm()
            products("lru", "C")
            products("qk", "C")
            pe.wait_ge(sem.lru_in, 2)
            products("ifsv", "T", 264)
            if_rows()
            pe.wait_ge(sem.qk_in, 2)
            products("vo", "T")
            lru_gates()
            pe.wait_ge(sem.ifsv_in, 2)
            products("sqk", "C")
            mlstm_cols()
            pe.wait_ge(sem.vo_in, 2)
            products(("gate", 0), "T")
            mlstm_scores()
            pe.wait_ge(sem.sqk_in, 2)
            products(("gate", 1), "T")
            mlstm_out()
            pe.wait_ge(sem.gate_in, 2)
            products(("gate", 2), "T")
            mlstm_turn()
            sb_scores()
            pe.wait_ge(sem.gate_in, 4)
            products(("gate", 3), "T")
            sb_sums()
            pe.wait_ge(sem.gate_in, 6)
            products(("gate", 4), "T")
            sb_out()
            pe.wait_ge(sem.gate_in, 8)
            products(("gate", 5), "T")
            pe.wait_ge(sem.act_hl, me.seen("act_hl"))
            for b in range(3):
                pe.wait_ge(sem.gate_in, 12)
                if b:
                    pe.wait_ge(sem.merge, 4 * b)
                products(("branch", b), "W", b)
            turn_merged()
            pe.wait_ge(sem.merge, 12)
            for c in range(2):
                products(("wo", c), "T")
            norm()
            n1 = F1 // 256
            for c in range(n1 + 1):
                if c < n1:
                    if c >= 2:
                        pe.wait_ge(sem.hid_a, c - 1)
                    products(("up1", c), "C")
                if c >= 1:
                    pe.wait_ge(sem.hid_hl, c)
                    products(("down1", c - 1), "F", c - 1, 2, c == 1, c == n1)
            norm()
            products("za", "T")
            za_in()
            products("q2", "C")
            pe.wait_ge(sem.za_in, 2)
            products("k2", "C")
            moba_scores(0)
            pe.wait_ge(sem.qk2_in, 2)
            products("zc", "C")
            spatial()
            pe.wait_ge(sem.qk2_in, 4)
            products("v2", "T")
            moba_scores(1)
            norm()
            pe.wait_ge(sem.zc_in, 1)
            products(("kv", 0), "C")
            moba_turn(0)
            pe.wait_ge(sem.v2_in, 2)
            products(("kv", 1), "C")
            moba_turn(1)
            pe.wait_ge(sem.kv_in, 2)
            products(("kv", 2), "T")
            group_norm()
            pe.wait_ge(sem.kv_in, 4)
            products(("kv", 3), "T")
            pe.wait_ge(sem.act_hl, me.seen("act_hl"))
            pe.wait_ge(sem.kv_in, 8)
            for c in range(2):
                products(("mixout", c), "T")
            norm()
            for c in range(2):
                products(("xq", c), "C")
            x_scores()
            x_out()
            for c in range(2):
                products(("xo", c), "T")
            norm()
            n2 = F2 // NB
            for c in range(n2 + 1):
                if c < n2:
                    if c >= 2:
                        pe.wait_ge(sem.hid_a, F1 // 256 + 2 * (c - 1))
                    products(("up2", c), "C")
                if c >= 1:
                    pe.wait_ge(sem.hid_hl, F1 // 256 + 2 * c)
                    products(("down2", c - 1), "F", c - 1, 4, c == 1, c == n2)


_INS = ["x", "norm_mix_g", "w_in", "conv_lru_w", "lru_wa", "lru_ba", "lru_wx", "lru_bx", "lru_lambda",
        "conv_mlstm_w", "mlstm_ig_b", "mlstm_fg_b", "w_out_lru", "w_out_mlstm", "w_out_sb", "w_o", "norm_ffn_g",
        "w_ffn_in", "w_ffn_out", "final_norm_g", "mem_2", "pre_mix_g_2", "w_in_2", "gate_ln_g_2", "gate_ln_b_2",
        "w_s_2", "b_s_2", "w_dw_2", "b_dw_2", "conv_gn_g_2", "conv_gn_b_2", "w_out_2", "post_mix_g_2", "pre_x_g_2",
        "mem_g_2", "w_xq_2", "w_xkv_2", "w_xo_2", "post_x_g_2", "pre_ffn_g_2", "w_ff1_2", "w_ff2_2", "post_ffn_g_2"]
_FLAT = {name for name, _ in VEC_A} | {"w_dw_2"}


def kernel(**inputs):
    import numpy as _np
    import concourse.bacc as _bacc
    from concourse.bass_utils import run_bass_kernel_spmd as _run

    nc = _bacc.Bacc("TRN2", target_bir_lowering=False, num_devices=1)
    arrays, args = {}, {}
    for name in _INS:
        a = _np.ascontiguousarray(inputs[name])
        if a.ndim > 1 and a.shape[0] == 1:
            a = a[0]
        if name in _FLAT:
            a = a.reshape(-1)
        arrays[f"in_{name}_dram"] = a
        args[name] = nc.dram_tensor(f"in_{name}_dram", a.shape, mybir.dt.from_np(a.dtype), kind="ExternalInput").ap()
    out = nc.dram_tensor("out_0_dram", (T, D), F32, kind="ExternalOutput").ap()
    two_blocks(nc, args, out)
    r = _run(nc, [arrays], core_ids=[0])
    return r.results[0]["out_0_dram"].reshape(1, T, D)
```

```python
from contextlib import ExitStack
import math

import concourse.bass as bass
from concourse import mybir

P = 128
T = 256
TT = T // P
D = 1024
KD = D // P
F1 = 2816
F2 = 4096
NB = 512
EPS = 1e-6
RAW = 3
SPLIT = 3
ARENA = 17466
LEAD = 2
GROUP = 2048
DIAG = 3 * P

F32 = mybir.dt.float32
F32R = mybir.dt.float32r
ALU = mybir.AluOpType
ACT = mybir.ActivationFunctionType
AX = mybir.AxisListType

VEC_A = [("norm_mix_g", 8), ("norm_ffn_g", 8), ("pre_mix_g_2", 8), ("mem_g_2", 8), ("pre_x_g_2", 8),
         ("pre_ffn_g_2", 8), ("lru_ba", 2), ("lru_bx", 2), ("lru_lambda", 2), ("conv_lru_w", 8),
         ("conv_mlstm_w", 16), ("b_dw_2", 2), ("conv_gn_g_2", 2), ("conv_gn_b_2", 2), ("b_s_2", 4)]
VEC_OFF = {}
_n = 0
for _name, _rows in VEC_A:
    VEC_OFF[_name] = _n
    _n += _rows
VEC_ROWS = _n
DW_TAPS = 31
DW_ROWS = 2 * DW_TAPS


def plan_weights(w):
    groups, chunks = [], {}

    def add(key, src, row0, kts, cols, view):
        ids = []
        per = GROUP // view
        for k in range(0, kts, per):
            nk = min(per, kts - k)
            dmas = [(src, row0 + k * P, nk, d, c, n) for d, c, n in cols]
            groups.append((dmas, view, nk, max(d + n for d, _, n in cols)))
            ids.append((len(groups) - 1, list(range(k, k + nk))))
        chunks[key] = ids

    win = w["w_in"]
    for key, cols in (("lru", [(0, 0, 512)]), ("qk", [(0, 512, 512)]), ("ifsv", [(0, 1536, 8), (8, 2056, 256)]),
                      ("vo", [(0, 1024, 512)]), ("sqk", [(0, 1544, 512)])):
        add(key, win, 0, KD, cols, NB)
    for c in range(6):
        add(("gate", c), win, 0, KD, [(0, 2312 + c * NB, NB)], NB)
    for b, name in enumerate(("w_out_lru", "w_out_mlstm", "w_out_sb")):
        add(("branch", b), w[name], 0, 2, [(0, 0, D)], D)
    for c in range(2):
        add(("wo", c), w["w_o"], 0, KD, [(0, c * NB, NB)], NB)
    n1 = F1 // 256
    for c in range(n1 + 1):
        if c < n1:
            add(("up1", c), w["w_ffn_in"], 0, KD, [(0, c * 256, 256), (256, F1 + c * 256, 256)], NB)
        if c >= 1:
            add(("down1", c - 1), w["w_ffn_out"], (c - 1) * 256, 2, [(0, 0, D)], D)

    def add_kv(c):
        add(("kv", c), w["w_xkv_2"], 0, KD, [(0, c * NB, NB)], NB)

    add_kv(0)
    for key, c in (("zc", 2048), ("q2", 512), ("k2", 1024), ("za", 0), ("v2", 1536)):
        add(key, w["w_in_2"], 0, KD, [(0, c, NB)], NB)
    for c in range(1, 4):
        add_kv(c)
    for key, row in (("mix_top", 0), ("mix_bottom", 4 * P)):
        for c in range(2):
            add((key, c), w["w_out_2"], row, 4, [(0, c * NB, NB)], NB)
    for c in range(2):
        add(("xq", c), w["w_xq_2"], 0, KD, [(0, c * NB, NB)], NB)
    for c in range(2):
        add(("xo", c), w["w_xo_2"], 0, KD, [(0, c * NB, NB)], NB)
    n2 = F2 // NB
    for c in range(n2 + 1):
        if c < n2:
            add(("up2", c), w["w_ff1_2"], 0, KD, [(0, c * NB, NB)], NB)
        if c >= 1:
            add(("down2", c - 1), w["w_ff2_2"], (c - 1) * NB, 4, [(0, 0, D)], D)
    return groups, chunks


class Semaphores:

    def __init__(self, new):
        self.act_h = new("act_h")
        self.act_hl = new("act_hl")
        self.act_step = new("act_step")
        self.bias_in = new("bias_in")
        self.cols = new("cols")
        self.cols_turned = new("cols_turned")
        self.consts = new("consts")
        self.conv_done = new("conv_done")
        self.dist = new("dist")
        self.dve_step = new("dve_step")
        self.dw_in = new("dw_in")
        self.exp_m = new("exp_m")
        self.gate_in = new("gate_in")
        self.gate_w = new("gate_w")
        self.gn_mean = new("gn_mean")
        self.gn_sd = new("gn_sd")
        self.gn_sq = new("gn_sq")
        self.gn_t = new("gn_t")
        self.gn_var = new("gn_var")
        self.gn_y = new("gn_y")
        self.gn_z = new("gn_z")
        self.hid_a = new("hid_a")
        self.hid_h = new("hid_h")
        self.hid_hl = new("hid_hl")
        self.hid_t = new("hid_t")
        self.ident = new("ident")
        self.if_rows = new("if_rows")
        self.if_turned = new("if_turned")
        self.ifsv_in = new("ifsv_in")
        self.kv_in = new("kv_in")
        self.lam_e = new("lam_e")
        self.ln_in = new("ln_in")
        self.ln_rstd = new("ln_rstd")
        self.ln_stat = new("ln_stat")
        self.log_f = new("log_f")
        self.low_by_dve = new("low_by_dve")
        self.low_by_pool = new("low_by_pool")
        self.lru_cols = new("lru_cols")
        self.lru_conv = new("lru_conv")
        self.lru_gelu = new("lru_gelu")
        self.lru_in = new("lru_in")
        self.lru_sqrt = new("lru_sqrt")
        self.lru_t = new("lru_t")
        self.lru_tg = new("lru_tg")
        self.lru_z = new("lru_z")
        self.m_bc = new("m_bc")
        self.m_conv = new("m_conv")
        self.m_e = new("m_e")
        self.m_e_masked = new("m_e_masked")
        self.m_p = new("m_p")
        self.m_qk = new("m_qk")
        self.m_s = new("m_s")
        self.m_stab = new("m_stab")
        self.m_tanh = new("m_tanh")
        self.m_turned = new("m_turned")
        self.m_y = new("m_y")
        self.m_yb = new("m_yb")
        self.mem_in = new("mem_in")
        self.merge = new("merge")
        self.merged = new("merged")
        self.mixed = new("mixed")
        self.mo_max = new("mo_max")
        self.mo_n = new("mo_n")
        self.mo_o = new("mo_o")
        self.mo_p = new("mo_p")
        self.mo_s = new("mo_s")
        self.mo_sc = new("mo_sc")
        self.mo_t = new("mo_t")
        self.mo_turned = new("mo_turned")
        self.pool_step = new("pool_step")
        self.post_read = new("post_read")
        self.post_sum = new("post_sum")
        self.qk2_in = new("qk2_in")
        self.qk_in = new("qk_in")
        self.row_in = new("row_in")
        self.rstd = new("rstd")
        self.sb_a = new("sb_a")
        self.sb_a_masked = new("sb_a_masked")
        self.sb_ln = new("sb_ln")
        self.sb_masked = new("sb_masked")
        self.sb_o = new("sb_o")
        self.sb_sp = new("sb_sp")
        self.sb_sum = new("sb_sum")
        self.sb_z = new("sb_z")
        self.sqk_in = new("sqk_in")
        self.stored = new("stored")
        self.sumsq = new("sumsq")
        self.turned = new("turned")
        self.v2_in = new("v2_in")
        self.vec_in = new("vec_in")
        self.vec_out = new("vec_out")
        self.vec_turned = new("vec_turned")
        self.vn = new("vn")
        self.vo_in = new("vo_in")
        self.w_high = new("w_high")
        self.w_used = new("w_used")
        self.ws_in = new("ws_in")
        self.ws_masked = new("ws_masked")
        self.ws_out = new("ws_out")
        self.ws_turned = new("ws_turned")
        self.x_in = new("x_in")
        self.x_max = new("x_max")
        self.x_n = new("x_n")
        self.x_o = new("x_o")
        self.x_p = new("x_p")
        self.x_ready = new("x_ready")
        self.x_s = new("x_s")
        self.x_t = new("x_t")
        self.x_turned = new("x_turned")
        self.zg = new("zg")
        self.tile0_used = new("tile0_used")
        self.x1_in = new("x1_in")
        self.diag = new("diag")
        self.xq_in = new("xq_in")
        self.y_a = new("y_a")
        self.y_b = new("y_b")
        self.y_c = new("y_c")
        self.ya2_tok = new("ya2_tok")
        self.ya2_turned = new("ya2_turned")
        self.za_in = new("za_in")
        self.zc_in = new("zc_in")
        self.zc_t = new("zc_t")


def two_blocks(nc, w, out):
    groups, chunks = plan_weights(w)
    n_groups = len(groups)
    ctx = ExitStack()
    with ctx:
        def sb(name, shape, dt=F32):
            return ctx.enter_context(nc.sbuf_tensor(name, shape, dt))

        raw = [sb(f"raw{s}", [P, GROUP]) for s in range(RAW)]
        high = [sb(f"high{s}", [P, GROUP], F32R) for s in range(SPLIT)]
        low = [sb(f"low{s}", [P, GROUP], F32R) for s in range(SPLIT)]
        act_h = sb("act_h", [P, KD, T], F32R)
        act_l = sb("act_l", [P, KD, T], F32R)
        hid_h = [sb(f"hid_h{i}", [P, 4, T], F32R) for i in range(2)]
        hid_l = [sb(f"hid_l{i}", [P, 4, T], F32R) for i in range(2)]
        hid1_h = [sb(f"hid1_h{i}", [P, 2, T], F32R) for i in range(2)]
        hid1_l = [sb(f"hid1_l{i}", [P, 2, T], F32R) for i in range(2)]
        x = sb("x", [P, TT, D])
        xn = sb("xn", [P, TT, D])
        diag = sb("diag", [P, TT, P])
        row_g = sb("row_g", [P, D])
        vec_rows = sb("vec_rows", [P, P])
        dw_rows = sb("dw_rows", [P, P])
        vec = sb("vec", [P, VEC_ROWS])
        dw = sb("dw", [P, DW_ROWS])
        ident = sb("ident", [P, P])
        block_mean = sb("block_mean", [P, P])
        if_bias = sb("if_bias", [4, 2])
        neg_half = sb("neg_half", [P, 4])
        sums = sb("sums", [P, TT, 2])
        var = sb("var", [P, 32])
        rstd = sb("rstd", [P, 32])
        tiny = sb("tiny", [P, 40])
        neg_max = sb("neg_max", [P, 16])
        soft = sb("soft", [P, 16])

        arena = sb("arena", [P, ARENA])
        top = [0]

        def carve(*shape):
            size = math.prod(shape)
            a = arena[:, top[0]:top[0] + size]
            top[0] += size
            assert top[0] <= ARENA, top[0]
            if len(shape) == 2:
                a = a.rearrange("p (a b) -> p a b", a=shape[0])
            if len(shape) == 3:
                a = a.rearrange("p (a b c) -> p a b c", a=shape[0], b=shape[1])
            return a

        y = carve(6, T)
        gates = carve(TT, 3 * D)
        m_v = carve(TT, 4, 65)
        m_o = carve(TT, T)
        s_q = carve(2, T)
        s_k = carve(2, T)
        s_v = carve(TT, T)
        if_tok = carve(TT, 8)
        cols = carve(2, TT, 4)
        MEM = top[0]
        m_e = carve(4, DIAG)
        m_tmp = carve(TT, T)
        rows = carve(6, T)
        neg_tri = carve(P)
        neg_one = carve(P)
        head_row = carve(4, P)
        gate_w = [carve(2, P), carve(2, P)]
        ones4 = carve(T)
        era = top[0]
        lru_x = carve(2, T + 3)
        lru_g = carve(2, T)
        m_x = carve(4, T + 3)
        m_x_used = m_x[:, :, 0:T].rearrange("p (a b) s -> p a b s", b=2)
        m_qk = gates[:, :, 2 * NB:3 * NB].rearrange("p a (b s) -> p a b s", b=2)
        top1 = top[0]
        top[0] = era
        sb_a = carve(4, DIAG)
        top[0] = max(top[0], top1)
        l_r, l_i, l_u, l_a = (gates[:, :, 2 * D + i * T:2 * D + (i + 1) * T] for i in range(4))
        l_s, xa = (gates[:, :, D + NB + i * T:D + NB + (i + 1) * T] for i in range(2))
        mem = arena[:, MEM:MEM + TT * D].rearrange("p (t d) -> p t d", t=TT)
        top[0] = 0
        h_act = carve(2 * T)
        h_tmp = carve(2 * T)
        h_val = carve(2 * T)
        top[0] = 0
        spatial_w = carve(4, P)
        spatial_t = carve(4, P)
        k_mem = carve(KD, T)
        v_mem = carve(TT, D)
        attn = top[0]
        sc = carve(8, DIAG)
        pt = carve(4, DIAG)
        q2 = carve(4, T)
        k2 = carve(4, T)
        v2 = carve(TT, NB)
        zg = carve(TT, NB)
        vn = carve(TT, T)
        dist = carve(DIAG)
        glu = carve(2, T + DW_TAPS - 1)
        cv = carve(2, T)
        cx = carve(2 * T)
        cs = carve(2 * T)
        ln_g = carve(T)
        ln_b = carve(T)
        top[0] = attn
        post_junk = carve(TT, D)
        top[0] = attn
        x_p = carve(4, TT, T)
        x_pt = carve(4, TT, T)
        x_q = carve(KD, T)

        bank = [ctx.enter_context(nc.psum_tensor(f"bank{i}", [P, NB], F32)) for i in range(8)]

        sem = Semaphores(lambda name: ctx.enter_context(nc.semaphore(name)))
        raw_in = [ctx.enter_context(nc.semaphore(f"raw_in{s}")) for s in range(RAW)]

        def arrived(g):
            return 16 * sum(len(groups[i][0]) for i in range(g % RAW, g + 1, RAW))

        def low_sem(g):
            return sem.low_by_pool if g % 2 else sem.low_by_dve

        def before(g):
            return g // 2 + 1

        def part(tiles, g):
            _, view, nk, width = groups[g]
            return tiles[g % len(tiles)][:, :].rearrange("p (k n) -> p k n", n=view)[:, 0:nk, 0:width]

        def split_of(kt, is_mem):
            if is_mem:
                return hid_h[kt // 4][:, kt % 4, :], hid_l[kt // 4][:, kt % 4, :]
            return act_h[:, kt, :], act_l[:, kt, :]

        def hidden_of(c, first_ffn):
            return (hid1_h[c % 2], hid1_l[c % 2]) if first_ffn else (hid_h[c % 2], hid_l[c % 2])

        def col(name, i=0):
            return vec[:, VEC_OFF[name] + i:VEC_OFF[name] + i + 1]

        def f32(ap):
            return ap.bitcast(F32)

        def flat(ap):
            return ap.rearrange("p a b -> p (a b)")

        def in2(ap):
            return ap.rearrange("p (a b) -> p a b", a=2)

        NORM_GAIN = ["norm_mix_g", "norm_ffn_g", "pre_mix_g_2", "mem_g_2", "pre_x_g_2", "pre_ffn_g_2"]
        X_READY_END = 4 + 4 + 2 + 3 * TT
        FINAL, POST = 6, 7
        SQRT_2_PI = math.sqrt(2 / math.pi)
        block = ctx.enter_context(nc.Block())

        class Count:

            def __init__(self):
                self.steps, self.counts, self.used, self.pairs = 0, {}, 0, 0

            def seen(self, name, n=1):
                self.counts[name] = self.counts.get(name, 0) + n
                return self.counts[name]

            def step(self):
                self.steps += 1
                return self.steps

            def pair(self, back=0):
                i = 2 * ((self.pairs - 1 - back) % 2)
                return bank[i], bank[i + 1]

            def groups_of(self, key, mode):
                for g, kts in chunks[key]:
                    yield g, kts
                    self.used += 1
                self.pairs += {"W": 2, "F": 0}.get(mode, 1)

        @block.sync
        def _(sp):
            for g, (dmas, view, nk, width) in enumerate(groups):
                if g >= RAW:
                    sp.wait_ge(low_sem(g - RAW), before(g - RAW))
                tile = part(raw, g)
                for src, row, n, d, c, cw in dmas:
                    sp.dma_start(tile[:, 0:n, d:d + cw],
                                 src[row:row + n * P, c:c + cw].rearrange("(k p) n -> p k n", p=P))\
                      .then_inc(raw_in[g % RAW], 16)
            for t in range(TT):
                sp.wait_ge(sem.x_ready, X_READY_END - TT + 1 + t)
                sp.dma_start(out[t * P:(t + 1) * P, :], x[:, t, :]).then_inc(sem.stored, 16)
            sp.wait_ge(sem.stored, 16 * TT)

        @block.gpsimd
        def _(pool):
            me = Count()
            split = [0]

            def split_low(upto):
                while split[0] < min(upto, n_groups):
                    g = split[0]
                    split[0] += 1
                    if g % 2 == 0:
                        continue
                    pool.wait_ge(sem.w_high, g + 1)
                    if g >= SPLIT:
                        pool.wait_ge(sem.w_used, g - SPLIT + 1)
                    pool.tensor_tensor(part(low, g), part(raw, g), f32(part(high, g)), ALU.subtract)\
                        .then_inc(sem.low_by_pool, 1)

            def rsqrt(k, t, halves):
                v = var[:, 2 * k + t:2 * k + t + 1]
                if halves:
                    pool.tensor_scalar(v, sums[:, t, 0:1], sums[:, t, 1:2], EPS, ALU.add, ALU.add)\
                        .then_inc(sem.pool_step, 1)
                else:
                    pool.tensor_scalar(v, sums[:, t, 0:1], EPS, None, ALU.add).then_inc(sem.pool_step, 1)
                pool.wait_ge(sem.pool_step, me.step())
                pool.tensor_tensor(rstd[:, 2 * k + t:2 * k + t + 1], v, neg_half[:, 0:1], ALU.pow)\
                    .then_inc(sem.rstd, 1)

            def setup():
                pool.memset(ident[:, :], 0.0).then_inc(sem.pool_step, 1)
                pool.wait_ge(sem.pool_step, me.step())
                pool.affine_select(out=ident[:, :], in_=ident[:, :], compare_op=ALU.not_equal, fill=1.0, base=0,
                                   pattern=[[-1, P]], channel_multiplier=1).then_inc(sem.ident, 1)
                pool.memset(gate_w[0], 0.0)
                pool.memset(neg_half[:, :], -0.5)
                pool.memset(gate_w[1], 0.0).then_inc(sem.pool_step, 1)
                pool.wait_ge(sem.pool_step, me.step())
                for i, name in enumerate(("lru_wa", "lru_wx")):
                    for g in range(4):
                        q = 64 * (g % 2)
                        pool.dma_start(gate_w[i][q:q + 64, g // 2, q:q + 64], w[name][g]).then_inc(sem.gate_w, 16)
                split_low(LEAD)
                pool.memset(neg_tri, -1.0).then_inc(sem.pool_step, 1)
                pool.wait_ge(sem.pool_step, me.step())
                pool.affine_select(out=neg_tri, in_=neg_tri, compare_op=ALU.is_ge, fill=0.0, base=0,
                                   pattern=[[-1, P]], channel_multiplier=1).then_inc(sem.consts, 1)
                pool.memset(neg_one, -1.0).then_inc(sem.consts, 1)
                pool.memset(head_row[0:4], 0.0).then_inc(sem.pool_step, 1)
                pool.wait_ge(sem.pool_step, me.step())
                pool.affine_select(out=head_row[0:4], in_=head_row[0:4], compare_op=ALU.not_equal, fill=1.0, base=0,
                                   pattern=[[-1, 4], [0, P]], channel_multiplier=1).then_inc(sem.consts, 1)
                pool.memset(block_mean[:, :], 0.0).then_inc(sem.pool_step, 1)
                pool.wait_ge(sem.pool_step, me.step())
                pool.memset(block_mean[0:64, 0:64], 1 / 64).then_inc(sem.consts, 1)
                pool.wait_ge(sem.consts, me.seen("consts", 4))
                pool.memset(block_mean[64:P, 64:P], 1 / 64).then_inc(sem.consts, 1)
                pool.wait_ge(sem.consts, me.seen("consts"))

            def norm(n):
                for t in range(TT):
                    pool.wait_ge(sem.sumsq, me.seen("sumsq", {FINAL: 2, 1: 3 - 2 * t}.get(n, 1)))
                    rsqrt(n, t, n in (FINAL, 1))

            def mlstm_cols():
                pool.wait_ge(sem.m_e, me.seen("m_e", 8))
                for a in (0, 2 * P):
                    part_e = m_e[:, :, a:a + P]
                    pool.affine_select(out=part_e, in_=part_e, compare_op=ALU.is_ge, fill=0.0, base=0,
                                       pattern=[[0, 4], [1, P]], channel_multiplier=-1).then_inc(sem.m_e_masked, 1)

            def strict(done, masked):
                pool.wait_ge(done, 4)
                for a in (0, 2 * P):
                    part_a = sb_a[:, :, a:a + P]
                    pool.affine_select(out=part_a, in_=part_a, compare_op=ALU.is_gt, fill=0.0, base=0,
                                       pattern=[[0, 4], [1, P]], channel_multiplier=-1).then_inc(masked, 1)

            def block2_masks():
                pool.wait_ge(sem.ws_in, me.seen("ws_in", 16))
                pool.affine_select(out=spatial_w, in_=spatial_w, compare_op=ALU.is_ge, fill=0.0, base=0,
                                   pattern=[[0, 4], [-1, P]], channel_multiplier=1).then_inc(sem.ws_masked, 1)
                pool.iota(dist[:, 0:P], [[1, P]], base=0, channel_multiplier=-1,
                          allow_small_or_imprecise_dtypes=True).then_inc(sem.pool_step, 1)
                pool.wait_ge(sem.pool_step, me.step())
                pool.iota(dist[:, P:DIAG], [[1, 2 * P]], base=-P, channel_multiplier=-1,
                          allow_small_or_imprecise_dtypes=True).then_inc(sem.pool_step, 1)
                pool.wait_ge(sem.pool_step, me.step())
                for a in (0, 2 * P):
                    pool.affine_select(out=dist[:, a:a + P], in_=dist[:, a:a + P], compare_op=ALU.is_ge,
                                       fill=-1e30, base=0, pattern=[[-1, P]], channel_multiplier=1)\
                        .then_inc(sem.dist, 1)

            def ln_rstd():
                pool.wait_ge(sem.ln_stat, me.seen("ln_stat", 2))
                v = tiny[:, 17:20:2]
                pool.tensor_scalar(v, v, EPS, None, ALU.add).then_inc(sem.pool_step, 1)
                pool.wait_ge(sem.pool_step, me.step())
                pool.tensor_tensor(rstd[:, 24:26], v, neg_half[:, 0:2], ALU.pow).then_inc(sem.ln_rstd, 1)

            def post_norm(i):
                for t in range(TT):
                    pool.wait_ge(sem.post_sum, me.seen("post_sum", 2 if i == 2 else 3 - 2 * t))
                    rsqrt(POST + i, t, True)

            def ahead_of(key, mode):
                for g, _ in me.groups_of(key, mode):
                    split_low(g + LEAD + 1)

            setup()
            norm(0)
            ahead_of("lru", "C")
            ahead_of("qk", "C")
            ahead_of("ifsv", "T")
            ahead_of("vo", "T")
            ahead_of("sqk", "C")
            mlstm_cols()
            ahead_of(("gate", 0), "T")
            ahead_of(("gate", 1), "T")
            ahead_of(("gate", 2), "T")
            strict(sem.sb_sp, sem.sb_masked)
            ahead_of(("gate", 3), "T")
            strict(sem.sb_a, sem.sb_a_masked)
            norm(3)
            ahead_of(("gate", 4), "T")
            ahead_of(("gate", 5), "T")
            for b in range(3):
                ahead_of(("branch", b), "W")
            for c in range(2):
                ahead_of(("wo", c), "T")
            norm(1)
            n1 = F1 // 256
            for c in range(n1 + 1):
                if c < n1:
                    ahead_of(("up1", c), "C")
                if c >= 1:
                    ahead_of(("down1", c - 1), "F")
            norm(FINAL)
            norm(2)
            ahead_of(("kv", 0), "C")
            block2_masks()
            ahead_of("zc", "C")
            ahead_of("q2", "C")
            ahead_of("k2", "C")
            ahead_of("za", "T")
            ln_rstd()
            ahead_of("v2", "T")
            ahead_of(("kv", 1), "C")
            ahead_of(("kv", 2), "T")
            ahead_of(("kv", 3), "T")
            for c in range(2):
                ahead_of(("mix_top", c), "T")
            for c in range(2):
                ahead_of(("mix_bottom", c), "T")
            post_norm(0)
            norm(4)
            for c in range(2):
                ahead_of(("xq", c), "C")
            for c in range(2):
                ahead_of(("xo", c), "T")
            post_norm(1)
            norm(5)
            n2 = F2 // NB
            for c in range(n2 + 1):
                if c < n2:
                    ahead_of(("up2", c), "C")
                if c >= 1:
                    ahead_of(("down2", c - 1), "F")
            post_norm(2)

        @block.scalar
        def _(act):
            me = Count()
            split = [0]

            def f(dst, src, func, **k):
                return act.activation(dst, src, func, **k)

            def split_high(upto):
                while split[0] < min(upto, n_groups):
                    g = split[0]
                    split[0] += 1
                    act.wait_ge(raw_in[g % RAW], arrived(g))
                    if g >= SPLIT:
                        act.wait_ge(sem.w_used, g - SPLIT + 1)
                    f(part(high, g), part(raw, g), ACT.Copy).then_inc(sem.w_high, 1)

            def setup():
                act.dma_start(x[:, 0, :], w["x"][0:P, :]).then_inc(sem.x_in, 16)
                act.dma_start(x[:, 1, :], w["x"][P:T, :]).then_inc(sem.x1_in, 16)
                for name, n in VEC_A:
                    act.dma_start(vec_rows[VEC_OFF[name]:VEC_OFF[name] + n, :], w[name].rearrange("(r c) -> r c", c=P))\
                       .then_inc(sem.vec_in, 16)
                act.dma_start(dw_rows[0:DW_ROWS, :], w["w_dw_2"].rearrange("(r c) -> r c", c=P))\
                   .then_inc(sem.dw_in, 16)
                for i, name in enumerate(("mlstm_ig_b", "mlstm_fg_b")):
                    act.dma_start(if_bias[:, i:i + 1], w[name].rearrange("(a b) -> a b", b=1)).then_inc(sem.bias_in, 16)
                load_row("final_norm_g")
                split_high(LEAD)

            def load_row(name):
                act.dma_start(row_g[:, :], w[name].partition_broadcast(P)).then_inc(sem.row_in, 16)

            def vectors():
                act.wait_ge(sem.vec_turned, me.seen("vec_turned", 2))
                f(vec[:, :], bank[4][:, 0:VEC_ROWS], ACT.Copy).then_inc(sem.vec_out, 1)
                f(dw[:, :], bank[4][:, P:P + DW_ROWS], ACT.Copy).then_inc(sem.vec_out, 1)
                act.wait_ge(sem.vec_out, me.seen("vec_out", 2))
                lam = vec[:, VEC_OFF["lru_lambda"]:VEC_OFF["lru_lambda"] + 2]
                f(tiny[:, 0:2], lam, ACT.Abs).then_inc(sem.act_step, 1)
                act.wait_ge(sem.act_step, me.step())
                f(tiny[:, 2:4], tiny[:, 0:2], ACT.Exp, scale=-1.0).then_inc(sem.lam_e, 1)

            def square(src, t, c, junk, done):
                f(junk, src, ACT.Square, scale=1 / math.sqrt(D), accum_out=sums[:, t, c:c + 1]).then_inc(done, 1)

            def norm_stat(n):
                if n in (1, FINAL):
                    me.seen("tile0_used")
                if n == 1:
                    for c in range(2):
                        for t in range(TT):
                            act.wait_ge(sem.x_ready, me.seen("x_ready"))
                            cut = slice(c * NB, (c + 1) * NB)
                            square(x[:, t, cut], t, c, xn[:, t, cut], sem.sumsq)
                elif n == FINAL:
                    for t in range(TT):
                        for c in range(2):
                            act.wait_ge(sem.x_ready, me.seen("x_ready"))
                            cut = slice(c * NB, (c + 1) * NB)
                            square(x[:, t, cut], t, c, xn[:, t, cut], sem.sumsq)
                else:
                    if n == 3:
                        act.wait_ge(sem.mem_in, me.seen("mem_in", 16))
                    for t in range(TT):
                        if n == 0:
                            act.wait_ge((sem.x_in, sem.x1_in)[t], 16)
                        elif n != 3:
                            act.wait_ge(sem.x_ready, me.seen("x_ready"))
                        square((mem if n == 3 else x)[:, t, :], t, 0, xn[:, t, :], sem.sumsq)
                if n == 2:
                    load_row("post_mix_g_2")
                    act.dma_start(ln_g, w["gate_ln_g_2"].partition_broadcast(P)).then_inc(sem.ln_in, 16)
                    act.dma_start(ln_b, w["gate_ln_b_2"].partition_broadcast(P)).then_inc(sem.ln_in, 16)
                    act.dma_start(spatial_w, w["w_s_2"].rearrange("h t s -> t h s")).then_inc(sem.ws_in, 16)
                if n == 4:
                    load_row("post_x_g_2")
                if n == 5:
                    load_row("post_ffn_g_2")

            def norm_split(n):
                if n != 3:
                    act.wait_ge(sem.w_used, me.used)
                for q in range(4):
                    act.wait_ge(sem.turned, me.seen("turned"))
                    for k in range(2):
                        kt = 2 * q + k
                        ins = f(split_of(kt, n == 3)[0], bank[4 + q][:, k * T:(k + 1) * T], ACT.Copy,
                                scale=col(NORM_GAIN[n], kt))
                    ins.then_inc(sem.act_h, 1)

            def norm(n):
                norm_stat(n)
                norm_split(n)

            def copy_pair(d0, d1, done, scale=1.0, func=ACT.Copy):
                act.wait_ge(sem.w_used, me.used)
                b0, b1 = me.pair()
                for d, b in ((d0, b0), (d1, b1)):
                    src = b[:, :]
                    if len(d.shape) == 3:
                        src = src.rearrange("p (a b) -> p a b", a=d.shape[1])
                    f(d, src, func, scale=scale).then_inc(done, 1)


            def gate_in(c):
                if c >= 3:
                    act.wait_ge(sem.y_a, 1)
                copy_pair(gates[:, 0, c * NB:(c + 1) * NB], gates[:, 1, c * NB:(c + 1) * NB], sem.gate_in, 0.5, ACT.Tanh)

            def ifsv_in():
                act.wait_ge(sem.w_used, me.used)
                for t, b in enumerate(me.pair()):
                    f(if_tok[:, t, :], b[:, 0:8], ACT.Copy)
                    f(s_v[:, t, :], b[:, 8:264], ACT.Copy).then_inc(sem.ifsv_in, 1)

            def vo_in():
                act.wait_ge(sem.w_used, me.used)
                for t, b in enumerate(me.pair()):
                    f(m_v[:, t, :, 0:64], b[:, 0:T].rearrange("p (h d) -> p h d", h=4), ACT.Copy)
                    f(m_o[:, t, :], b[:, T:2 * T], ACT.Tanh, scale=0.5).then_inc(sem.vo_in, 1)

            def sqk_in():
                act.wait_ge(sem.w_used, me.used)
                b0, b1 = me.pair()
                f(flat(s_q), b0[:, :], ACT.Copy, scale=0.125).then_inc(sem.sqk_in, 1)
                f(flat(s_k), b1[:, :], ACT.Copy).then_inc(sem.sqk_in, 1)

            def if_rows():
                act.wait_ge(sem.if_rows, me.seen("if_rows"))
                f(rows[0:4, 2, :], rows[0:4, 0, :], ACT.Abs).then_inc(sem.act_step, 1)
                act.wait_ge(sem.act_step, me.step())
                f(rows[0:4, 2, :], rows[0:4, 2, :], ACT.Exp, scale=-1.0).then_inc(sem.act_step, 1)
                act.wait_ge(sem.act_step, me.step())
                f(rows[0:4, 2, :], rows[0:4, 2, :], ACT.Ln, bias=1.0).then_inc(sem.log_f, 1)
                act.wait_ge(sem.m_stab, me.seen("m_stab"))
                f(rows[0:4, 5, :], rows[0:4, 5, :], ACT.Exp, scale=-1.0).then_inc(sem.exp_m, 1)

            def lru_gates():
                act.wait_ge(sem.lru_z, me.seen("lru_z"))
                act.wait_ge(sem.lru_cols, me.seen("lru_cols"))
                for i, (b, dst) in enumerate(((bank[4], l_r), (bank[5], l_i))):
                    for c in range(2):
                        k = 8 + 2 * i + c
                        ins = f(dst[:, c, :], b[:, c * T:(c + 1) * T], ACT.Tanh, scale=0.5, bias=tiny[:, k:k + 1])
                    ins.then_inc(sem.lru_t, 1)
                act.wait_ge(sem.lru_t, me.seen("lru_t"))
                for c in range(2):
                    k = 12 + c
                    ins = f(l_r[:, c, :], l_r[:, c, :], ACT.Tanh, scale=tiny[:, k:k + 1], bias=tiny[:, k:k + 1])
                ins.then_inc(sem.lru_t, 1)
                act.wait_ge(sem.lru_t, me.seen("lru_t", 2))
                f(l_s, l_r, ACT.Sqrt, scale=-4.0).then_inc(sem.lru_sqrt, 1)

            def lru_scan():
                act.wait_ge(sem.lru_gelu, me.seen("lru_gelu"))
                f(xa, xa, ACT.Tanh, scale=SQRT_2_PI).then_inc(sem.lru_tg, 1)

            def mlstm_cols():
                act.wait_ge(sem.cols, me.seen("cols"))
                act.wait_ge(sem.m_bc, me.seen("m_bc", 2))
                for h in range(4):
                    b = bank[4 + h // 2]
                    o = (h % 2) * T
                    f(m_e[:, h, 0:T], b[:, o:o + T], ACT.Exp, scale=-1.0, bias=cols[:, 0, 0, h:h + 1])\
                        .then_inc(sem.m_e, 1)
                    f(m_e[:, h, T:DIAG], b[:, o + P:o + T], ACT.Exp, scale=-1.0, bias=cols[:, 0, 1, h:h + 1])\
                        .then_inc(sem.m_e, 1)

            def mlstm_qk():
                act.wait_ge(sem.m_conv, me.seen("m_conv", 4))
                f(m_x_used, m_qk, ACT.Tanh, scale=0.5).then_inc(sem.m_tanh, 1)

            def mlstm_turn():
                act.wait_ge(sem.m_turned, me.seen("m_turned"))
                f(flat(y[:, 2:4, :]), bank[4][:, :], ACT.Copy, scale=0.5).then_inc(sem.y_b, 1)
                act.dma_start(mem, w["mem_2"].rearrange("(t p) d -> p t d", p=P)).then_inc(sem.mem_in, 16)

            def sb_scores():
                act.wait_ge(sem.y_a, 1)
                for h in range(4):
                    act.wait_ge(sem.sb_z, me.seen("sb_z"))
                    ins = f(sb_a[:, h, :], bank[4 + h][:, 0:DIAG], ACT.Abs)
                ins.then_inc(sem.act_step, 1)
                act.wait_ge(sem.act_step, me.step())
                f(flat(sb_a), flat(sb_a), ACT.Exp, scale=-1.0).then_inc(sem.act_step, 1)
                act.wait_ge(sem.act_step, me.step())
                f(flat(sb_a), flat(sb_a), ACT.Ln, bias=1.0).then_inc(sem.sb_ln, 1)

            def sb_sums():
                for h in range(4):
                    act.wait_ge(sem.sb_sum, me.seen("sb_sum"))
                    f(sb_a[:, h, :], bank[4 + h][:, 0:DIAG], ACT.Exp).then_inc(sem.sb_a, 1)

            def sb_out():
                act.wait_ge(sem.sb_o, me.seen("sb_o"))
                f(flat(y[:, 4:6, :]), bank[4][:, :], ACT.Copy).then_inc(sem.y_c, 1)

            def split_y():
                act.wait_ge(sem.y_a, 1)
                act.wait_ge(sem.y_b, 1)
                act.wait_ge(sem.y_c, 1)
                act.wait_ge(sem.w_used, me.used)
                f(flat(act_h[:, 0:6, :]), flat(y[:, 0:6, :]), ACT.Copy).then_inc(sem.act_h, 1)

            def turn_merged():
                act.wait_ge(sem.w_used, me.used)
                for q in range(4):
                    act.wait_ge(sem.turned, me.seen("turned"))
                    f(flat(act_h[:, 2 * q:2 * q + 2, :]), bank[4 + q][:, :], ACT.Copy, scale=0.5)\
                        .then_inc(sem.act_h, 1)

            def hidden1(c):
                act.wait_ge(sem.w_used, me.used)
                b0, _ = me.pair()
                f(h_act, b0[:, :], ACT.Tanh, scale=0.5).then_inc(sem.hid_t, 1)
                act.wait_ge(sem.hid_a, me.seen("hid_a", 1))
                f(flat(hidden_of(c, True)[0]), h_val, ACT.Copy).then_inc(sem.hid_h, 1)

            def hidden2(c):
                act.wait_ge(sem.w_used, me.used)
                for b in range(2):
                    src = me.pair()[b]
                    f(h_act, src[:, :], ACT.Relu).then_inc(sem.hid_t, 1)
                    act.wait_ge(sem.hid_a, me.seen("hid_a", 1))
                    f(flat(hid_h[c % 2][:, 2 * b:2 * b + 2, :]), h_val, ACT.Copy).then_inc(sem.hid_h, 1)

            def za_in():
                copy_pair(zg[:, 0, :], zg[:, 1, :], sem.za_in, 1.0, ACT.Gelu)

            def spatial_w_out():
                act.wait_ge(sem.ws_turned, me.seen("ws_turned"))
                f(spatial_t, bank[7][:, :].rearrange("p (h t) -> p h t", h=4), ACT.Copy).then_inc(sem.ws_out, 1)

            def qk2_in(i):
                d = (q2, k2)[i]
                copy_pair(d[:, 0:2, :], d[:, 2:4, :], sem.qk2_in, (0.125, 1.0)[i])

            def kv_in(c):
                if c < 2:
                    copy_pair(k_mem[:, 4 * c:4 * c + 2, :], k_mem[:, 4 * c + 2:4 * c + 4, :], sem.kv_in)
                else:
                    a = (c - 2) * NB
                    copy_pair(v_mem[:, 0, a:a + NB], v_mem[:, 1, a:a + NB], sem.kv_in)

            def zc_in():
                act.wait_ge(sem.w_used, me.used)
                f(cs, me.pair()[1][:, :], ACT.Tanh, scale=0.5).then_inc(sem.zc_t, 1)

            def high_of_bank(q, b, done):
                act.wait_ge(done, me.seen(done.name))
                f(flat(act_h[:, 2 * q:2 * q + 2, :]), b[:, :], ACT.Copy).then_inc(sem.act_h, 1)

            def moba_exp(i):
                act.wait_ge(sem.mo_max, me.seen("mo_max", 2))
                for h in range(4 * i, 4 * i + 4):
                    for t, (a, n) in enumerate(((0, P), (P, 2 * P))):
                        k = 8 * t + h
                        ins = f(sc[:, h, a:a + n], sc[:, h, a:a + n], ACT.Exp, bias=neg_max[:, k:k + 1],
                                accum_out=soft[:, k:k + 1])
                    ins.then_inc(sem.mo_p, 1)

            def moba_turned():
                for h in range(4):
                    act.wait_ge(sem.mo_turned, me.seen("mo_turned"))
                    f(pt[:, h, :], bank[4 + h][:, 0:DIAG], ACT.Copy).then_inc(sem.mo_t, 1)

            def group_norm():
                act.wait_ge(sem.gn_var, me.seen("gn_var"))
                f(cs, bank[7][:, :], ACT.Sqrt, bias=EPS).then_inc(sem.gn_sd, 1)
                act.wait_ge(sem.gn_z, me.seen("gn_z", 2))
                f(cs, cx, ACT.Tanh, scale=0.5).then_inc(sem.gn_t, 1)

            def group_norm_high():
                act.wait_ge(sem.gn_y, me.seen("gn_y"))
                f(flat(act_h[:, 6:8, :]), cx, ACT.Copy, scale=0.5).then_inc(sem.act_h, 1)

            def post_in(c):
                for t, b in enumerate(me.pair()):
                    if c == 1 and t == 0:
                        act.wait_ge(sem.tile0_used, me.seen("tile0_used"))
                    else:
                        act.wait_ge(sem.w_used, me.used)
                    square(b[:, :], t, c, post_junk[:, t, c * NB:(c + 1) * NB], sem.post_sum)

            def post_acc():
                for t in range(TT):
                    if t == 0:
                        act.wait_ge(sem.tile0_used, me.seen("tile0_used"))
                    else:
                        act.wait_ge(sem.w_used, me.used)
                    for c in range(2):
                        square(bank[4 + 2 * t + c][:, :], t, c, post_junk[:, t, c * NB:(c + 1) * NB], sem.post_sum)

            def x_scores():
                for h in range(4):
                    act.wait_ge(sem.x_max, me.seen("x_max"))
                    for t in range(TT):
                        k = 2 * h + t
                        ins = f(x_p[:, h, t, :], bank[4 + h][:, t * T:(t + 1) * T], ACT.Exp, bias=neg_max[:, k:k + 1],
                                accum_out=soft[:, k:k + 1])
                    ins.then_inc(sem.x_p, 1)
                for h in range(4):
                    act.wait_ge(sem.x_turned, me.seen("x_turned"))
                    f(flat(x_pt[:, h, :, :]), bank[4 + h][:, :], ACT.Copy).then_inc(sem.x_t, 1)

            def x_out():
                act.wait_ge(sem.w_used, me.used)
                for q in range(4):
                    act.wait_ge(sem.x_o, me.seen("x_o"))
                    f(flat(act_h[:, 2 * q:2 * q + 2, :]), bank[4 + q][:, :], ACT.Copy).then_inc(sem.act_h, 1)

            def ahead_of(key, mode):
                for g, _ in me.groups_of(key, mode):
                    split_high(g + LEAD + 1)

            def ahead_of_half(key, i):
                split_high(chunks[key][i][0] + LEAD + 1)
                me.used += 1
                me.pairs += i

            setup()
            vectors()
            norm(0)
            ahead_of("lru", "C")
            copy_pair(lru_x[:, :, 3:], lru_g, sem.lru_in)
            ahead_of("qk", "C")
            copy_pair(m_x[:, 0:2, 3:], m_x[:, 2:4, 3:], sem.qk_in)
            ahead_of("ifsv", "T")
            ifsv_in()
            if_rows()
            ahead_of("vo", "T")
            vo_in()
            lru_gates()
            ahead_of("sqk", "C")
            sqk_in()
            mlstm_cols()
            mlstm_qk()
            ahead_of(("gate", 0), "T")
            gate_in(0)
            ahead_of(("gate", 1), "T")
            gate_in(1)
            lru_scan()
            ahead_of(("gate", 2), "T")
            gate_in(2)
            mlstm_turn()
            sb_scores()
            ahead_of(("gate", 3), "T")
            gate_in(3)
            sb_sums()
            norm_stat(3)
            ahead_of(("gate", 4), "T")
            gate_in(4)
            norm_split(3)
            sb_out()
            ahead_of(("gate", 5), "T")
            gate_in(5)
            split_y()
            for b in range(3):
                ahead_of(("branch", b), "W")
            turn_merged()
            for c in range(2):
                ahead_of(("wo", c), "T")
            norm(1)
            n1 = F1 // 256
            for c in range(n1 + 1):
                if c < n1:
                    ahead_of(("up1", c), "C")
                    hidden1(c)
                if c >= 1:
                    ahead_of(("down1", c - 1), "F")
            norm_stat(FINAL)
            norm_stat(2)
            ahead_of(("kv", 0), "C")
            norm_split(2)
            kv_in(0)
            ahead_of("zc", "C")
            zc_in()
            ahead_of("q2", "C")
            qk2_in(0)
            ahead_of("k2", "C")
            qk2_in(1)
            spatial_w_out()
            ahead_of("za", "T")
            moba_exp(0)
            ahead_of_half("v2", 0)
            za_in()
            ahead_of_half("v2", 1)
            moba_exp(1)
            copy_pair(v2[:, 0, :], v2[:, 1, :], sem.v2_in)
            ahead_of_half(("kv", 1), 0)
            moba_turned()
            ahead_of_half(("kv", 1), 1)
            kv_in(1)
            high_of_bank(1, bank[4], sem.mo_o)
            ahead_of(("kv", 2), "T")
            kv_in(2)
            ahead_of_half(("kv", 3), 0)
            moba_turned()
            ahead_of_half(("kv", 3), 1)
            kv_in(3)
            high_of_bank(0, bank[5], sem.ya2_turned)
            high_of_bank(2, bank[4], sem.mo_o)
            for c in range(2):
                ahead_of(("mix_top", c), "T")
            group_norm()
            group_norm_high()
            for c in range(2):
                ahead_of(("mix_bottom", c), "T")
                post_in(c)
            norm(4)
            for c in range(2):
                ahead_of(("xq", c), "C")
                copy_pair(x_q[:, 4 * c:4 * c + 2, :], x_q[:, 4 * c + 2:4 * c + 4, :], sem.xq_in, 1 / 16)
            x_scores()
            x_out()
            for c in range(2):
                ahead_of(("xo", c), "T")
                post_in(c)
            norm(5)
            n2 = F2 // NB
            for c in range(n2 + 1):
                if c < n2:
                    ahead_of(("up2", c), "C")
                    hidden2(c)
                if c >= 1:
                    ahead_of(("down2", c - 1), "F")
            post_acc()

        @block.vector
        def _(dve):
            me = Count()
            split = [0]
            stt, ts, tt = dve.scalar_tensor_tensor, dve.tensor_scalar, dve.tensor_tensor
            MUL, ADD, SUB, MAX, MIN = ALU.mult, ALU.add, ALU.subtract, ALU.max, ALU.min

            def split_low(upto):
                while split[0] < min(upto, n_groups):
                    g = split[0]
                    split[0] += 1
                    if g % 2:
                        continue
                    dve.wait_ge(sem.w_high, g + 1)
                    if g >= SPLIT:
                        dve.wait_ge(sem.w_used, g - SPLIT + 1)
                    tt(part(low, g), part(raw, g), f32(part(high, g)), SUB).then_inc(sem.low_by_dve, 1)

            def setup():
                dve.memset(lru_x[:, :, 0:3], 0.0)
                dve.memset(m_x[:, :, 0:3], 0.0)
                dve.memset(m_v[:, :, :, 64:65], 1.0)
                dve.memset(ones4[0:4], 1.0).then_inc(sem.dve_step, 1)
                dve.wait_ge(sem.dve_step, me.step())
                split_low(LEAD)

            def vectors():
                dve.wait_ge(sem.lam_e, me.seen("lam_e"))
                e, s_, p_, q_ = tiny[:, 2:4], tiny[:, 4:6], tiny[:, 6:8], tiny[:, 14:16]
                ts(s_, e, 2.0, None, ADD).then_inc(sem.dve_step, 1)
                dve.wait_ge(sem.dve_step, me.step())
                dve.reciprocal(s_, s_).then_inc(sem.dve_step, 1)
                dve.wait_ge(sem.dve_step, me.step())
                tt(s_, s_, e, MUL).then_inc(sem.dve_step, 1)
                dve.wait_ge(sem.dve_step, me.step())
                tt(p_, s_, s_, MUL).then_inc(sem.dve_step, 1)
                dve.wait_ge(sem.dve_step, me.step())
                ts(q_, p_, 1 / 15, None, MUL).then_inc(sem.dve_step, 1)
                dve.wait_ge(sem.dve_step, me.step())
                for k in (13, 11, 9, 7, 5, 3):
                    stt(q_, q_, 1 / k, p_, ADD, MUL).then_inc(sem.dve_step, 1)
                    dve.wait_ge(sem.dve_step, me.step())
                stt(q_, q_, 1.0, s_, ADD, MUL).then_inc(sem.dve_step, 1)
                dve.wait_ge(sem.dve_step, me.step())
                lam = vec[:, VEC_OFF["lru_lambda"]:VEC_OFF["lru_lambda"] + 2]
                ts(s_, lam, -1.0, 0.0, MUL, MAX).then_inc(sem.dve_step, 1)
                dve.wait_ge(sem.dve_step, me.step())
                stt(s_, q_, 2.0, s_, MUL, ADD).then_inc(sem.dve_step, 1)
                dve.wait_ge(sem.dve_step, me.step())
                ts(tiny[:, 12:14], s_, -2.0, None, MUL)
                k = VEC_OFF["lru_ba"]
                ts(tiny[:, 8:12], vec[:, k:k + 4], 0.5, None, MUL).then_inc(sem.lru_cols, 1)

            def norm_diag(n):
                for t in range(TT):
                    dve.wait_ge(sem.rstd, me.seen("rstd"))
                    ts(diag[:, t, :], ident[:, :], rstd[:, 2 * n + t:2 * n + t + 1], None, MUL).then_inc(sem.diag, 1)

            def norm_split(n):
                for q in range(4):
                    dve.wait_ge(sem.act_h, me.seen("act_h"))
                    for k in range(2):
                        kt = 2 * q + k
                        h_, l_ = split_of(kt, n == 3)
                        ins = stt(l_, bank[4 + q][:, k * T:(k + 1) * T], col(NORM_GAIN[n], kt), f32(h_), MUL, SUB)
                    ins.then_inc(sem.act_hl, 1)

            def norm(n):
                norm_diag(n)
                norm_split(n)

            def final_norm():
                dve.wait_ge(sem.row_in, me.seen("row_in", 16))
                for t in range(TT):
                    dve.wait_ge(sem.rstd, me.seen("rstd"))
                    k = 2 * FINAL + t
                    stt(x[:, t, :], x[:, t, :], rstd[:, k:k + 1], row_g[:, :], MUL, MUL).then_inc(sem.x_ready, 1)

            def conv(dst, src, taps, weight, tiles, first, done=None, tile_of=lambda dst, c: dst[:, c, :]):
                for j in taps:
                    for c in range(tiles):
                        window = src[:, c, j:j + T]
                        if j == first:
                            ins = ts(tile_of(dst, c), window, weight(j, c), None, MUL)
                        else:
                            ins = stt(tile_of(dst, c), window, weight(j, c), tile_of(dst, c), MUL, ADD)
                        if c == tiles - 1 or (done and j == taps[-1]):
                            if done and j == taps[-1]:
                                ins.then_inc(done, 1)
                            else:
                                ins.then_inc(sem.dve_step, 1)
                                dve.wait_ge(sem.dve_step, me.step())

            def lru_conv():
                dve.wait_ge(sem.lru_in, me.seen("lru_in", 2))
                conv(xa, lru_x, range(4), lambda j, c: col("conv_lru_w", 2 * j + c), 2, 0, sem.lru_conv)

            def if_rows():
                dve.wait_ge(sem.if_turned, me.seen("if_turned"))
                dve.wait_ge(sem.bias_in, me.seen("bias_in", 32))
                ts(rows[0:4, 0, :], bank[6][0:4, T:2 * T], if_bias[:, 1:2], None, ADD)
                ts(rows[0:4, 1, :], bank[6][0:4, 0:T], if_bias[:, 0:1], None, ADD).then_inc(sem.if_rows, 1)
                dve.wait_ge(sem.log_f, me.seen("log_f"))
                r = [rows[0:4, i, :] for i in range(6)]
                stt(r[0], r[0], 0.0, r[2], MIN, SUB).then_inc(sem.dve_step, 1)
                dve.wait_ge(sem.dve_step, me.step())
                dve.tensor_tensor_scan(r[3], ones4[0:4], r[0], 0.0, MUL, ADD).then_inc(sem.dve_step, 1)
                dve.wait_ge(sem.dve_step, me.step())
                tt(r[1], r[1], r[3], SUB).then_inc(sem.dve_step, 1)
                dve.wait_ge(sem.dve_step, me.step())
                dve.tensor_tensor_scan(r[4], r[1], r[1], 0.0, MAX, MAX).then_inc(sem.dve_step, 1)
                dve.wait_ge(sem.dve_step, me.step())
                tt(r[5], r[3], r[4], ADD).then_inc(sem.m_stab, 1)

            def mlstm_cols():
                dve.wait_ge(sem.cols_turned, me.seen("cols_turned"))
                dve.tensor_copy(cols.rearrange("p a b c -> p (a b c)"), bank[7][:, 0:16]).then_inc(sem.cols, 1)

            def mlstm_qk():
                dve.wait_ge(sem.qk_in, me.seen("qk_in", 2))
                conv(m_qk, m_x, range(4), lambda j, c: col("conv_mlstm_w", 4 * j + c), 4, 0, sem.m_conv,
                     lambda dst, c: dst[:, c // 2, c % 2, :])
                dve.wait_ge(sem.m_tanh, me.seen("m_tanh"))
                stt(m_qk, m_x_used, 1.0, m_qk, ADD, MUL).then_inc(sem.m_qk, 1)

            def mlstm_scores():
                dve.wait_ge(sem.m_e_masked, me.seen("m_e_masked", 2))
                for h in range(4):
                    dve.wait_ge(sem.m_s, me.seen("m_s"))
                    b = bank[(6, 7, 4, 5)[h]]
                    stt(m_e[:, h, :], b[:, 0:DIAG], 1 / 32, m_e[:, h, :], MUL, MUL).then_inc(sem.m_p, 1)

            def mlstm_out():
                dve.wait_ge(sem.m_y, me.seen("m_y"))
                dve.wait_ge(sem.vo_in, me.seen("vo_in", 2))
                for t in range(TT):
                    b = bank[6 + t][:, 0:260].rearrange("p (h d) -> p h d", h=4)
                    den, neg = tiny[:, 20 + 4 * t:24 + 4 * t], tiny[:, 28:32]
                    dve.tensor_copy(den, b[:, :, 64]).then_inc(sem.dve_step, 1)
                    dve.wait_ge(sem.dve_step, me.step())
                    stt(den, den, -1.0, den, MUL, MAX).then_inc(sem.dve_step, 1)
                    dve.wait_ge(sem.dve_step, me.step())
                    tt(den, den, cols[:, 1, t, :], MAX).then_inc(sem.dve_step, 1)
                    dve.wait_ge(sem.dve_step, me.step())
                    dve.reciprocal(den, den).then_inc(sem.dve_step, 1)
                    dve.wait_ge(sem.dve_step, me.step())
                    out_t = m_tmp[:, t, :].rearrange("p (h d) -> p h d", h=4)
                    tt(out_t, b[:, :, 0:64], den.unsqueeze(2).broadcast_to([P, 4, 64]), MUL).then_inc(sem.dve_step, 1)
                    dve.wait_ge(sem.dve_step, me.step())
                    stt(m_tmp[:, t, :], m_o[:, t, :], 1.0, m_tmp[:, t, :], ADD, MUL).then_inc(sem.m_yb, 1)

            def lru_scan():
                dve.wait_ge(sem.lru_sqrt, me.seen("lru_sqrt"))
                ts(l_u, l_r, -1.0, 1.0, MUL, ADD).then_inc(sem.dve_step, 1)
                dve.wait_ge(sem.dve_step, me.step())
                dve.reciprocal(l_u, l_u).then_inc(sem.dve_step, 1)
                dve.wait_ge(sem.dve_step, me.step())
                stt(l_a, l_r, 1.0, l_u, ADD, MUL)
                stt(l_i, l_i, 1.0, xa, ADD, MUL)
                tt(l_s, l_s, l_u, MUL).then_inc(sem.dve_step, 1)
                dve.wait_ge(sem.dve_step, me.step())
                stt(l_i, l_i, 0.5, l_s, MUL, MUL).then_inc(sem.dve_step, 1)
                dve.wait_ge(sem.dve_step, me.step())
                for c in range(2):
                    dve.tensor_tensor_scan(l_s[:, c, :], l_a[:, c, :], l_i[:, c, :], 0.0, MUL, ADD).then_inc(sem.dve_step, 1)
                    dve.wait_ge(sem.dve_step, me.step())
                tt(xa, lru_g, lru_g, MUL).then_inc(sem.dve_step, 1)
                dve.wait_ge(sem.dve_step, me.step())
                ts(xa, xa, 0.044715, 1.0, MUL, ADD).then_inc(sem.dve_step, 1)
                dve.wait_ge(sem.dve_step, me.step())
                tt(xa, xa, lru_g, MUL).then_inc(sem.lru_gelu, 1)
                dve.wait_ge(sem.lru_tg, me.seen("lru_tg"))
                stt(lru_g, xa, 1.0, lru_g, ADD, MUL).then_inc(sem.dve_step, 1)
                dve.wait_ge(sem.dve_step, me.step())
                stt(y[:, 0:2, :], lru_g, 0.5, l_s, MUL, MUL).then_inc(sem.y_a, 1)

            def sb_scores():
                dve.wait_ge(sem.sb_ln, me.seen("sb_ln"))
                for h in range(4):
                    stt(sb_a[:, h, :], bank[4 + h][:, 0:DIAG], 0.0, sb_a[:, h, :], MAX, ADD).then_inc(sem.sb_sp, 1)

            def split_y():
                dve.wait_ge(sem.act_h, me.seen("act_h"))
                tt(flat(act_l[:, 0:6, :]), flat(y[:, 0:6, :]), f32(flat(act_h[:, 0:6, :])), SUB).then_inc(sem.act_hl, 1)

            def merge(b):
                dve.wait_ge(sem.w_used, me.used)
                for c in range(2):
                    for t in range(TT):
                        src = me.pair(1 - c)[t]
                        g = gates[:, t, b * D + c * NB:b * D + (c + 1) * NB]
                        m = xn[:, t, c * NB:(c + 1) * NB]
                        if b == 0:
                            stt(m, g, 1.0, src[:, :], ADD, MUL).then_inc(sem.merge, 1)
                        else:
                            tmp = (h_act, h_tmp)[t]
                            stt(tmp, g, 1.0, src[:, :], ADD, MUL).then_inc(sem.merge, 1)
                            dve.wait_ge(sem.merge, 4 * b + 2 * c + t + 1)
                            tt(m, m, tmp, ADD).then_inc(sem.merged, 1)

            def low_of_bank(q, scale=1.0, b=None):
                dve.wait_ge(sem.act_h, me.seen("act_h"))
                stt(flat(act_l[:, 2 * q:2 * q + 2, :]), (b or bank[4 + q])[:, :], scale,
                    f32(flat(act_h[:, 2 * q:2 * q + 2, :])), MUL, SUB).then_inc(sem.act_hl, 1)

            def turn_merged():
                for q in range(4):
                    low_of_bank(q, 0.5)

            def x_out():
                for q in range(4):
                    low_of_bank(q)

            def wait_tile(t, split):
                if split and t == 0:
                    dve.wait_ge(sem.tile0_used, me.seen("tile0_used"))
                else:
                    dve.wait_ge(sem.w_used, me.used)

            def add_x(c):
                for t, b in enumerate(me.pair()):
                    wait_tile(t, c == 1)
                    o = x[:, t, c * NB:(c + 1) * NB]
                    tt(o, b[:, :], o, ADD).then_inc(sem.x_ready, 1)

            def add_acc():
                for t in range(TT):
                    wait_tile(t, True)
                    for c in range(2):
                        o = x[:, t, c * NB:(c + 1) * NB]
                        tt(o, bank[4 + 2 * t + c][:, :], o, ADD).then_inc(sem.x_ready, 1)

            def hidden1(c):
                dve.wait_ge(sem.hid_t, me.seen("hid_t"))
                b0, b1 = me.pair()
                stt(h_tmp, h_act, 1.0, b0[:, :], ADD, MUL).then_inc(sem.dve_step, 1)
                dve.wait_ge(sem.dve_step, me.step())
                stt(h_val, h_tmp, 0.5, b1[:, :], MUL, MUL).then_inc(sem.hid_a, 1)
                dve.wait_ge(sem.hid_h, me.seen("hid_h"))
                hh, hl = hidden_of(c, True)
                tt(flat(hl), h_val, f32(flat(hh)), SUB).then_inc(sem.hid_hl, 1)
                dve.wait_ge(sem.hid_hl, me.seen("hid_hl"))

            def hidden2(c):
                for b in range(2):
                    dve.wait_ge(sem.hid_t, me.seen("hid_t"))
                    tt(h_val, h_act, h_act, MUL).then_inc(sem.hid_a, 1)
                    dve.wait_ge(sem.hid_h, me.seen("hid_h"))
                    hl = flat(hid_l[c % 2][:, 2 * b:2 * b + 2, :])
                    tt(hl, h_val, f32(flat(hid_h[c % 2][:, 2 * b:2 * b + 2, :])), SUB).then_inc(sem.hid_hl, 1)
                    dve.wait_ge(sem.hid_hl, me.seen("hid_hl"))

            def za_in():
                dve.wait_ge(sem.za_in, me.seen("za_in", 2))
                for t in range(TT):
                    k = 20 + 6 * t
                    dve.bn_stats(tiny[:, k:k + 6], zg[:, t, T:2 * T]).then_inc(sem.dve_step, 1)
                    dve.wait_ge(sem.dve_step, me.step())
                    dve.bn_aggr(tiny[:, 16 + 2 * t:18 + 2 * t], tiny[:, k:k + 6]).then_inc(sem.ln_stat, 1)

            def ln_apply():
                dve.wait_ge(sem.ln_rstd, me.seen("ln_rstd"))
                dve.wait_ge(sem.ln_in, me.seen("ln_in", 32))
                for t in range(TT):
                    ts(vn[:, t, :], zg[:, t, T:2 * T], tiny[:, 16 + 2 * t:17 + 2 * t], rstd[:, 24 + t:25 + t],
                            SUB, MUL).then_inc(sem.dve_step, 1)
                    dve.wait_ge(sem.dve_step, me.step())
                    tt(vn[:, t, :], vn[:, t, :], ln_g, MUL).then_inc(sem.dve_step, 1)
                    dve.wait_ge(sem.dve_step, me.step())
                    tt(vn[:, t, :], vn[:, t, :], ln_b, ADD).then_inc(sem.vn, 1)

            def spatial():
                dve.wait_ge(sem.mixed, me.seen("mixed"))
                for t in range(TT):
                    for h in range(4):
                        d = slice(h * 64, h * 64 + 64)
                        ins = stt(vn[:, t, d], bank[5][:, t * T + h * 64:t * T + h * 64 + 64], col("b_s_2", h),
                                  zg[:, t, d], ADD, MUL)
                    ins.then_inc(sem.ya2_tok, 1)

            def moba_scores(i):
                if i == 0:
                    dve.wait_ge(sem.dist, me.seen("dist", 2))
                for h in range(4 * i, 4 * i + 4):
                    dve.wait_ge(sem.mo_s, me.seen("mo_s"))
                    stt(sc[:, h, :], dist, 2.0 ** -(h + 1), bank[4 + h % 4][:, 0:DIAG], MUL, ADD)\
                        .then_inc(sem.mo_sc, 1)
                dve.wait_ge(sem.mo_sc, me.seen("mo_sc", 4))
                r = slice(4 * i, 4 * i + 4)
                for t, (a, n) in enumerate(((0, P), (P, 2 * P))):
                    dve.tensor_reduce(neg_max[:, 8 * t + 4 * i:8 * t + 4 * i + 4], sc[:, r, a:a + n], AX.X, MAX,
                                      negate=True).then_inc(sem.mo_max, 1)

            def moba_norm(i):
                dve.wait_ge(sem.mo_p, me.seen("mo_p", 4))
                for t in range(TT):
                    k = 8 * t + 4 * i
                    ins = dve.reciprocal(soft[:, k:k + 4], soft[:, k:k + 4])
                ins.then_inc(sem.dve_step, 1)
                dve.wait_ge(sem.dve_step, me.step())
                for h in range(4 * i, 4 * i + 4):
                    for t, (a, n) in enumerate(((0, P), (P, 2 * P))):
                        k = 8 * t + h
                        ins = ts(sc[:, h, a:a + n], sc[:, h, a:a + n], soft[:, k:k + 1], None, MUL)
                    ins.then_inc(sem.mo_n, 1)

            def zc_in():
                dve.memset(glu[:, :, 0:DW_TAPS - 1], 0.0).then_inc(sem.dve_step, 1)
                dve.wait_ge(sem.dve_step, me.step())
                dve.wait_ge(sem.zc_t, me.seen("zc_t"))
                stt(glu[:, :, DW_TAPS - 1:], in2(cs), 1.0, in2(me.pair()[0][:, :]), ADD, MUL).then_inc(sem.zc_in, 1)
                dve.wait_ge(sem.zc_in, me.seen("zc_in"))

            def conv_dw(first, end):
                conv(cv, glu, range(first, end), lambda j, c: dw[:, 2 * j + c:2 * j + c + 1], 2, 0)

            def conv_bias():
                for c in range(2):
                    ts(cv[:, c, :], cv[:, c, :], 0.5, col("b_dw_2", c), MUL, ADD).then_inc(sem.conv_done, 1)
                dve.wait_ge(sem.conv_done, me.seen("conv_done", 2))

            def group_mean():
                dve.wait_ge(sem.gn_mean, me.seen("gn_mean"))
                tt(cx, flat(cv), bank[6][:, :], SUB).then_inc(sem.dve_step, 1)
                dve.wait_ge(sem.dve_step, me.step())
                tt(cs, cx, cx, MUL).then_inc(sem.gn_sq, 1)

            def group_norm():
                dve.wait_ge(sem.gn_sd, me.seen("gn_sd"))
                dve.reciprocal(cs, cs).then_inc(sem.dve_step, 1)
                dve.wait_ge(sem.dve_step, me.step())
                tt(cx, cx, cs, MUL).then_inc(sem.dve_step, 1)
                dve.wait_ge(sem.dve_step, me.step())
                for c in range(2):
                    a = cx[:, c * T:(c + 1) * T]
                    ts(a, a, col("conv_gn_g_2", c), col("conv_gn_b_2", c), MUL, ADD).then_inc(sem.gn_z, 1)
                dve.wait_ge(sem.gn_t, me.seen("gn_t"))
                stt(cx, cs, 1.0, cx, ADD, MUL).then_inc(sem.gn_y, 1)

            def group_norm_low():
                dve.wait_ge(sem.act_h, me.seen("act_h"))
                stt(flat(act_l[:, 6:8, :]), cx, 0.5, f32(flat(act_h[:, 6:8, :])), MUL, SUB).then_inc(sem.act_hl, 1)

            def gain(b, t, c):
                dve.wait_ge(sem.post_sum, me.seen("post_sum"))
                if c == 0 and t == 0:
                    dve.wait_ge(sem.row_in, me.seen("row_in", 16))
                cut = slice(c * NB, (c + 1) * NB)
                tt(xn[:, t, cut], b[:, :], row_g[:, cut], MUL).then_inc(sem.zg, 1)

            def add_normed(i, t):
                dve.wait_ge(sem.zg, me.seen("zg", {2: 2}.get(i, 3 - 2 * t)))
                dve.wait_ge(sem.rstd, me.seen("rstd"))
                k = 2 * (POST + i) + t
                stt(x[:, t, :], xn[:, t, :], rstd[:, k:k + 1], x[:, t, :], MUL, ADD).then_inc(sem.x_ready, 1)

            def post_first():
                for t, b in enumerate(me.pair()):
                    gain(b, t, 0)

            def post_last(i):
                for t, b in enumerate(me.pair()):
                    gain(b, t, 1)
                    add_normed(i, t)

            def post_acc(i):
                for t in range(TT):
                    for c in range(2):
                        gain(bank[4 + 2 * t + c], t, c)
                    add_normed(i, t)

            def x_scores():
                for h in range(4):
                    dve.wait_ge(sem.x_s, me.seen("x_s"))
                    dve.tensor_reduce(neg_max[:, 2 * h:2 * h + 2], in2(bank[4 + h][:, :]), AX.X, MAX, negate=True)\
                        .then_inc(sem.x_max, 1)
                for h in range(4):
                    dve.wait_ge(sem.x_p, me.seen("x_p"))
                    dve.reciprocal(soft[:, 2 * h:2 * h + 2], soft[:, 2 * h:2 * h + 2]).then_inc(sem.dve_step, 1)
                    dve.wait_ge(sem.dve_step, me.step())
                    for t in range(TT):
                        ins = ts(x_p[:, h, t, :], x_p[:, h, t, :], soft[:, 2 * h + t:2 * h + t + 1], None, MUL)
                    ins.then_inc(sem.x_n, 1)

            def ahead_of(key, mode):
                for g, _ in me.groups_of(key, mode):
                    split_low(g + LEAD + 1)

            setup()
            vectors()
            norm(0)
            ahead_of("lru", "C")
            lru_conv()
            ahead_of("qk", "C")
            ahead_of("ifsv", "T")
            if_rows()
            ahead_of("vo", "T")
            ahead_of("sqk", "C")
            mlstm_cols()
            mlstm_qk()
            ahead_of(("gate", 0), "T")
            mlstm_scores()
            ahead_of(("gate", 1), "T")
            mlstm_out()
            lru_scan()
            ahead_of(("gate", 2), "T")
            sb_scores()
            ahead_of(("gate", 3), "T")
            ahead_of(("gate", 4), "T")
            norm(3)
            ahead_of(("gate", 5), "T")
            split_y()
            for b in range(3):
                ahead_of(("branch", b), "W")
                merge(b)
            turn_merged()
            for c in range(2):
                ahead_of(("wo", c), "T")
                add_x(c)
            norm(1)
            n1 = F1 // 256
            for c in range(n1 + 1):
                if c < n1:
                    ahead_of(("up1", c), "C")
                    hidden1(c)
                if c >= 1:
                    ahead_of(("down1", c - 1), "F")
            add_acc()
            final_norm()
            norm_diag(2)
            ahead_of(("kv", 0), "C")
            norm_split(2)
            ahead_of("zc", "C")
            zc_in()
            ahead_of("q2", "C")
            conv_dw(0, 8)
            ahead_of("k2", "C")
            conv_dw(8, 17)
            ahead_of("za", "T")
            moba_scores(0)
            conv_dw(17, 20)
            moba_norm(0)
            ahead_of("v2", "T")
            za_in()
            moba_scores(1)
            ln_apply()
            ahead_of(("kv", 1), "C")
            moba_norm(1)
            conv_dw(20, 25)
            ahead_of(("kv", 2), "T")
            low_of_bank(1, b=bank[4])
            spatial()
            conv_dw(25, 29)
            ahead_of(("kv", 3), "T")
            conv_dw(29, DW_TAPS)
            conv_bias()
            low_of_bank(0, b=bank[5])
            low_of_bank(2, b=bank[4])
            group_mean()
            for c in range(2):
                ahead_of(("mix_top", c), "T")
            group_norm()
            group_norm_low()
            ahead_of(("mix_bottom", 0), "T")
            post_first()
            ahead_of(("mix_bottom", 1), "T")
            post_last(0)
            norm(4)
            for c in range(2):
                ahead_of(("xq", c), "C")
            x_scores()
            x_out()
            ahead_of(("xo", 0), "T")
            post_first()
            ahead_of(("xo", 1), "T")
            post_last(1)
            norm(5)
            n2 = F2 // NB
            for c in range(n2 + 1):
                if c < n2:
                    ahead_of(("up2", c), "C")
                    hidden2(c)
                if c >= 1:
                    ahead_of(("down2", c - 1), "F")
            post_acc(2)

        @block.tensor
        def _(pe):
            me = Count()

            def mm(dst, lhs, rhs, start=True, stop=True, loose=True):
                return pe.matmul(dst, lhs, rhs, start=start, stop=stop, skip_group_check=loose)

            def mm3(dst, lhs_h, lhs_l, rhs_h, rhs_l, start, stop):
                mm(dst, lhs_l, rhs_h, start, False)
                mm(dst, lhs_h, rhs_l, False, False)
                return mm(dst, lhs_h, rhs_h, False, stop)

            def products(key, mode, c=0, width=NB, fresh=False, tile0=False, first=True, last=True, kt0=0, is_mem=False):
                parity = me.pairs % 2
                ids = chunks[key]
                n_kt = sum(len(kts) for _, kts in ids)
                for g, kts in me.groups_of(key, mode):
                    pe.wait_ge(low_sem(g), before(g))
                    wh, wl = part(high, g), part(low, g)
                    by_tile = tile0 and kts[-1] == n_kt - 1
                    order = [(j, kt, t) for j, kt in enumerate(kts) for t in range(TT)]
                    if by_tile:
                        order = [(j, kt, t) for t in range(TT) for j, kt in enumerate(kts)]
                    for j, kt, t in order:
                        s0, s1 = kt == 0 and first, kt == n_kt - 1 and last
                        tok = slice(t * P, (t + 1) * P)
                        if fresh and t == 0 and kt % 2 == 0:
                            pe.wait_ge(sem.act_hl, me.seen("act_hl"))
                        if mode == "F":
                            in_h, in_l = (half[:, kt, :] for half in hidden_of(c, key[0] == "down1"))
                        else:
                            in_h, in_l = split_of(2 * c + kt if mode == "W" else kt0 + kt, is_mem)
                        if mode == "T":
                            ins = mm3(bank[2 * parity + t][:, 0:width], in_h[:, tok], in_l[:, tok],
                                      wh[:, j, 0:width], wl[:, j, 0:width], s0, s1)
                        elif mode == "C":
                            for i in (2 * t, 2 * t + 1):
                                ch = slice(i * P, (i + 1) * P)
                                o = (i % 2) * T
                                ins = mm3(bank[2 * parity + i // 2][:, o:o + T], wh[:, j, ch], wl[:, j, ch],
                                          in_h, in_l, s0 and o == 0, s1)
                        elif mode == "W":
                            for n in range(2):
                                ins = mm3(bank[2 * ((parity + n) % 2) + t][:, :], in_h[:, tok], in_l[:, tok],
                                          wh[:, j, n * NB:(n + 1) * NB], wl[:, j, n * NB:(n + 1) * NB], s0, s1)
                        else:
                            for n in range(2):
                                ins = mm3(bank[4 + 2 * t + n][:, :], in_h[:, tok], in_l[:, tok],
                                          wh[:, j, n * NB:(n + 1) * NB], wl[:, j, n * NB:(n + 1) * NB], s0, s1)
                        if by_tile and t == 0 and s1:
                            ins.then_inc(sem.tile0_used, 1)
                    ins.then_inc(sem.w_used, 1)

            def turn(dst, src):
                n = src.shape[0]
                return pe.transpose(dst, src, ident[0:n, 0:n])

            def vectors():
                pe.wait_ge(sem.ident, me.seen("ident"))
                pe.wait_ge(sem.vec_in, me.seen("vec_in", 16 * len(VEC_A)))
                turn(bank[4][:, 0:VEC_ROWS], vec_rows[0:VEC_ROWS, :]).then_inc(sem.vec_turned, 1)
                pe.wait_ge(sem.dw_in, me.seen("dw_in", 16))
                turn(bank[4][:, P:P + DW_ROWS], dw_rows[0:DW_ROWS, :]).then_inc(sem.vec_turned, 1)
                pe.wait_ge(sem.vec_out, me.seen("vec_out", 2))

            def turn_x():
                for q in range(4):
                    for k in range(2):
                        for t in range(TT):
                            kt = 2 * q + k
                            ins = turn(bank[4 + q][:, k * T + t * P:k * T + (t + 1) * P], xn[:, t, kt * P:(kt + 1) * P])
                    ins.then_inc(sem.turned, 1)

            def norm(src=x):
                for t in range(TT):
                    pe.wait_ge(sem.diag, me.seen("diag"))
                    for kt in range(KD):
                        o = (kt % 2) * T + t * P
                        ins = mm(bank[4 + kt // 2][:, o:o + P], src[:, t, kt * P:(kt + 1) * P], diag[:, t, :])
                        if t == 1 and kt % 2:
                            ins.then_inc(sem.turned, 1)

            def if_rows():
                pe.wait_ge(sem.ifsv_in, 2)
                for k in range(2):
                    for t in range(TT):
                        ins = turn(bank[6][0:4, k * T + t * P:k * T + (t + 1) * P], if_tok[:, t, 4 * k:4 * k + 4])
                ins.then_inc(sem.if_turned, 1)

            def lru_gates():
                pe.wait_ge(sem.lru_conv, me.seen("lru_conv", 2))
                pe.wait_ge(sem.gate_w, me.seen("gate_w", 16 * 8))
                for i in range(2):
                    for c in range(2):
                        ins = mm(bank[4 + i][:, c * T:(c + 1) * T], gate_w[i][:, c, :], xa[:, c, :])
                ins.then_inc(sem.lru_z, 1)

            def mlstm_cols():
                pe.wait_ge(sem.exp_m, me.seen("exp_m"))
                for k, r in enumerate((1, 5)):
                    for t in range(TT):
                        o = 8 * k + 4 * t
                        ins = turn(bank[7][:, o:o + 4], rows[0:4, r, t * P:(t + 1) * P])
                ins.then_inc(sem.cols_turned, 1)
                pe.wait_ge(sem.consts, me.seen("consts", 5))
                pe.wait_ge(sem.lru_t, 2)
                for h in range(4):
                    ins = mm(bank[4 + h // 2][:, (h % 2) * T:(h % 2 + 1) * T], head_row[0:4, h, :], rows[0:4, 4, :])
                    if h % 2:
                        ins.then_inc(sem.m_bc, 1)

            def scores(dst, q, k, h):
                p_ = slice(64 * (h % 2), 64 * (h % 2) + 64)
                mm(dst[:, 0:T], k[p_, h // 2, 0:P], q[p_, h // 2, :])
                return mm(dst[:, T:DIAG], k[p_, h // 2, P:T], q[p_, h // 2, P:T], start=False)

            def mlstm_scores():
                pe.wait_ge(sem.m_qk, me.seen("m_qk"))
                pe.wait_ge(sem.m_e, me.seen("m_e", 8))
                pe.wait_ge(sem.cols, me.seen("cols"))
                for h in range(4):
                    scores(bank[(6, 7, 4, 5)[h]], m_qk[:, 0], m_qk[:, 1], h).then_inc(sem.m_s, 1)

            def mlstm_out():
                pe.wait_ge(sem.m_p, me.seen("m_p", 4))
                pe.wait_ge(sem.vo_in, 2)
                for h in range(4):
                    o = slice(65 * h, 65 * h + 65)
                    mm(bank[6][:, o], m_e[:, h, 0:P], m_v[:, 0, h, :], start=h == 0)
                    mm(bank[7][:, o], m_e[:, h, P:T], m_v[:, 0, h, :], start=h == 0, stop=False)
                    ins = mm(bank[7][:, o], m_e[:, h, T:DIAG], m_v[:, 1, h, :], start=False)
                ins.then_inc(sem.m_y, 1)

            def turn_256(dst, src):
                for c in range(2):
                    for t in range(TT):
                        ins = turn(dst[:, c * T + t * P:c * T + (t + 1) * P], src[:, t, c * P:(c + 1) * P])
                return ins

            def mlstm_turn():
                pe.wait_ge(sem.m_yb, me.seen("m_yb", 2))
                turn_256(bank[4], m_tmp).then_inc(sem.m_turned, 1)

            def sb_scores():
                pe.wait_ge(sem.sqk_in, 2)
                pe.wait_ge(sem.y_b, me.seen("y_b"))
                for h in range(4):
                    scores(bank[4 + h], s_q, s_k, h).then_inc(sem.sb_z, 1)

            def sb_sums():
                pe.wait_ge(sem.sb_masked, me.seen("sb_masked", 2))
                pe.wait_ge(sem.sb_sp, me.seen("sb_sp", 4))
                for h in range(4):
                    b, a = bank[4 + h], sb_a[:, h, :]
                    scores(b, s_q, s_k, h)
                    mm(b[:, 0:T], neg_tri, a[:, 0:T], start=False)
                    mm(b[:, P:T], neg_one, a[:, T:DIAG], start=False)
                    mm(b[:, T:DIAG], neg_tri, a[:, T:DIAG], start=False).then_inc(sem.sb_sum, 1)

            def weighted(dst, v, p, h, hh, start):
                q = slice(64 * (h % 2), 64 * (h % 2) + 64)
                d = slice(64 * h, 64 * h + 64)
                mm(dst[q, 0:T], v[:, 0, d], p[:, hh, 0:T], start=start, stop=False)
                return mm(dst[q, P:T], v[:, 1, d], p[:, hh, T:DIAG], start=False)

            def sb_out():
                pe.wait_ge(sem.sb_a_masked, me.seen("sb_a_masked", 2))
                pe.wait_ge(sem.sb_a, me.seen("sb_a", 4))
                for h in (0, 1, 2, 3):
                    ins = weighted(bank[4][:, (h // 2) * T:(h // 2 + 1) * T], s_v, sb_a, h, h, h < 2)
                ins.then_inc(sem.sb_o, 1)

            def turn_merged():
                pe.wait_ge(sem.merged, me.seen("merged", 8))
                pe.wait_ge(sem.y_c, 1)
                turn_x()


            def spatial_w_turn():
                pe.wait_ge(sem.ws_masked, me.seen("ws_masked"))
                for h in range(4):
                    ins = turn(bank[7][:, h * P:(h + 1) * P], spatial_w[:, h, :])
                ins.then_inc(sem.ws_turned, 1)

            def moba_scores(i):
                if i == 1:
                    pe.wait_ge(sem.mo_sc, me.seen("mo_sc", 4))
                for h in range(4 * i, 4 * i + 4):
                    if h == 3:
                        pe.wait_ge(sem.ws_out, me.seen("ws_out"))
                    q = slice(64 * (h % 2), 64 * (h % 2) + 64)
                    b = bank[4 + h % 4]
                    mm(b[:, 0:P], q2[q, h // 2, 0:P], k2[q, h // 2, 0:P])
                    mm(b[:, P:DIAG], q2[q, h // 2, P:T], k2[q, h // 2, :], start=False).then_inc(sem.mo_s, 1)

            def moba_turn(i):
                if i == 0:
                    pe.wait_ge(sem.mo_sc, me.seen("mo_sc", 4))
                else:
                    pe.wait_ge(sem.act_hl, me.seen("act_hl"))
                    pe.wait_ge(sem.ya2_tok, me.seen("ya2_tok", 2))
                for h in range(4):
                    pe.wait_ge(sem.mo_n, me.seen("mo_n"))
                    for k in range(3):
                        ins = turn(bank[4 + h][:, k * P:(k + 1) * P], sc[:, 4 * i + h, k * P:(k + 1) * P])
                    ins.then_inc(sem.mo_turned, 1)

            def moba_values(i):
                for h in range(4):
                    ins = weighted(bank[4][:, (h // 2) * T:(h // 2 + 1) * T], v2, pt, 4 * i + h, h, h < 2)
                ins.then_inc(sem.mo_o, 1)

            def spatial():
                pe.wait_ge(sem.vn, me.seen("vn", 2))
                for t in range(TT):
                    for h in range(4):
                        o = t * T + h * 64
                        ins = mm(bank[5][:, o:o + 64], spatial_t[:, h, :], vn[:, t, h * 64:h * 64 + 64])
                ins.then_inc(sem.mixed, 1)

            def group_mean():
                pe.wait_ge(sem.conv_done, me.seen("conv_done", 2))
                mm(bank[6][:, :], block_mean[:, :], flat(cv)).then_inc(sem.gn_mean, 1)

            def group_var():
                pe.wait_ge(sem.gn_sq, me.seen("gn_sq"))
                mm(bank[7][:, :], block_mean[:, :], cs).then_inc(sem.gn_var, 1)

            def x_scores():
                pe.wait_ge(sem.xq_in, 4)
                for h in range(4):
                    for t in range(TT):
                        for k in range(2):
                            ins = mm(bank[4 + h][:, t * T:(t + 1) * T], x_q[:, 2 * h + k, t * P:(t + 1) * P],
                                     k_mem[:, 2 * h + k, :], start=k == 0, stop=k == 1)
                    ins.then_inc(sem.x_s, 1)
                for h in range(4):
                    pe.wait_ge(sem.x_n, me.seen("x_n"))
                    for m in range(2):
                        for t in range(TT):
                            ins = turn(bank[4 + h][:, m * T + t * P:m * T + (t + 1) * P],
                                       x_p[:, h, t, m * P:(m + 1) * P])
                    ins.then_inc(sem.x_turned, 1)

            def x_out():
                pe.wait_ge(sem.x_t, me.seen("x_t", 4))
                for h in range(4):
                    for c in range(2):
                        for m in range(2):
                            ch = slice((2 * h + c) * P, (2 * h + c + 1) * P)
                            ins = mm(bank[4 + h][:, c * T:(c + 1) * T], v_mem[:, m, ch], x_pt[:, h, m, :],
                                     start=m == 0, stop=m == 1)
                    ins.then_inc(sem.x_o, 1)

            vectors()
            norm()
            products("lru", "C", fresh=True)
            products("qk", "C")
            pe.wait_ge(sem.lru_in, 2)
            products("ifsv", "T", width=264)
            if_rows()
            pe.wait_ge(sem.qk_in, 2)
            products("vo", "T")
            lru_gates()
            pe.wait_ge(sem.ifsv_in, 2)
            products("sqk", "C")
            mlstm_cols()
            pe.wait_ge(sem.vo_in, 2)
            products(("gate", 0), "T")
            mlstm_scores()
            pe.wait_ge(sem.sqk_in, 2)
            products(("gate", 1), "T")
            mlstm_out()
            pe.wait_ge(sem.gate_in, 2)
            products(("gate", 2), "T")
            mlstm_turn()
            sb_scores()
            pe.wait_ge(sem.gate_in, 4)
            products(("gate", 3), "T")
            sb_sums()
            pe.wait_ge(sem.gate_in, 6)
            products(("gate", 4), "T")
            pe.wait_ge(sem.sb_a, 4)
            norm(mem)
            pe.wait_ge(sem.act_hl, me.seen("act_hl", 4))
            sb_out()
            pe.wait_ge(sem.gate_in, 8)
            products(("gate", 5), "T")
            pe.wait_ge(sem.act_hl, me.seen("act_hl"))
            for b in range(3):
                pe.wait_ge(sem.gate_in, 12)
                if b:
                    pe.wait_ge(sem.merge, 4 * b)
                products(("branch", b), "W", b)
            turn_merged()
            pe.wait_ge(sem.merge, 12)
            for c in range(2):
                products(("wo", c), "T", fresh=c == 0, tile0=c == 1)
            norm()
            n1 = F1 // 256
            for c in range(n1 + 1):
                if c < n1:
                    if c >= 2:
                        pe.wait_ge(sem.hid_a, c - 1)
                    products(("up1", c), "C", fresh=c == 0)
                if c >= 1:
                    pe.wait_ge(sem.hid_hl, c)
                    products(("down1", c - 1), "F", c - 1, tile0=c == n1, first=c == 1, last=c == n1)
            products(("kv", 0), "C", is_mem=True)
            norm()
            products("zc", "C", fresh=True)
            pe.wait_ge(sem.kv_in, 2)
            products("q2", "C")
            pe.wait_ge(sem.zc_in, 1)
            products("k2", "C")
            spatial_w_turn()
            pe.wait_ge(sem.qk2_in, 3)
            moba_scores(0)
            products("za", "T")
            pe.wait_ge(sem.qk2_in, 4)
            moba_scores(1)
            products("v2", "T")
            moba_turn(0)
            pe.wait_ge(sem.za_in, 2)
            products(("kv", 1), "C", is_mem=True)
            pe.wait_ge(sem.v2_in, 2)
            pe.wait_ge(sem.mo_t, me.seen("mo_t", 4))
            moba_values(0)
            spatial()
            products(("kv", 2), "T", is_mem=True)
            moba_turn(1)
            pe.wait_ge(sem.kv_in, 4)
            products(("kv", 3), "T", is_mem=True)
            pe.wait_ge(sem.mo_t, me.seen("mo_t", 4))
            turn_256(bank[5], vn).then_inc(sem.ya2_turned, 1)
            moba_values(1)
            group_mean()
            pe.wait_ge(sem.act_hl, me.seen("act_hl"))
            pe.wait_ge(sem.kv_in, 6)
            products(("mix_top", 0), "T", last=False)
            group_var()
            pe.wait_ge(sem.kv_in, 8)
            products(("mix_top", 1), "T", last=False)
            for c in range(2):
                products(("mix_bottom", c), "T", kt0=4, fresh=c == 0, tile0=c == 1, first=False)
            norm()
            for c in range(2):
                products(("xq", c), "C", fresh=c == 0)
            x_scores()
            x_out()
            for c in range(2):
                products(("xo", c), "T", fresh=c == 0, tile0=c == 1)
            norm()
            n2 = F2 // NB
            for c in range(n2 + 1):
                if c < n2:
                    if c >= 2:
                        pe.wait_ge(sem.hid_a, F1 // 256 + 2 * (c - 1))
                    products(("up2", c), "C", fresh=c == 0)
                if c >= 1:
                    pe.wait_ge(sem.hid_hl, F1 // 256 + 2 * c)
                    products(("down2", c - 1), "F", c - 1, tile0=c == n2, first=c == 1, last=c == n2)


_INS = ["x", "norm_mix_g", "w_in", "conv_lru_w", "lru_wa", "lru_ba", "lru_wx", "lru_bx", "lru_lambda",
        "conv_mlstm_w", "mlstm_ig_b", "mlstm_fg_b", "w_out_lru", "w_out_mlstm", "w_out_sb", "w_o", "norm_ffn_g",
        "w_ffn_in", "w_ffn_out", "final_norm_g", "mem_2", "pre_mix_g_2", "w_in_2", "gate_ln_g_2", "gate_ln_b_2",
        "w_s_2", "b_s_2", "w_dw_2", "b_dw_2", "conv_gn_g_2", "conv_gn_b_2", "w_out_2", "post_mix_g_2", "pre_x_g_2",
        "mem_g_2", "w_xq_2", "w_xkv_2", "w_xo_2", "post_x_g_2", "pre_ffn_g_2", "w_ff1_2", "w_ff2_2", "post_ffn_g_2"]
_FLAT = {name for name, _ in VEC_A} | {"w_dw_2"}


def kernel(**inputs):
    import numpy as _np
    import concourse.bacc as _bacc
    from concourse.bass_utils import run_bass_kernel_spmd as _run

    nc = _bacc.Bacc("TRN2", target_bir_lowering=False, num_devices=1)
    arrays, args = {}, {}
    for name in _INS:
        a = _np.ascontiguousarray(inputs[name])
        if a.ndim > 1 and a.shape[0] == 1:
            a = a[0]
        if name in _FLAT:
            a = a.reshape(-1)
        arrays[f"in_{name}_dram"] = a
        args[name] = nc.dram_tensor(f"in_{name}_dram", a.shape, mybir.dt.from_np(a.dtype), kind="ExternalInput").ap()
    out = nc.dram_tensor("out_0_dram", (T, D), F32, kind="ExternalOutput").ap()
    two_blocks(nc, args, out)
    r = _run(nc, [arrays], core_ids=[0])
    return r.results[0]["out_0_dram"].reshape(1, T, D)
```

```python
from contextlib import ExitStack
import math

import concourse.bass as bass
from concourse import mybir

P = 128
T = 256
TT = T // P
D = 1024
KD = D // P
F1 = 2816
F2 = 4096
NB = 512
EPS = 1e-6
RAW = 3
SPLIT = 3
ARENA = 17466
LEAD = 2
GROUP = 2048
WARM = 16, 8
DIAG = 3 * P

F32 = mybir.dt.float32
F32R = mybir.dt.float32r
ALU = mybir.AluOpType
ACT = mybir.ActivationFunctionType
AX = mybir.AxisListType

VEC_A = [("norm_mix_g", 8), ("norm_ffn_g", 8), ("pre_mix_g_2", 8), ("mem_g_2", 8), ("pre_x_g_2", 8),
         ("pre_ffn_g_2", 8), ("lru_ba", 2), ("lru_bx", 2), ("lru_lambda", 2), ("conv_lru_w", 8),
         ("conv_mlstm_w", 16), ("b_dw_2", 2), ("conv_gn_g_2", 2), ("conv_gn_b_2", 2), ("b_s_2", 4)]
VEC_OFF = {}
_n = 0
for _name, _rows in VEC_A:
    VEC_OFF[_name] = _n
    _n += _rows
VEC_ROWS = _n
DW_TAPS = 31
DW_ROWS = 2 * DW_TAPS


def plan_weights(w):
    groups, chunks = [], {}

    def add(key, src, row0, kts, cols, view):
        ids = []
        per = GROUP // view
        for k in range(0, kts, per):
            nk = min(per, kts - k)
            dmas = [(src, row0 + k * P, nk, d, c, n) for d, c, n in cols]
            groups.append((dmas, view, nk, max(d + n for d, _, n in cols)))
            ids.append((len(groups) - 1, list(range(k, k + nk))))
        chunks[key] = ids

    win = w["w_in"]
    for key, cols in (("lru", [(0, 0, 512)]), ("qk", [(0, 512, 512)]), ("ifsv", [(0, 1536, 8), (8, 2056, 256)]),
                      ("vo", [(0, 1024, 512)]), ("sqk", [(0, 1544, 512)])):
        add(key, win, 0, KD, cols, NB)
    for c in range(6):
        add(("gate", c), win, 0, KD, [(0, 2312 + c * NB, NB)], NB)
    for b, name in enumerate(("w_out_lru", "w_out_mlstm", "w_out_sb")):
        add(("branch", b), w[name], 0, 2, [(0, 0, D)], D)
    for key, row in (("wo_top", 0), ("wo_bottom", 4 * P)):
        for c in range(2):
            add((key, c), w["w_o"], row, 4, [(0, c * NB, NB)], NB)
    n1 = F1 // 256
    for c in range(n1 + 1):
        if c < n1:
            add(("up1", c), w["w_ffn_in"], 0, KD, [(0, c * 256, 256), (256, F1 + c * 256, 256)], NB)
        if c >= 1:
            add(("down1", c - 1), w["w_ffn_out"], (c - 1) * 256, 2, [(0, 0, D)], D)

    def add_kv(c):
        add(("kv", c), w["w_xkv_2"], 0, KD, [(0, c * NB, NB)], NB)

    add_kv(0)
    for key, c in (("zc", 2048), ("q2", 512), ("k2", 1024), ("za", 0), ("v2", 1536)):
        add(key, w["w_in_2"], 0, KD, [(0, c, NB)], NB)
    for c in range(1, 3):
        add_kv(c)
    for key, row in (("mix_top", 0), ("mix_bottom", 4 * P)):
        for c in range(2):
            add((key, c), w["w_out_2"], row, 4, [(0, c * NB, NB)], NB)
    add_kv(3)
    for c in range(2):
        add(("xq", c), w["w_xq_2"], 0, KD, [(0, c * NB, NB)], NB)
    for c in range(2):
        add(("xo", c), w["w_xo_2"], 0, KD, [(0, c * NB, NB)], NB)
    n2 = F2 // NB
    for c in range(n2 + 1):
        if c < n2:
            add(("up2", c), w["w_ff1_2"], 0, KD, [(0, c * NB, NB)], NB)
        if c >= 1:
            add(("down2", c - 1), w["w_ff2_2"], (c - 1) * NB, 4, [(0, 0, D)], D)
    return groups, chunks


class Semaphores:

    def __init__(self, new):
        self.act_h = new("act_h")
        self.act_hl = new("act_hl")
        self.act_step = new("act_step")
        self.bias_in = new("bias_in")
        self.cols = new("cols")
        self.cols_turned = new("cols_turned")
        self.consts = new("consts")
        self.conv_done = new("conv_done")
        self.dist = new("dist")
        self.dve_step = new("dve_step")
        self.dw_in = new("dw_in")
        self.exp_m = new("exp_m")
        self.gain_in = new("gain_in")
        self.gain_turned = new("gain_turned")
        self.gate_in = new("gate_in")
        self.gate_w = new("gate_w")
        self.gate_w_zero = new("gate_w_zero")
        self.gn_mean = new("gn_mean")
        self.gn_sd = new("gn_sd")
        self.gn_sq = new("gn_sq")
        self.gn_t = new("gn_t")
        self.gn_var = new("gn_var")
        self.gn_y = new("gn_y")
        self.gn_z = new("gn_z")
        self.hid_a = new("hid_a")
        self.hid_h = new("hid_h")
        self.hid_hl = new("hid_hl")
        self.hid_t = new("hid_t")
        self.ident = new("ident")
        self.if_rows = new("if_rows")
        self.if_turned = new("if_turned")
        self.ifsv_in = new("ifsv_in")
        self.kv_in = new("kv_in")
        self.lam_e = new("lam_e")
        self.ln_in = new("ln_in")
        self.ln_rstd = new("ln_rstd")
        self.ln_stat = new("ln_stat")
        self.log_f = new("log_f")
        self.low_by_dve = new("low_by_dve")
        self.low_by_pool = new("low_by_pool")
        self.lru_cols = new("lru_cols")
        self.lru_conv = new("lru_conv")
        self.lru_gelu = new("lru_gelu")
        self.lru_in = new("lru_in")
        self.lru_sqrt = new("lru_sqrt")
        self.lru_t = new("lru_t")
        self.lru_tg = new("lru_tg")
        self.lru_z = new("lru_z")
        self.m_bc = new("m_bc")
        self.m_conv = new("m_conv")
        self.m_e = new("m_e")
        self.m_e_masked = new("m_e_masked")
        self.m_p = new("m_p")
        self.m_qk = new("m_qk")
        self.m_s = new("m_s")
        self.m_stab = new("m_stab")
        self.m_tanh = new("m_tanh")
        self.m_turned = new("m_turned")
        self.m_y = new("m_y")
        self.m_yb = new("m_yb")
        self.mem_in = new("mem_in")
        self.merge = new("merge")
        self.merged = new("merged")
        self.merged_1 = new("merged_1")
        self.half_used = new("half_used")
        self.mixed = new("mixed")
        self.mo_max = new("mo_max")
        self.mo_n = new("mo_n")
        self.mo_o = new("mo_o")
        self.mo_p = new("mo_p")
        self.mo_s = new("mo_s")
        self.mo_sc = new("mo_sc")
        self.mo_t = new("mo_t")
        self.mo_turned = new("mo_turned")
        self.pool_step = new("pool_step")
        self.post_sum = new("post_sum")
        self.qk2_in = new("qk2_in")
        self.qk_in = new("qk_in")
        self.row_in = new("row_in")
        self.rstd = new("rstd")
        self.sb_a = new("sb_a")
        self.sb_a_masked = new("sb_a_masked")
        self.sb_ln = new("sb_ln")
        self.sb_masked = new("sb_masked")
        self.sb_o = new("sb_o")
        self.sb_sp = new("sb_sp")
        self.sb_sum = new("sb_sum")
        self.sb_z = new("sb_z")
        self.sqk_in = new("sqk_in")
        self.stored = new("stored")
        self.sumsq = new("sumsq")
        self.turned = new("turned")
        self.v2_in = new("v2_in")
        self.vec_in = new("vec_in")
        self.vec_out = new("vec_out")
        self.vec_turned = new("vec_turned")
        self.vn = new("vn")
        self.vo_in = new("vo_in")
        self.w_high = new("w_high")
        self.w_used = new("w_used")
        self.ws_in = new("ws_in")
        self.ws_masked = new("ws_masked")
        self.ws_out = new("ws_out")
        self.ws_turned = new("ws_turned")
        self.x_in = new("x_in")
        self.x_max = new("x_max")
        self.x_n = new("x_n")
        self.x_o = new("x_o")
        self.x_p = new("x_p")
        self.x_ready = new("x_ready")
        self.x_s = new("x_s")
        self.x_t = new("x_t")
        self.x_turned = new("x_turned")
        self.zg = new("zg")
        self.tile0_used = new("tile0_used")
        self.x1_in = new("x1_in")
        self.diag = new("diag")
        self.xq_in = new("xq_in")
        self.y_a = new("y_a")
        self.y_b = new("y_b")
        self.y_c = new("y_c")
        self.ya2_tok = new("ya2_tok")
        self.ya2_turned = new("ya2_turned")
        self.za_in = new("za_in")
        self.zc_in = new("zc_in")
        self.zc_t = new("zc_t")


def two_blocks(nc, w, out):
    groups, chunks = plan_weights(w)
    n_groups = len(groups)
    ctx = ExitStack()
    with ctx:
        def sb(name, shape, dt=F32):
            return ctx.enter_context(nc.sbuf_tensor(name, shape, dt))

        def flat(ap):
            return ap.rearrange("p a b -> p (a b)")

        raw = [sb(f"raw{s}", [P, GROUP]) for s in range(RAW)]
        high = [sb(f"high{s}", [P, GROUP], F32R) for s in range(SPLIT)]
        low = [sb(f"low{s}", [P, GROUP], F32R) for s in range(SPLIT)]
        act_h = sb("act_h", [P, KD, T], F32R)
        act_l = sb("act_l", [P, KD, T], F32R)
        hid_h = [sb(f"hid_h{i}", [P, 4, T], F32R) for i in range(2)]
        hid_l = [sb(f"hid_l{i}", [P, 4, T], F32R) for i in range(2)]
        hid1_h = [sb(f"hid1_h{i}", [P, 2, T], F32R) for i in range(2)]
        hid1_l = [sb(f"hid1_l{i}", [P, 2, T], F32R) for i in range(2)]
        x = sb("x", [P, TT, D])
        xn = sb("xn", [P, TT, D])
        diag = sb("diag", [P, TT, P])
        row_g = sb("row_g", [P, D])
        vec_rows = sb("vec_rows", [P, P])
        dw_rows = sb("dw_rows", [P, P])
        vec = sb("vec", [P, VEC_ROWS])
        dw = sb("dw", [P, DW_ROWS])
        ident = sb("ident", [P, P])
        block_mean = sb("block_mean", [P, P])
        if_bias = sb("if_bias", [4, 2])
        neg_half = sb("neg_half", [P, 4])
        sums = sb("sums", [P, TT, 2])
        var = sb("var", [P, 32])
        rstd = sb("rstd", [P, 32])
        tiny = sb("tiny", [P, 40])
        neg_max = sb("neg_max", [P, 16])
        soft = sb("soft", [P, 16])

        arena = sb("arena", [P, ARENA])
        top = [0]

        def carve(*shape):
            size = math.prod(shape)
            a = arena[:, top[0]:top[0] + size]
            top[0] += size
            assert top[0] <= ARENA, top[0]
            if len(shape) == 2:
                a = a.rearrange("p (a b) -> p a b", a=shape[0])
            if len(shape) == 3:
                a = a.rearrange("p (a b c) -> p a b c", a=shape[0], b=shape[1])
            return a

        y = carve(6, T)
        gates = carve(TT, 3 * D)
        SHARE = top[0]
        m_v = carve(TT, 4, 65)
        m_o = carve(TT, T)
        s_q = carve(2, T)
        s_k = carve(2, T)
        s_v = carve(TT, T)
        if_tok = carve(TT, 8)
        cols = carve(2, TT, 4)
        MEM = top[0]
        m_e = carve(4, DIAG)
        m_tmp = carve(TT, T)
        rows = carve(6, T)
        neg_tri = carve(P)
        neg_one = carve(P)
        head_row = carve(4, P)
        gate_w = [carve(2, P), carve(2, P)]
        ones4 = carve(T)
        era = top[0]
        lru_x = carve(2, T + 3)
        lru_g = carve(2, T)
        m_x = carve(4, T + 3)
        m_x_used = m_x[:, :, 0:T].rearrange("p (a b) s -> p a b s", b=2)
        m_qk = gates[:, :, 2 * NB:3 * NB].rearrange("p a (b s) -> p a b s", b=2)
        top1 = top[0]
        top[0] = era
        sb_a = carve(4, DIAG)
        top[0] = max(top[0], top1)
        l_r, l_i, l_u, l_a = (gates[:, :, 2 * D + i * T:2 * D + (i + 1) * T] for i in range(4))
        l_s, xa = (gates[:, :, D + NB + i * T:D + NB + (i + 1) * T] for i in range(2))
        mem = arena[:, MEM:MEM + TT * D].rearrange("p (t d) -> p t d", t=TT)
        share_1 = [arena[:, SHARE + i * NB:SHARE + (i + 1) * NB] for i in range(4)]
        share_2 = [flat(s_v)] + [arena[:, era + i * NB:era + (i + 1) * NB] for i in range(3)]
        top[0] = 0
        h_act = carve(2 * T)
        h_tmp = carve(2 * T)
        h_val = carve(2 * T)
        top[0] = 0
        spatial_w = carve(4, P)
        spatial_t = carve(4, P)
        k_mem = carve(KD, T)
        v_mem = carve(TT, D)
        attn = top[0]
        sc = carve(8, DIAG)
        pt = carve(4, DIAG)
        q2 = carve(4, T)
        k2 = carve(4, T)
        v2 = carve(TT, NB)
        zg = carve(TT, NB)
        vn = carve(TT, T)
        dist = carve(DIAG)
        glu = carve(2, T + DW_TAPS - 1)
        cv = carve(2, T)
        cx = carve(2 * T)
        cs = carve(2 * T)
        ln_g = carve(T)
        ln_b = carve(T)
        top[0] = attn
        post_junk = carve(TT, D)
        top[0] = attn
        x_p = carve(4, TT, T)
        x_pt = carve(4, TT, T)
        x_q = carve(KD, T)

        bank = [ctx.enter_context(nc.psum_tensor(f"bank{i}", [P, NB], F32)) for i in range(8)]

        sem = Semaphores(lambda name: ctx.enter_context(nc.semaphore(name)))
        raw_in = [ctx.enter_context(nc.semaphore(f"raw_in{s}")) for s in range(RAW)]

        def arrived(g):
            return 16 * sum(len(groups[i][0]) for i in range(g % RAW, g + 1, RAW))

        def by_pool(g):
            return g % 2 == 1 and g != 1

        def low_sem(g):
            return sem.low_by_pool if by_pool(g) else sem.low_by_dve

        def before(g):
            return sum(by_pool(i) == by_pool(g) for i in range(g + 1))

        def part(tiles, g):
            _, view, nk, width = groups[g]
            return tiles[g % len(tiles)][:, :].rearrange("p (k n) -> p k n", n=view)[:, 0:nk, 0:width]

        def split_of(kt, is_mem):
            if is_mem:
                return hid_h[kt // 4][:, kt % 4, :], hid_l[kt // 4][:, kt % 4, :]
            return act_h[:, kt, :], act_l[:, kt, :]

        def branch_of(b):
            return (hid1_h[b], hid1_l[b]) if b < 2 else (act_h[:, 4:6, :], act_l[:, 4:6, :])

        def hidden_of(c, first_ffn):
            return (hid1_h[c % 2], hid1_l[c % 2]) if first_ffn else (hid_h[c % 2], hid_l[c % 2])

        def col(name, i=0):
            return vec[:, VEC_OFF[name] + i:VEC_OFF[name] + i + 1]

        def f32(ap):
            return ap.bitcast(F32)

        def in2(ap):
            return ap.rearrange("p (a b) -> p a b", a=2)

        TURN_BANK = (4, 5, 6, 7), (5, 6, 7, 4)
        NORM_GAIN = ["norm_mix_g", "norm_ffn_g", "pre_mix_g_2", "mem_g_2", "pre_x_g_2", "pre_ffn_g_2"]
        X_READY_END = 4 + 4 + 2 + 3 * TT
        FINAL, POST = 6, 7
        SQRT_2_PI = math.sqrt(2 / math.pi)
        block = ctx.enter_context(nc.Block())

        class Count:

            def __init__(self):
                self.steps, self.counts, self.used, self.pairs = 0, {}, 0, 0

            def seen(self, name, n=1):
                self.counts[name] = self.counts.get(name, 0) + n
                return self.counts[name]

            def step(self):
                self.steps += 1
                return self.steps

            def pair(self, back=0):
                i = 2 * ((self.pairs - 1 - back) % 2)
                return bank[i], bank[i + 1]

            def groups_of(self, key, mode):
                for g, kts in chunks[key]:
                    yield g, kts
                    self.used += 1
                self.pairs += {"W": 2, "F": 0}.get(mode, 1)

        @block.sync
        def _(sp):
            sp.dma_start(vec_rows[0:KD, :], w["norm_mix_g"].rearrange("(r c) -> r c", c=P)).then_inc(sem.gain_in, 16)
            sp.dma_start(x[:, 1, :], w["x"][P:T, :]).then_inc(sem.x1_in, 16)
            for g, (dmas, view, nk, width) in enumerate(groups):
                if g == RAW:
                    for name, n in VEC_A[1:]:
                        sp.dma_start(vec_rows[VEC_OFF[name]:VEC_OFF[name] + n, :], w[name].rearrange("(r c) -> r c", c=P))\
                          .then_inc(sem.vec_in, 16)
                    sp.dma_start(dw_rows[0:DW_ROWS, :], w["w_dw_2"].rearrange("(r c) -> r c", c=P)).then_inc(sem.dw_in, 16)
                    for i, name in enumerate(("mlstm_ig_b", "mlstm_fg_b")):
                        sp.dma_start(if_bias[:, i:i + 1], w[name].rearrange("(a b) -> a b", b=1)).then_inc(sem.bias_in, 16)
                if g == RAW + 2:
                    sp.wait_ge(sem.gate_w_zero, 1)
                    for i, name in enumerate(("lru_wa", "lru_wx")):
                        for k in range(4):
                            q = 64 * (k % 2)
                            sp.dma_start(gate_w[i][q:q + 64, k // 2, q:q + 64], w[name][k]).then_inc(sem.gate_w, 16)
                if g >= RAW:
                    sp.wait_ge(low_sem(g - RAW), before(g - RAW))
                tile = part(raw, g)
                for src, row, n, d, c, cw in dmas:
                    sp.dma_start(tile[:, 0:n, d:d + cw],
                                 src[row:row + n * P, c:c + cw].rearrange("(k p) n -> p k n", p=P))\
                      .then_inc(raw_in[g % RAW], 16)
            for t in range(TT):
                sp.wait_ge(sem.x_ready, X_READY_END - TT + 1 + t)
                sp.dma_start(out[t * P:(t + 1) * P, :], x[:, t, :]).then_inc(sem.stored, 16)
            sp.wait_ge(sem.stored, 16 * TT)

        @block.gpsimd
        def _(pool):
            me = Count()
            split = [0]

            def split_low(upto):
                while split[0] < min(upto, n_groups):
                    g = split[0]
                    split[0] += 1
                    if not by_pool(g):
                        continue
                    pool.wait_ge(sem.w_high, g + 1)
                    if g >= SPLIT:
                        pool.wait_ge(sem.w_used, g - SPLIT + 1)
                    pool.tensor_tensor(part(low, g), part(raw, g), f32(part(high, g)), ALU.subtract)\
                        .then_inc(sem.low_by_pool, 1)

            def rsqrt(k, t, halves):
                v = var[:, 2 * k + t:2 * k + t + 1]
                if halves:
                    pool.tensor_scalar(v, sums[:, t, 0:1], sums[:, t, 1:2], EPS, ALU.add, ALU.add)\
                        .then_inc(sem.pool_step, 1)
                else:
                    pool.tensor_scalar(v, sums[:, t, 0:1], EPS, None, ALU.add).then_inc(sem.pool_step, 1)
                pool.wait_ge(sem.pool_step, me.step())
                pool.tensor_tensor(rstd[:, 2 * k + t:2 * k + t + 1], v, neg_half[:, 0:1], ALU.pow)\
                    .then_inc(sem.rstd, 1)

            def setup():
                pool.memset(ident[:, :], 0.0).then_inc(sem.pool_step, 1)
                pool.wait_ge(sem.pool_step, me.step())
                pool.affine_select(out=ident[:, :], in_=ident[:, :], compare_op=ALU.not_equal, fill=1.0, base=0,
                                   pattern=[[-1, P]], channel_multiplier=1).then_inc(sem.ident, 1)
                pool.memset(neg_half[:, :], -0.5).then_inc(sem.pool_step, 1)
                pool.wait_ge(sem.pool_step, me.step())

            def constants():
                pool.memset(gate_w[0], 0.0)
                pool.memset(gate_w[1], 0.0).then_inc(sem.gate_w_zero, 1)
                pool.memset(neg_tri, -1.0).then_inc(sem.pool_step, 1)
                pool.wait_ge(sem.pool_step, me.step())
                pool.affine_select(out=neg_tri, in_=neg_tri, compare_op=ALU.is_ge, fill=0.0, base=0,
                                   pattern=[[-1, P]], channel_multiplier=1).then_inc(sem.consts, 1)
                pool.memset(neg_one, -1.0).then_inc(sem.consts, 1)
                pool.memset(head_row[0:4], 0.0).then_inc(sem.pool_step, 1)
                pool.wait_ge(sem.pool_step, me.step())
                pool.affine_select(out=head_row[0:4], in_=head_row[0:4], compare_op=ALU.not_equal, fill=1.0, base=0,
                                   pattern=[[-1, 4], [0, P]], channel_multiplier=1).then_inc(sem.consts, 1)
                pool.memset(block_mean[:, :], 0.0).then_inc(sem.pool_step, 1)
                pool.wait_ge(sem.pool_step, me.step())
                pool.memset(block_mean[0:64, 0:64], 1 / 64).then_inc(sem.consts, 1)
                pool.wait_ge(sem.consts, me.seen("consts", 4))
                pool.memset(block_mean[64:P, 64:P], 1 / 64).then_inc(sem.consts, 1)
                pool.wait_ge(sem.consts, me.seen("consts"))

            def norm(n):
                for t in range(TT):
                    pool.wait_ge(sem.sumsq, me.seen("sumsq", {FINAL: 2, 1: 3 - 2 * t}.get(n, 1)))
                    rsqrt(n, t, n in (FINAL, 1))

            def mlstm_cols():
                pool.wait_ge(sem.m_e, me.seen("m_e", 8))
                for a in (0, 2 * P):
                    part_e = m_e[:, :, a:a + P]
                    pool.affine_select(out=part_e, in_=part_e, compare_op=ALU.is_ge, fill=0.0, base=0,
                                       pattern=[[0, 4], [1, P]], channel_multiplier=-1).then_inc(sem.m_e_masked, 1)

            def strict(done, masked):
                pool.wait_ge(done, 4)
                for a in (0, 2 * P):
                    part_a = sb_a[:, :, a:a + P]
                    pool.affine_select(out=part_a, in_=part_a, compare_op=ALU.is_gt, fill=0.0, base=0,
                                       pattern=[[0, 4], [1, P]], channel_multiplier=-1).then_inc(masked, 1)

            def block2_masks():
                pool.wait_ge(sem.ws_in, me.seen("ws_in", 16))
                pool.affine_select(out=spatial_w, in_=spatial_w, compare_op=ALU.is_ge, fill=0.0, base=0,
                                   pattern=[[0, 4], [-1, P]], channel_multiplier=1).then_inc(sem.ws_masked, 1)
                pool.iota(dist[:, 0:P], [[1, P]], base=0, channel_multiplier=-1,
                          allow_small_or_imprecise_dtypes=True).then_inc(sem.pool_step, 1)
                pool.wait_ge(sem.pool_step, me.step())
                pool.iota(dist[:, P:DIAG], [[1, 2 * P]], base=-P, channel_multiplier=-1,
                          allow_small_or_imprecise_dtypes=True).then_inc(sem.pool_step, 1)
                pool.wait_ge(sem.pool_step, me.step())
                for a in (0, 2 * P):
                    pool.affine_select(out=dist[:, a:a + P], in_=dist[:, a:a + P], compare_op=ALU.is_ge,
                                       fill=-1e30, base=0, pattern=[[-1, P]], channel_multiplier=1)\
                        .then_inc(sem.dist, 1)

            def ln_rstd():
                pool.wait_ge(sem.ln_stat, me.seen("ln_stat", 2))
                v = tiny[:, 17:20:2]
                pool.tensor_scalar(v, v, EPS, None, ALU.add).then_inc(sem.pool_step, 1)
                pool.wait_ge(sem.pool_step, me.step())
                pool.tensor_tensor(rstd[:, 24:26], v, neg_half[:, 0:2], ALU.pow).then_inc(sem.ln_rstd, 1)

            def merge_1():
                for c in range(2):
                    for t in range(TT):
                        pool.wait_ge(sem.merge, 4 + 2 * c + t + 1)
                        m = xn[:, t, c * NB:(c + 1) * NB]
                        pool.tensor_tensor(m, m, share_1[2 * c + t], ALU.add).then_inc(sem.merged_1, 1)

            def post_norm(i):
                for t in range(TT):
                    pool.wait_ge(sem.post_sum, me.seen("post_sum", 2 if i == 2 else 3 - 2 * t))
                    rsqrt(POST + i, t, True)

            def ahead_of(key, mode, hold=False):
                for g, _ in me.groups_of(key, mode):
                    if not (hold and g == chunks[key][-1][0]):
                        split_low(g + LEAD + 1)

            setup()
            norm(0)
            constants()
            ahead_of("lru", "C")
            ahead_of("qk", "C")
            ahead_of("ifsv", "T")
            ahead_of("vo", "T")
            ahead_of("sqk", "C")
            mlstm_cols()
            ahead_of(("gate", 0), "T")
            ahead_of(("gate", 1), "T")
            ahead_of(("gate", 2), "T")
            strict(sem.sb_sp, sem.sb_masked)
            ahead_of(("gate", 3), "T")
            strict(sem.sb_a, sem.sb_a_masked)
            norm(3)
            ahead_of(("gate", 4), "T")
            ahead_of(("gate", 5), "T")
            for b in range(3):
                ahead_of(("branch", b), "W")
                if b == 1:
                    merge_1()
            for c in range(2):
                ahead_of(("wo_top", c), "T")
            for c in range(2):
                ahead_of(("wo_bottom", c), "T")
            norm(1)
            n1 = F1 // 256
            for c in range(n1 + 1):
                if c < n1:
                    ahead_of(("up1", c), "C")
                if c >= 1:
                    ahead_of(("down1", c - 1), "F")
            norm(FINAL)
            norm(2)
            ahead_of(("kv", 0), "C")
            block2_masks()
            ahead_of("zc", "C")
            ahead_of("q2", "C")
            ahead_of("k2", "C")
            ahead_of("za", "T")
            ln_rstd()
            ahead_of("v2", "T")
            ahead_of(("kv", 1), "C")
            ahead_of(("kv", 2), "T")
            for c in range(2):
                ahead_of(("mix_top", c), "T")
            for c in range(2):
                ahead_of(("mix_bottom", c), "T")
            post_norm(0)
            norm(4)
            ahead_of(("kv", 3), "T")
            for c in range(2):
                ahead_of(("xq", c), "C")
            for c in range(2):
                ahead_of(("xo", c), "T", hold=c == 1)
            post_norm(1)
            norm(5)
            split_low(me.used + LEAD)
            n2 = F2 // NB
            for c in range(n2 + 1):
                if c < n2:
                    ahead_of(("up2", c), "C")
                if c >= 1:
                    ahead_of(("down2", c - 1), "F")
            post_norm(2)

        @block.scalar
        def _(act):
            me = Count()
            split = [0]

            def f(dst, src, func, **k):
                return act.activation(dst, src, func, **k)

            def split_high(upto):
                while split[0] < min(upto, n_groups):
                    g = split[0]
                    split[0] += 1
                    act.wait_ge(raw_in[g % RAW], arrived(g))
                    if g >= SPLIT:
                        act.wait_ge(sem.w_used, g - SPLIT + 1)
                    f(part(high, g), part(raw, g), ACT.Copy).then_inc(sem.w_high, 1)

            def setup():
                act.dma_start(x[:, 0, :], w["x"][0:P, :]).then_inc(sem.x_in, 16)

            def load_row(name):
                act.dma_start(row_g[:, :], w[name].partition_broadcast(P)).then_inc(sem.row_in, 16)

            def gain_0():
                act.wait_ge(sem.gain_turned, 1)
                f(vec[:, 0:KD], bank[4][:, 0:KD], ACT.Copy).then_inc(sem.vec_out, 1)
                act.wait_ge(sem.vec_out, me.seen("vec_out"))

            def vectors():
                act.wait_ge(sem.vec_turned, me.seen("vec_turned", 2))
                f(vec[:, KD:VEC_ROWS], bank[4][:, KD:VEC_ROWS], ACT.Copy).then_inc(sem.vec_out, 1)
                f(dw[:, :], bank[4][:, P:P + DW_ROWS], ACT.Copy).then_inc(sem.vec_out, 1)
                act.wait_ge(sem.vec_out, me.seen("vec_out", 2))
                lam = vec[:, VEC_OFF["lru_lambda"]:VEC_OFF["lru_lambda"] + 2]
                f(tiny[:, 0:2], lam, ACT.Abs).then_inc(sem.act_step, 1)
                act.wait_ge(sem.act_step, me.step())
                f(tiny[:, 2:4], tiny[:, 0:2], ACT.Exp, scale=-1.0).then_inc(sem.lam_e, 1)

            def square(src, t, c, junk, done):
                f(junk, src, ACT.Square, scale=1 / math.sqrt(D), accum_out=sums[:, t, c:c + 1]).then_inc(done, 1)

            def norm_stat(n):
                if n in (1, FINAL):
                    me.seen("tile0_used")
                if n == 1:
                    for c in range(2):
                        for t in range(TT):
                            act.wait_ge(sem.x_ready, me.seen("x_ready"))
                            cut = slice(c * NB, (c + 1) * NB)
                            square(x[:, t, cut], t, c, xn[:, t, cut], sem.sumsq)
                elif n == FINAL:
                    for t in range(TT):
                        for c in range(2):
                            act.wait_ge(sem.x_ready, me.seen("x_ready"))
                            cut = slice(c * NB, (c + 1) * NB)
                            square(x[:, t, cut], t, c, xn[:, t, cut], sem.sumsq)
                else:
                    if n == 3:
                        act.wait_ge(sem.mem_in, me.seen("mem_in", 16))
                    for t in range(TT):
                        if n == 0:
                            act.wait_ge((sem.x_in, sem.x1_in)[t], 16)
                        elif n != 3:
                            act.wait_ge(sem.x_ready, me.seen("x_ready"))
                        square((mem if n == 3 else x)[:, t, :], t, 0, xn[:, t, :], sem.sumsq)
                if n == 2:
                    load_row("post_mix_g_2")
                    act.dma_start(ln_g, w["gate_ln_g_2"].partition_broadcast(P)).then_inc(sem.ln_in, 16)
                    act.dma_start(ln_b, w["gate_ln_b_2"].partition_broadcast(P)).then_inc(sem.ln_in, 16)
                    act.dma_start(spatial_w, w["w_s_2"].rearrange("h t s -> t h s")).then_inc(sem.ws_in, 16)
                if n == 4:
                    load_row("post_x_g_2")
                if n == 5:
                    load_row("post_ffn_g_2")

            def norm_split(n):
                if n != 3:
                    act.wait_ge(sem.w_used, me.used)
                for q in range(4):
                    act.wait_ge(sem.turned, me.seen("turned"))
                    for k in range(2):
                        kt = 2 * q + k
                        ins = f(split_of(kt, n == 3)[0], bank[4 + q][:, k * T:(k + 1) * T], ACT.Copy,
                                scale=col(NORM_GAIN[n], kt))
                    ins.then_inc(sem.act_h, 1)

            def norm(n):
                norm_stat(n)
                norm_split(n)

            def copy_pair(d0, d1, done, scale=1.0, func=ACT.Copy):
                act.wait_ge(sem.w_used, me.used)
                b0, b1 = me.pair()
                for d, b in ((d0, b0), (d1, b1)):
                    src = b[:, :]
                    if len(d.shape) == 3:
                        src = src.rearrange("p (a b) -> p a b", a=d.shape[1])
                    f(d, src, func, scale=scale).then_inc(done, 1)


            def gate_in(c):
                if c >= 3:
                    act.wait_ge(sem.y_a, 1)
                copy_pair(gates[:, 0, c * NB:(c + 1) * NB], gates[:, 1, c * NB:(c + 1) * NB], sem.gate_in, 0.5, ACT.Tanh)

            def ifsv_in():
                act.wait_ge(sem.w_used, me.used)
                for t, b in enumerate(me.pair()):
                    f(if_tok[:, t, :], b[:, 0:8], ACT.Copy)
                    f(s_v[:, t, :], b[:, 8:264], ACT.Copy).then_inc(sem.ifsv_in, 1)

            def vo_in():
                act.wait_ge(sem.w_used, me.used)
                for t, b in enumerate(me.pair()):
                    f(m_v[:, t, :, 0:64], b[:, 0:T].rearrange("p (h d) -> p h d", h=4), ACT.Copy)
                    f(m_o[:, t, :], b[:, T:2 * T], ACT.Tanh, scale=0.5).then_inc(sem.vo_in, 1)

            def sqk_in():
                act.wait_ge(sem.w_used, me.used)
                b0, b1 = me.pair()
                f(flat(s_q), b0[:, :], ACT.Copy, scale=0.125).then_inc(sem.sqk_in, 1)
                f(flat(s_k), b1[:, :], ACT.Copy).then_inc(sem.sqk_in, 1)

            def if_rows():
                act.wait_ge(sem.if_rows, me.seen("if_rows"))
                f(rows[0:4, 2, :], rows[0:4, 0, :], ACT.Abs).then_inc(sem.act_step, 1)
                act.wait_ge(sem.act_step, me.step())
                f(rows[0:4, 2, :], rows[0:4, 2, :], ACT.Exp, scale=-1.0).then_inc(sem.act_step, 1)
                act.wait_ge(sem.act_step, me.step())
                f(rows[0:4, 2, :], rows[0:4, 2, :], ACT.Ln, bias=1.0).then_inc(sem.log_f, 1)
                act.wait_ge(sem.m_stab, me.seen("m_stab"))
                f(rows[0:4, 5, :], rows[0:4, 5, :], ACT.Exp, scale=-1.0).then_inc(sem.exp_m, 1)

            def lru_gates():
                act.wait_ge(sem.lru_z, me.seen("lru_z"))
                act.wait_ge(sem.lru_cols, me.seen("lru_cols"))
                for i, (b, dst) in enumerate(((bank[4], l_r), (bank[5], l_i))):
                    for c in range(2):
                        k = 8 + 2 * i + c
                        ins = f(dst[:, c, :], b[:, c * T:(c + 1) * T], ACT.Tanh, scale=0.5, bias=tiny[:, k:k + 1])
                    ins.then_inc(sem.lru_t, 1)
                act.wait_ge(sem.lru_t, me.seen("lru_t"))
                for c in range(2):
                    k = 12 + c
                    ins = f(l_r[:, c, :], l_r[:, c, :], ACT.Tanh, scale=tiny[:, k:k + 1], bias=tiny[:, k:k + 1])
                ins.then_inc(sem.lru_t, 1)
                act.wait_ge(sem.lru_t, me.seen("lru_t", 2))
                f(l_s, l_r, ACT.Sqrt, scale=-4.0).then_inc(sem.lru_sqrt, 1)

            def lru_scan():
                act.wait_ge(sem.lru_gelu, me.seen("lru_gelu"))
                f(xa, xa, ACT.Tanh, scale=SQRT_2_PI).then_inc(sem.lru_tg, 1)

            def mlstm_cols():
                act.wait_ge(sem.cols, me.seen("cols"))
                act.wait_ge(sem.m_bc, me.seen("m_bc", 2))
                for h in range(4):
                    b = bank[4 + h // 2]
                    o = (h % 2) * T
                    f(m_e[:, h, 0:T], b[:, o:o + T], ACT.Exp, scale=-1.0, bias=cols[:, 0, 0, h:h + 1])\
                        .then_inc(sem.m_e, 1)
                    f(m_e[:, h, T:DIAG], b[:, o + P:o + T], ACT.Exp, scale=-1.0, bias=cols[:, 0, 1, h:h + 1])\
                        .then_inc(sem.m_e, 1)

            def mlstm_qk():
                act.wait_ge(sem.m_conv, me.seen("m_conv", 4))
                f(m_x_used, m_qk, ACT.Tanh, scale=0.5).then_inc(sem.m_tanh, 1)

            def mlstm_turn():
                act.wait_ge(sem.m_turned, me.seen("m_turned"))
                f(flat(y[:, 2:4, :]), bank[4][:, :], ACT.Copy, scale=0.5).then_inc(sem.y_b, 1)
                act.dma_start(mem, w["mem_2"].rearrange("(t p) d -> p t d", p=P)).then_inc(sem.mem_in, 16)

            def sb_scores():
                act.wait_ge(sem.y_a, 1)
                for h in (1, 2, 3, 0):
                    act.wait_ge(sem.sb_z, me.seen("sb_z"))
                    ins = f(sb_a[:, h, :], bank[4 + h][:, 0:DIAG], ACT.Abs)
                ins.then_inc(sem.act_step, 1)
                act.wait_ge(sem.act_step, me.step())
                f(flat(sb_a), flat(sb_a), ACT.Exp, scale=-1.0).then_inc(sem.act_step, 1)
                act.wait_ge(sem.act_step, me.step())
                f(flat(sb_a), flat(sb_a), ACT.Ln, bias=1.0).then_inc(sem.sb_ln, 1)

            def sb_sums():
                for h in range(4):
                    act.wait_ge(sem.sb_sum, me.seen("sb_sum"))
                    f(sb_a[:, h, :], bank[4 + h][:, 0:DIAG], ACT.Exp).then_inc(sem.sb_a, 1)

            def sb_out():
                act.wait_ge(sem.sb_o, me.seen("sb_o"))
                f(flat(y[:, 4:6, :]), bank[4][:, :], ACT.Copy).then_inc(sem.y_c, 1)

            def high_of_branch(b):
                act.wait_ge((sem.y_a, sem.y_b, sem.y_c)[b], 1)
                if b == 2:
                    act.wait_ge(sem.w_used, me.used)
                f(flat(branch_of(b)[0]), flat(y[:, 2 * b:2 * b + 2, :]), ACT.Copy).then_inc(sem.act_h, 1)

            def turn_merged(c):
                if c == 0:
                    act.wait_ge(sem.w_used, me.used)
                for q in (2 * c, 2 * c + 1):
                    act.wait_ge(sem.turned, me.seen("turned"))
                    f(flat(act_h[:, 2 * q:2 * q + 2, :]), bank[4 + q][:, :], ACT.Copy, scale=0.5)\
                        .then_inc(sem.act_h, 1)

            def hidden1(c):
                act.wait_ge(sem.w_used, me.used)
                b0, _ = me.pair()
                f(h_act, b0[:, :], ACT.Tanh, scale=0.5).then_inc(sem.hid_t, 1)
                act.wait_ge(sem.hid_a, me.seen("hid_a", 1))
                f(flat(hidden_of(c, True)[0]), h_val, ACT.Copy).then_inc(sem.hid_h, 1)

            def hidden2(c):
                act.wait_ge(sem.w_used, me.used)
                for b in range(2):
                    src = me.pair()[b]
                    f(h_act, src[:, :], ACT.Relu).then_inc(sem.hid_t, 1)
                    act.wait_ge(sem.hid_a, me.seen("hid_a", 1))
                    f(flat(hid_h[c % 2][:, 2 * b:2 * b + 2, :]), h_val, ACT.Copy).then_inc(sem.hid_h, 1)

            def za_in():
                copy_pair(zg[:, 0, :], zg[:, 1, :], sem.za_in, 1.0, ACT.Gelu)

            def spatial_w_out():
                act.wait_ge(sem.ws_turned, me.seen("ws_turned"))
                f(spatial_t, bank[7][:, :].rearrange("p (h t) -> p h t", h=4), ACT.Copy).then_inc(sem.ws_out, 1)

            def qk2_in(i):
                d = (q2, k2)[i]
                copy_pair(d[:, 0:2, :], d[:, 2:4, :], sem.qk2_in, (0.125, 1.0)[i])

            def kv_in(c):
                if c < 2:
                    copy_pair(k_mem[:, 4 * c:4 * c + 2, :], k_mem[:, 4 * c + 2:4 * c + 4, :], sem.kv_in)
                else:
                    a = (c - 2) * NB
                    copy_pair(v_mem[:, 0, a:a + NB], v_mem[:, 1, a:a + NB], sem.kv_in)

            def zc_in():
                act.wait_ge(sem.w_used, me.used)
                f(cs, me.pair()[1][:, :], ACT.Tanh, scale=0.5).then_inc(sem.zc_t, 1)

            def high_of_bank(q, b, done):
                act.wait_ge(done, me.seen(done.name))
                f(flat(act_h[:, 2 * q:2 * q + 2, :]), b[:, :], ACT.Copy).then_inc(sem.act_h, 1)

            def moba_exp(i):
                act.wait_ge(sem.mo_max, me.seen("mo_max", 2))
                for h in range(4 * i, 4 * i + 4):
                    for t, (a, n) in enumerate(((0, P), (P, 2 * P))):
                        k = 8 * t + h
                        ins = f(sc[:, h, a:a + n], sc[:, h, a:a + n], ACT.Exp, bias=neg_max[:, k:k + 1],
                                accum_out=soft[:, k:k + 1])
                    ins.then_inc(sem.mo_p, 1)

            def moba_turned(i, heads=range(4)):
                for h in heads:
                    act.wait_ge(sem.mo_turned, me.seen("mo_turned"))
                    f(pt[:, h, :], bank[TURN_BANK[i][h]][:, 0:DIAG], ACT.Copy).then_inc(sem.mo_t, 1)

            def group_sd():
                act.wait_ge(sem.gn_var, me.seen("gn_var"))
                f(cs, bank[4][:, :], ACT.Sqrt, bias=EPS).then_inc(sem.gn_sd, 1)

            def group_tanh():
                act.wait_ge(sem.gn_z, me.seen("gn_z", 2))
                f(cs, cx, ACT.Tanh, scale=0.5).then_inc(sem.gn_t, 1)

            def group_norm_high():
                act.wait_ge(sem.gn_y, me.seen("gn_y"))
                f(flat(act_h[:, 6:8, :]), cx, ACT.Copy, scale=0.5).then_inc(sem.act_h, 1)

            def post_in(c):
                for t, b in enumerate(me.pair()):
                    if c == 1 and t == 0:
                        act.wait_ge(sem.tile0_used, me.seen("tile0_used"))
                    else:
                        act.wait_ge(sem.w_used, me.used)
                    square(b[:, :], t, c, post_junk[:, t, c * NB:(c + 1) * NB], sem.post_sum)

            def post_acc():
                for t in range(TT):
                    if t == 0:
                        act.wait_ge(sem.tile0_used, me.seen("tile0_used"))
                    else:
                        act.wait_ge(sem.w_used, me.used)
                    for c in range(2):
                        square(bank[4 + 2 * t + c][:, :], t, c, post_junk[:, t, c * NB:(c + 1) * NB], sem.post_sum)

            def xq_in(c):
                copy_pair(x_q[:, 4 * c:4 * c + 2, :], x_q[:, 4 * c + 2:4 * c + 4, :], sem.xq_in, 1 / 16)

            def x_exp(i):
                for h in (2 * i, 2 * i + 1):
                    act.wait_ge(sem.x_max, me.seen("x_max"))
                    for t in range(TT):
                        k = 2 * h + t
                        ins = f(x_p[:, h, t, :], bank[4 + h][:, t * T:(t + 1) * T], ACT.Exp, bias=neg_max[:, k:k + 1],
                                accum_out=soft[:, k:k + 1])
                    ins.then_inc(sem.x_p, 1)

            def x_turned(i):
                for h in (2 * i, 2 * i + 1):
                    act.wait_ge(sem.x_turned, me.seen("x_turned"))
                    f(flat(x_pt[:, h, :, :]), bank[4 + h][:, :], ACT.Copy).then_inc(sem.x_t, 1)

            def x_out(i):
                act.wait_ge(sem.w_used, me.used)
                for q in (2 * i, 2 * i + 1):
                    act.wait_ge(sem.x_o, me.seen("x_o"))
                    f(flat(act_h[:, 2 * q:2 * q + 2, :]), bank[4 + q][:, :], ACT.Copy).then_inc(sem.act_h, 1)

            def ahead_of(key, mode, hold=False):
                for g, _ in me.groups_of(key, mode):
                    if not (hold and g == chunks[key][-1][0]):
                        split_high(g + LEAD + 1)

            def ahead_of_half(key, i):
                split_high(chunks[key][i][0] + LEAD + 1)
                me.used += 1
                me.pairs += i

            setup()
            norm_stat(0)
            load_row("final_norm_g")
            gain_0()
            split_high(1)
            norm_split(0)
            ahead_of("lru", "C")
            copy_pair(lru_x[:, :, 3:], lru_g, sem.lru_in)
            vectors()
            ahead_of("qk", "C")
            copy_pair(m_x[:, 0:2, 3:], m_x[:, 2:4, 3:], sem.qk_in)
            ahead_of("ifsv", "T")
            ifsv_in()
            if_rows()
            ahead_of("vo", "T")
            vo_in()
            lru_gates()
            ahead_of("sqk", "C")
            sqk_in()
            mlstm_cols()
            mlstm_qk()
            ahead_of(("gate", 0), "T")
            gate_in(0)
            lru_scan()
            ahead_of(("gate", 1), "T")
            gate_in(1)
            ahead_of(("gate", 2), "T")
            gate_in(2)
            mlstm_turn()
            sb_scores()
            ahead_of(("gate", 3), "T")
            gate_in(3)
            sb_sums()
            norm_stat(3)
            for b in range(2):
                high_of_branch(b)
            ahead_of(("gate", 4), "T")
            gate_in(4)
            norm_split(3)
            sb_out()
            ahead_of(("gate", 5), "T")
            gate_in(5)
            high_of_branch(2)
            for b in range(3):
                ahead_of(("branch", b), "W")
            for c in range(2):
                turn_merged(c)
                ahead_of(("wo_top", c), "T")
            for c in range(2):
                ahead_of(("wo_bottom", c), "T")
            norm(1)
            n1 = F1 // 256
            for c in range(n1 + 1):
                if c < n1:
                    ahead_of(("up1", c), "C")
                    hidden1(c)
                if c >= 1:
                    ahead_of(("down1", c - 1), "F")
            norm_stat(FINAL)
            norm_stat(2)
            ahead_of(("kv", 0), "C")
            norm_split(2)
            kv_in(0)
            ahead_of("zc", "C")
            zc_in()
            ahead_of("q2", "C")
            qk2_in(0)
            ahead_of("k2", "C")
            qk2_in(1)
            spatial_w_out()
            ahead_of("za", "T")
            moba_exp(0)
            ahead_of_half("v2", 0)
            za_in()
            ahead_of_half("v2", 1)
            moba_exp(1)
            copy_pair(v2[:, 0, :], v2[:, 1, :], sem.v2_in)
            ahead_of_half(("kv", 1), 0)
            moba_turned(0)
            ahead_of_half(("kv", 1), 1)
            kv_in(1)
            high_of_bank(1, bank[4], sem.mo_o)
            ahead_of(("kv", 2), "T")
            high_of_bank(0, bank[7], sem.ya2_turned)
            group_sd()
            kv_in(2)
            moba_turned(1, (0, 1))
            ahead_of(("mix_top", 0), "T")
            moba_turned(1, (2, 3))
            group_tanh()
            group_norm_high()
            ahead_of(("mix_top", 1), "T")
            high_of_bank(2, bank[5], sem.mo_o)
            for c in range(2):
                ahead_of(("mix_bottom", c), "T")
                post_in(c)
            norm_stat(4)
            ahead_of(("kv", 3), "T")
            norm_split(4)
            kv_in(3)
            ahead_of(("xq", 0), "C")
            xq_in(0)
            ahead_of_half(("xq", 1), 0)
            x_exp(0)
            ahead_of_half(("xq", 1), 1)
            xq_in(1)
            x_turned(0)
            x_exp(1)
            x_out(0)
            x_turned(1)
            x_out(1)
            for c in range(2):
                ahead_of(("xo", c), "T", hold=c == 1)
                post_in(c)
            norm_stat(5)
            split_high(me.used + LEAD)
            norm_split(5)
            n2 = F2 // NB
            for c in range(n2 + 1):
                if c < n2:
                    ahead_of(("up2", c), "C")
                    hidden2(c)
                if c >= 1:
                    ahead_of(("down2", c - 1), "F")
            post_acc()

        @block.vector
        def _(dve):
            me = Count()
            split = [0]
            stt, ts, tt = dve.scalar_tensor_tensor, dve.tensor_scalar, dve.tensor_tensor
            MUL, ADD, SUB, MAX, MIN = ALU.mult, ALU.add, ALU.subtract, ALU.max, ALU.min

            def split_low(upto):
                while split[0] < min(upto, n_groups):
                    g = split[0]
                    split[0] += 1
                    if by_pool(g):
                        continue
                    dve.wait_ge(sem.w_high, g + 1)
                    if g >= SPLIT:
                        dve.wait_ge(sem.w_used, g - SPLIT + 1)
                    tt(part(low, g), part(raw, g), f32(part(high, g)), SUB).then_inc(sem.low_by_dve, 1)

            def setup():
                dve.memset(lru_x[:, :, 0:3], 0.0)
                dve.memset(m_x[:, :, 0:3], 0.0)
                dve.memset(m_v[:, :, :, 64:65], 1.0)
                dve.memset(ones4[0:4], 1.0).then_inc(sem.dve_step, 1)
                dve.wait_ge(sem.dve_step, me.step())

            def vectors():
                dve.wait_ge(sem.lam_e, me.seen("lam_e"))
                e, s_, p_, q_ = tiny[:, 2:4], tiny[:, 4:6], tiny[:, 6:8], tiny[:, 14:16]
                ts(s_, e, 2.0, None, ADD).then_inc(sem.dve_step, 1)
                dve.wait_ge(sem.dve_step, me.step())
                dve.reciprocal(s_, s_).then_inc(sem.dve_step, 1)
                dve.wait_ge(sem.dve_step, me.step())
                tt(s_, s_, e, MUL).then_inc(sem.dve_step, 1)
                dve.wait_ge(sem.dve_step, me.step())
                tt(p_, s_, s_, MUL).then_inc(sem.dve_step, 1)
                dve.wait_ge(sem.dve_step, me.step())
                ts(q_, p_, 1 / 15, None, MUL).then_inc(sem.dve_step, 1)
                dve.wait_ge(sem.dve_step, me.step())
                for k in (13, 11, 9, 7, 5, 3):
                    stt(q_, q_, 1 / k, p_, ADD, MUL).then_inc(sem.dve_step, 1)
                    dve.wait_ge(sem.dve_step, me.step())
                stt(q_, q_, 1.0, s_, ADD, MUL).then_inc(sem.dve_step, 1)
                dve.wait_ge(sem.dve_step, me.step())
                lam = vec[:, VEC_OFF["lru_lambda"]:VEC_OFF["lru_lambda"] + 2]
                ts(s_, lam, -1.0, 0.0, MUL, MAX).then_inc(sem.dve_step, 1)
                dve.wait_ge(sem.dve_step, me.step())
                stt(s_, q_, 2.0, s_, MUL, ADD).then_inc(sem.dve_step, 1)
                dve.wait_ge(sem.dve_step, me.step())
                ts(tiny[:, 12:14], s_, -2.0, None, MUL)
                k = VEC_OFF["lru_ba"]
                ts(tiny[:, 8:12], vec[:, k:k + 4], 0.5, None, MUL).then_inc(sem.lru_cols, 1)

            def norm_diag(n):
                for t in range(TT):
                    dve.wait_ge(sem.rstd, me.seen("rstd"))
                    ts(diag[:, t, :], ident[:, :], rstd[:, 2 * n + t:2 * n + t + 1], None, MUL).then_inc(sem.diag, 1)

            def norm_split(n):
                for q in range(4):
                    dve.wait_ge(sem.act_h, me.seen("act_h"))
                    for k in range(2):
                        kt = 2 * q + k
                        h_, l_ = split_of(kt, n == 3)
                        ins = stt(l_, bank[4 + q][:, k * T:(k + 1) * T], col(NORM_GAIN[n], kt), f32(h_), MUL, SUB)
                    ins.then_inc(sem.act_hl, 1)

            def norm(n):
                norm_diag(n)
                norm_split(n)

            def final_norm():
                dve.wait_ge(sem.row_in, me.seen("row_in", 16))
                for t in range(TT):
                    dve.wait_ge(sem.rstd, me.seen("rstd"))
                    k = 2 * FINAL + t
                    stt(x[:, t, :], x[:, t, :], rstd[:, k:k + 1], row_g[:, :], MUL, MUL).then_inc(sem.x_ready, 1)

            def conv(dst, src, taps, weight, tiles, first, done=None, tile_of=lambda dst, c: dst[:, c, :]):
                for j in taps:
                    for c in range(tiles):
                        window = src[:, c, j:j + T]
                        if j == first:
                            ins = ts(tile_of(dst, c), window, weight(j, c), None, MUL)
                        else:
                            ins = stt(tile_of(dst, c), window, weight(j, c), tile_of(dst, c), MUL, ADD)
                        if c == tiles - 1 or (done and j == taps[-1]):
                            if done and j == taps[-1]:
                                ins.then_inc(done, 1)
                            else:
                                ins.then_inc(sem.dve_step, 1)
                                dve.wait_ge(sem.dve_step, me.step())

            def lru_conv():
                dve.wait_ge(sem.lru_in, me.seen("lru_in", 2))
                dve.wait_ge(sem.vec_out, 3)
                conv(xa, lru_x, range(4), lambda j, c: col("conv_lru_w", 2 * j + c), 2, 0, sem.lru_conv)

            def if_rows():
                dve.wait_ge(sem.if_turned, me.seen("if_turned"))
                dve.wait_ge(sem.bias_in, me.seen("bias_in", 32))
                ts(rows[0:4, 0, :], bank[6][0:4, T:2 * T], if_bias[:, 1:2], None, ADD)
                ts(rows[0:4, 1, :], bank[6][0:4, 0:T], if_bias[:, 0:1], None, ADD).then_inc(sem.if_rows, 1)
                dve.wait_ge(sem.log_f, me.seen("log_f"))
                r = [rows[0:4, i, :] for i in range(6)]
                stt(r[0], r[0], 0.0, r[2], MIN, SUB).then_inc(sem.dve_step, 1)
                dve.wait_ge(sem.dve_step, me.step())
                dve.tensor_tensor_scan(r[3], ones4[0:4], r[0], 0.0, MUL, ADD).then_inc(sem.dve_step, 1)
                dve.wait_ge(sem.dve_step, me.step())
                tt(r[1], r[1], r[3], SUB).then_inc(sem.dve_step, 1)
                dve.wait_ge(sem.dve_step, me.step())
                dve.tensor_tensor_scan(r[4], r[1], r[1], 0.0, MAX, MAX).then_inc(sem.dve_step, 1)
                dve.wait_ge(sem.dve_step, me.step())
                tt(r[5], r[3], r[4], ADD).then_inc(sem.m_stab, 1)

            def mlstm_cols():
                dve.wait_ge(sem.cols_turned, me.seen("cols_turned"))
                dve.tensor_copy(cols.rearrange("p a b c -> p (a b c)"), bank[7][:, 0:16]).then_inc(sem.cols, 1)

            def mlstm_qk():
                dve.wait_ge(sem.qk_in, me.seen("qk_in", 2))
                conv(m_qk, m_x, range(4), lambda j, c: col("conv_mlstm_w", 4 * j + c), 4, 0, sem.m_conv,
                     lambda dst, c: dst[:, c // 2, c % 2, :])
                dve.wait_ge(sem.m_tanh, me.seen("m_tanh"))
                stt(m_qk, m_x_used, 1.0, m_qk, ADD, MUL).then_inc(sem.m_qk, 1)

            def mlstm_scores():
                dve.wait_ge(sem.m_e_masked, me.seen("m_e_masked", 2))
                for h in range(4):
                    dve.wait_ge(sem.m_s, me.seen("m_s"))
                    b = bank[(6, 7, 4, 5)[h]]
                    stt(m_e[:, h, :], b[:, 0:DIAG], 1 / 32, m_e[:, h, :], MUL, MUL).then_inc(sem.m_p, 1)

            def mlstm_out():
                dve.wait_ge(sem.m_y, me.seen("m_y"))
                dve.wait_ge(sem.vo_in, me.seen("vo_in", 2))
                for t in range(TT):
                    b = bank[6 + t][:, 0:260].rearrange("p (h d) -> p h d", h=4)
                    den, neg = tiny[:, 20 + 4 * t:24 + 4 * t], tiny[:, 28:32]
                    dve.tensor_copy(den, b[:, :, 64]).then_inc(sem.dve_step, 1)
                    dve.wait_ge(sem.dve_step, me.step())
                    stt(den, den, -1.0, den, MUL, MAX).then_inc(sem.dve_step, 1)
                    dve.wait_ge(sem.dve_step, me.step())
                    tt(den, den, cols[:, 1, t, :], MAX).then_inc(sem.dve_step, 1)
                    dve.wait_ge(sem.dve_step, me.step())
                    dve.reciprocal(den, den).then_inc(sem.dve_step, 1)
                    dve.wait_ge(sem.dve_step, me.step())
                    out_t = m_tmp[:, t, :].rearrange("p (h d) -> p h d", h=4)
                    tt(out_t, b[:, :, 0:64], den.unsqueeze(2).broadcast_to([P, 4, 64]), MUL).then_inc(sem.dve_step, 1)
                    dve.wait_ge(sem.dve_step, me.step())
                    stt(m_tmp[:, t, :], m_o[:, t, :], 1.0, m_tmp[:, t, :], ADD, MUL).then_inc(sem.m_yb, 1)

            def lru_scan():
                dve.wait_ge(sem.lru_sqrt, me.seen("lru_sqrt"))
                ts(l_u, l_r, -1.0, 1.0, MUL, ADD).then_inc(sem.dve_step, 1)
                dve.wait_ge(sem.dve_step, me.step())
                dve.reciprocal(l_u, l_u).then_inc(sem.dve_step, 1)
                dve.wait_ge(sem.dve_step, me.step())
                stt(l_a, l_r, 1.0, l_u, ADD, MUL)
                stt(l_i, l_i, 1.0, xa, ADD, MUL)
                tt(l_s, l_s, l_u, MUL).then_inc(sem.dve_step, 1)
                dve.wait_ge(sem.dve_step, me.step())
                stt(l_i, l_i, 0.5, l_s, MUL, MUL).then_inc(sem.dve_step, 1)
                dve.wait_ge(sem.dve_step, me.step())
                for c in range(2):
                    dve.tensor_tensor_scan(l_s[:, c, :], l_a[:, c, :], l_i[:, c, :], 0.0, MUL, ADD).then_inc(sem.dve_step, 1)
                    dve.wait_ge(sem.dve_step, me.step())
                tt(xa, lru_g, lru_g, MUL).then_inc(sem.dve_step, 1)
                dve.wait_ge(sem.dve_step, me.step())
                ts(xa, xa, 0.044715, 1.0, MUL, ADD).then_inc(sem.dve_step, 1)
                dve.wait_ge(sem.dve_step, me.step())
                tt(xa, xa, lru_g, MUL).then_inc(sem.lru_gelu, 1)
                dve.wait_ge(sem.lru_tg, me.seen("lru_tg"))
                stt(lru_g, xa, 1.0, lru_g, ADD, MUL).then_inc(sem.dve_step, 1)
                dve.wait_ge(sem.dve_step, me.step())
                stt(y[:, 0:2, :], lru_g, 0.5, l_s, MUL, MUL).then_inc(sem.y_a, 1)

            def sb_scores():
                dve.wait_ge(sem.sb_ln, me.seen("sb_ln"))
                for h in range(4):
                    stt(sb_a[:, h, :], bank[4 + h][:, 0:DIAG], 0.0, sb_a[:, h, :], MAX, ADD).then_inc(sem.sb_sp, 1)

            def low_of_branch(b):
                dve.wait_ge(sem.act_h, me.seen("act_h"))
                h_, l_ = branch_of(b)
                tt(flat(l_), flat(y[:, 2 * b:2 * b + 2, :]), f32(flat(h_)), SUB).then_inc(sem.act_hl, 1)

            def merge(b):
                for c in range(2):
                    if c == 0:
                        dve.wait_ge(sem.half_used, me.seen("half_used"))
                    else:
                        dve.wait_ge(sem.w_used, me.used)
                    for t in range(TT):
                        src = me.pair(1 - c)[t]
                        g = gates[:, t, b * D + c * NB:b * D + (c + 1) * NB]
                        share = (xn[:, t, c * NB:(c + 1) * NB], share_1[2 * c + t], share_2[2 * c + t])[b]
                        stt(share, g, 1.0, src[:, :], ADD, MUL).then_inc(sem.merge, 1)
                    if b == 2:
                        if c == 1:
                            turn_merged(0)
                        for t in range(TT):
                            m = xn[:, t, c * NB:(c + 1) * NB]
                            dve.wait_ge(sem.merge, 8 + 2 * c + t + 1)
                            dve.wait_ge(sem.merged_1, 2 * c + t + 1)
                            tt(m, m, share_2[2 * c + t], ADD).then_inc(sem.merged, 1)

            def low_of_bank(q, scale=1.0, b=None):
                dve.wait_ge(sem.act_h, me.seen("act_h"))
                stt(flat(act_l[:, 2 * q:2 * q + 2, :]), (b or bank[4 + q])[:, :], scale,
                    f32(flat(act_h[:, 2 * q:2 * q + 2, :])), MUL, SUB).then_inc(sem.act_hl, 1)

            def turn_merged(c):
                for q in (2 * c, 2 * c + 1):
                    low_of_bank(q, 0.5)

            def x_out():
                for q in range(4):
                    low_of_bank(q)

            def wait_tile(t, split):
                if split and t == 0:
                    dve.wait_ge(sem.tile0_used, me.seen("tile0_used"))
                else:
                    dve.wait_ge(sem.w_used, me.used)

            def add_x(c):
                for t, b in enumerate(me.pair()):
                    wait_tile(t, c == 1)
                    o = x[:, t, c * NB:(c + 1) * NB]
                    tt(o, b[:, :], o, ADD).then_inc(sem.x_ready, 1)

            def add_acc():
                for t in range(TT):
                    wait_tile(t, True)
                    for c in range(2):
                        o = x[:, t, c * NB:(c + 1) * NB]
                        tt(o, bank[4 + 2 * t + c][:, :], o, ADD).then_inc(sem.x_ready, 1)

            def hidden1(c):
                dve.wait_ge(sem.hid_t, me.seen("hid_t"))
                b0, b1 = me.pair()
                stt(h_tmp, h_act, 1.0, b0[:, :], ADD, MUL).then_inc(sem.dve_step, 1)
                dve.wait_ge(sem.dve_step, me.step())
                stt(h_val, h_tmp, 0.5, b1[:, :], MUL, MUL).then_inc(sem.hid_a, 1)
                dve.wait_ge(sem.hid_h, me.seen("hid_h"))
                hh, hl = hidden_of(c, True)
                tt(flat(hl), h_val, f32(flat(hh)), SUB).then_inc(sem.hid_hl, 1)
                dve.wait_ge(sem.hid_hl, me.seen("hid_hl"))

            def hidden2(c):
                for b in range(2):
                    dve.wait_ge(sem.hid_t, me.seen("hid_t"))
                    tt(h_val, h_act, h_act, MUL).then_inc(sem.hid_a, 1)
                    dve.wait_ge(sem.hid_h, me.seen("hid_h"))
                    hl = flat(hid_l[c % 2][:, 2 * b:2 * b + 2, :])
                    tt(hl, h_val, f32(flat(hid_h[c % 2][:, 2 * b:2 * b + 2, :])), SUB).then_inc(sem.hid_hl, 1)
                    dve.wait_ge(sem.hid_hl, me.seen("hid_hl"))

            def za_in():
                dve.wait_ge(sem.za_in, me.seen("za_in", 2))
                for t in range(TT):
                    k = 20 + 6 * t
                    dve.bn_stats(tiny[:, k:k + 6], zg[:, t, T:2 * T]).then_inc(sem.dve_step, 1)
                    dve.wait_ge(sem.dve_step, me.step())
                    dve.bn_aggr(tiny[:, 16 + 2 * t:18 + 2 * t], tiny[:, k:k + 6]).then_inc(sem.ln_stat, 1)

            def ln_apply():
                dve.wait_ge(sem.ln_rstd, me.seen("ln_rstd"))
                dve.wait_ge(sem.ln_in, me.seen("ln_in", 32))
                for t in range(TT):
                    ts(vn[:, t, :], zg[:, t, T:2 * T], tiny[:, 16 + 2 * t:17 + 2 * t], rstd[:, 24 + t:25 + t],
                            SUB, MUL).then_inc(sem.dve_step, 1)
                    dve.wait_ge(sem.dve_step, me.step())
                    tt(vn[:, t, :], vn[:, t, :], ln_g, MUL).then_inc(sem.dve_step, 1)
                    dve.wait_ge(sem.dve_step, me.step())
                    tt(vn[:, t, :], vn[:, t, :], ln_b, ADD).then_inc(sem.vn, 1)

            def spatial():
                dve.wait_ge(sem.mixed, me.seen("mixed"))
                for t in range(TT):
                    for h in range(4):
                        d = slice(h * 64, h * 64 + 64)
                        ins = stt(vn[:, t, d], bank[5][:, t * T + h * 64:t * T + h * 64 + 64], col("b_s_2", h),
                                  zg[:, t, d], ADD, MUL)
                    ins.then_inc(sem.ya2_tok, 1)

            def moba_scores(i):
                if i == 0:
                    dve.wait_ge(sem.dist, me.seen("dist", 2))
                for h in range(4 * i, 4 * i + 4):
                    dve.wait_ge(sem.mo_s, me.seen("mo_s"))
                    stt(sc[:, h, :], dist, 2.0 ** -(h + 1), bank[4 + h % 4][:, 0:DIAG], MUL, ADD)\
                        .then_inc(sem.mo_sc, 1)
                dve.wait_ge(sem.mo_sc, me.seen("mo_sc", 4))
                r = slice(4 * i, 4 * i + 4)
                for t, (a, n) in enumerate(((0, P), (P, 2 * P))):
                    dve.tensor_reduce(neg_max[:, 8 * t + 4 * i:8 * t + 4 * i + 4], sc[:, r, a:a + n], AX.X, MAX,
                                      negate=True).then_inc(sem.mo_max, 1)

            def moba_norm(i):
                dve.wait_ge(sem.mo_p, me.seen("mo_p", 4))
                for t in range(TT):
                    k = 8 * t + 4 * i
                    ins = dve.reciprocal(soft[:, k:k + 4], soft[:, k:k + 4])
                ins.then_inc(sem.dve_step, 1)
                dve.wait_ge(sem.dve_step, me.step())
                for h in range(4 * i, 4 * i + 4):
                    for t, (a, n) in enumerate(((0, P), (P, 2 * P))):
                        k = 8 * t + h
                        ins = ts(sc[:, h, a:a + n], sc[:, h, a:a + n], soft[:, k:k + 1], None, MUL)
                    ins.then_inc(sem.mo_n, 1)

            def zc_in():
                dve.memset(glu[:, :, 0:DW_TAPS - 1], 0.0).then_inc(sem.dve_step, 1)
                dve.wait_ge(sem.dve_step, me.step())
                dve.wait_ge(sem.zc_t, me.seen("zc_t"))
                stt(glu[:, :, DW_TAPS - 1:], in2(cs), 1.0, in2(me.pair()[0][:, :]), ADD, MUL).then_inc(sem.zc_in, 1)
                dve.wait_ge(sem.zc_in, me.seen("zc_in"))

            def conv_dw(first, end):
                conv(cv, glu, range(first, end), lambda j, c: dw[:, 2 * j + c:2 * j + c + 1], 2, 0)

            def conv_bias():
                for c in range(2):
                    ts(cv[:, c, :], cv[:, c, :], 0.5, col("b_dw_2", c), MUL, ADD).then_inc(sem.conv_done, 1)
                dve.wait_ge(sem.conv_done, me.seen("conv_done", 2))

            def group_mean():
                dve.wait_ge(sem.gn_mean, me.seen("gn_mean"))
                tt(cx, flat(cv), bank[6][:, :], SUB).then_inc(sem.dve_step, 1)
                dve.wait_ge(sem.dve_step, me.step())
                tt(cs, cx, cx, MUL).then_inc(sem.gn_sq, 1)

            def group_norm():
                dve.wait_ge(sem.gn_sd, me.seen("gn_sd"))
                dve.reciprocal(cs, cs).then_inc(sem.dve_step, 1)
                dve.wait_ge(sem.dve_step, me.step())
                tt(cx, cx, cs, MUL).then_inc(sem.dve_step, 1)
                dve.wait_ge(sem.dve_step, me.step())
                for c in range(2):
                    a = cx[:, c * T:(c + 1) * T]
                    ts(a, a, col("conv_gn_g_2", c), col("conv_gn_b_2", c), MUL, ADD).then_inc(sem.gn_z, 1)

            def group_silu():
                dve.wait_ge(sem.gn_t, me.seen("gn_t"))
                stt(cx, cs, 1.0, cx, ADD, MUL).then_inc(sem.gn_y, 1)

            def group_norm_low():
                dve.wait_ge(sem.act_h, me.seen("act_h"))
                stt(flat(act_l[:, 6:8, :]), cx, 0.5, f32(flat(act_h[:, 6:8, :])), MUL, SUB).then_inc(sem.act_hl, 1)

            def gain(b, t, c):
                dve.wait_ge(sem.post_sum, me.seen("post_sum"))
                if c == 0 and t == 0:
                    dve.wait_ge(sem.row_in, me.seen("row_in", 16))
                cut = slice(c * NB, (c + 1) * NB)
                tt(xn[:, t, cut], b[:, :], row_g[:, cut], MUL).then_inc(sem.zg, 1)

            def add_normed(i, t):
                dve.wait_ge(sem.zg, me.seen("zg", {2: 2}.get(i, 3 - 2 * t)))
                dve.wait_ge(sem.rstd, me.seen("rstd"))
                k = 2 * (POST + i) + t
                stt(x[:, t, :], xn[:, t, :], rstd[:, k:k + 1], x[:, t, :], MUL, ADD).then_inc(sem.x_ready, 1)

            def post_first():
                for t, b in enumerate(me.pair()):
                    gain(b, t, 0)

            def post_last(i):
                for t, b in enumerate(me.pair()):
                    gain(b, t, 1)
                    add_normed(i, t)

            def post_acc(i):
                for t in range(TT):
                    for c in range(2):
                        gain(bank[4 + 2 * t + c], t, c)
                    add_normed(i, t)

            def x_max(i):
                for h in (2 * i, 2 * i + 1):
                    dve.wait_ge(sem.x_s, me.seen("x_s"))
                    dve.tensor_reduce(neg_max[:, 2 * h:2 * h + 2], in2(bank[4 + h][:, :]), AX.X, MAX, negate=True)\
                        .then_inc(sem.x_max, 1)

            def x_norm(i):
                for h in (2 * i, 2 * i + 1):
                    dve.wait_ge(sem.x_p, me.seen("x_p"))
                    dve.reciprocal(soft[:, 2 * h:2 * h + 2], soft[:, 2 * h:2 * h + 2]).then_inc(sem.dve_step, 1)
                    dve.wait_ge(sem.dve_step, me.step())
                    for t in range(TT):
                        ins = ts(x_p[:, h, t, :], x_p[:, h, t, :], soft[:, 2 * h + t:2 * h + t + 1], None, MUL)
                    ins.then_inc(sem.x_n, 1)

            def ahead_of(key, mode, hold=False):
                for g, _ in me.groups_of(key, mode):
                    if not (hold and g == chunks[key][-1][0]):
                        split_low(g + LEAD + 1)

            setup()
            norm_diag(0)
            split_low(1)
            norm_split(0)
            ahead_of("lru", "C")
            lru_conv()
            vectors()
            ahead_of("qk", "C")
            ahead_of("ifsv", "T")
            if_rows()
            ahead_of("vo", "T")
            ahead_of("sqk", "C")
            mlstm_cols()
            mlstm_qk()
            ahead_of(("gate", 0), "T")
            lru_scan()
            mlstm_scores()
            ahead_of(("gate", 1), "T")
            mlstm_out()
            ahead_of(("gate", 2), "T")
            sb_scores()
            ahead_of(("gate", 3), "T")
            for b in range(2):
                low_of_branch(b)
            ahead_of(("gate", 4), "T")
            norm(3)
            ahead_of(("gate", 5), "T")
            low_of_branch(2)
            for b in range(3):
                ahead_of(("branch", b), "W", hold=b != 1)
                merge(b)
            ahead_of(("wo_top", 0), "T")
            turn_merged(1)
            ahead_of(("wo_top", 1), "T")
            for c in range(2):
                ahead_of(("wo_bottom", c), "T", hold=c == 1)
                add_x(c)
            norm_diag(1)
            split_low(me.used + LEAD)
            norm_split(1)
            n1 = F1 // 256
            for c in range(n1 + 1):
                if c < n1:
                    ahead_of(("up1", c), "C")
                    hidden1(c)
                if c >= 1:
                    ahead_of(("down1", c - 1), "F")
            add_acc()
            final_norm()
            norm_diag(2)
            ahead_of(("kv", 0), "C")
            norm_split(2)
            ahead_of("zc", "C")
            zc_in()
            ahead_of("q2", "C")
            conv_dw(0, 8)
            ahead_of("k2", "C")
            conv_dw(8, 17)
            ahead_of("za", "T")
            moba_scores(0)
            conv_dw(17, 20)
            moba_norm(0)
            ahead_of("v2", "T")
            conv_dw(20, 24)
            za_in()
            moba_scores(1)
            ln_apply()
            conv_dw(24, 28)
            ahead_of(("kv", 1), "C")
            conv_dw(28, DW_TAPS)
            conv_bias()
            moba_norm(1)
            ahead_of(("kv", 2), "T")
            low_of_bank(1, b=bank[4])
            group_mean()
            spatial()
            low_of_bank(0, b=bank[7])
            group_norm()
            ahead_of(("mix_top", 0), "T")
            group_silu()
            group_norm_low()
            ahead_of(("mix_top", 1), "T")
            low_of_bank(2, b=bank[5])
            ahead_of(("mix_bottom", 0), "T")
            post_first()
            ahead_of(("mix_bottom", 1), "T")
            post_last(0)
            norm_diag(4)
            ahead_of(("kv", 3), "T")
            norm_split(4)
            for c in range(2):
                ahead_of(("xq", c), "C")
            for i in range(2):
                x_max(i)
                x_norm(i)
            x_out()
            ahead_of(("xo", 0), "T")
            post_first()
            ahead_of(("xo", 1), "T", hold=True)
            post_last(1)
            norm_diag(5)
            split_low(me.used + LEAD)
            norm_split(5)
            n2 = F2 // NB
            for c in range(n2 + 1):
                if c < n2:
                    ahead_of(("up2", c), "C")
                    hidden2(c)
                if c >= 1:
                    ahead_of(("down2", c - 1), "F")
            post_acc(2)

        @block.tensor
        def _(pe):
            me = Count()

            def mm(dst, lhs, rhs, start=True, stop=True, loose=True):
                return pe.matmul(dst, lhs, rhs, start=start, stop=stop, skip_group_check=loose)

            def mm3(dst, lhs_h, lhs_l, rhs_h, rhs_l, start, stop):
                mm(dst, lhs_l, rhs_h, start, False)
                mm(dst, lhs_h, rhs_l, False, False)
                return mm(dst, lhs_h, rhs_h, False, stop)

            def products(key, mode, c=0, width=NB, fresh=False, tile0=False, first=True, last=True, kt0=0, is_mem=False,
                         between=None, back_first=False):
                parity = me.pairs % 2
                ids = chunks[key]
                n_kt = sum(len(kts) for _, kts in ids)
                for g, kts in me.groups_of(key, mode):
                    if between and kts[0]:
                        between()
                    pe.wait_ge(low_sem(g), before(g))
                    wh, wl = part(high, g), part(low, g)
                    by_tile = tile0 and kts[-1] == n_kt - 1
                    tiles = list(enumerate(kts))
                    if back_first:
                        tiles = tiles[2:] + tiles[:2]
                    order = [(j, kt, t) for j, kt in tiles for t in range(TT)]
                    if by_tile:
                        order = [(j, kt, t) for t in range(TT) for j, kt in tiles]
                    for j, kt, t in order:
                        s0 = kt == 0 and first
                        s1 = kts[-1] == n_kt - 1 and kt == tiles[-1][1] and last
                        tok = slice(t * P, (t + 1) * P)
                        if fresh and t == 0 and kt % 2 == 0:
                            pe.wait_ge(sem.act_hl, me.seen("act_hl"))
                        if mode == "F":
                            in_h, in_l = (half[:, kt, :] for half in hidden_of(c, key[0] == "down1"))
                        else:
                            in_h, in_l = split_of(kt0 + kt, is_mem)
                        if mode == "T":
                            ins = mm3(bank[2 * parity + t][:, 0:width], in_h[:, tok], in_l[:, tok],
                                      wh[:, j, 0:width], wl[:, j, 0:width], s0, s1)
                        elif mode == "C":
                            for i in (2 * t, 2 * t + 1):
                                ch = slice(i * P, (i + 1) * P)
                                o = (i % 2) * T
                                ins = mm3(bank[2 * parity + i // 2][:, o:o + T], wh[:, j, ch], wl[:, j, ch],
                                          in_h, in_l, s0 and o == 0, s1)
                        else:
                            for n in range(2):
                                ins = mm3(bank[4 + 2 * t + n][:, :], in_h[:, tok], in_l[:, tok],
                                          wh[:, j, n * NB:(n + 1) * NB], wl[:, j, n * NB:(n + 1) * NB], s0, s1)
                        if by_tile and t == 0 and s1:
                            ins.then_inc(sem.tile0_used, 1)
                    ins.then_inc(sem.w_used, 1)

            def branch_products(b):
                parity = me.pairs % 2
                for g, kts in me.groups_of(("branch", b), "W"):
                    pe.wait_ge(low_sem(g), before(g))
                    wh, wl = part(high, g), part(low, g)
                    for n in range(2):
                        if b:
                            pe.wait_ge(sem.merge, 4 * (b - 1) + 2 * n + 2)
                        elif n:
                            pe.wait_ge(sem.gate_in, 12)
                        cut = slice(n * NB, (n + 1) * NB)
                        for t in range(TT):
                            tok = slice(t * P, (t + 1) * P)
                            for kt in kts:
                                in_h, in_l = branch_of(b)
                                ins = mm3(bank[2 * ((parity + n) % 2) + t][:, :], in_h[:, kt, tok], in_l[:, kt, tok],
                                          wh[:, kt, cut], wl[:, kt, cut], kt == 0, kt == kts[-1])
                        ins.then_inc((sem.half_used, sem.w_used)[n], 1)

            def turn(dst, src):
                n = src.shape[0]
                return pe.transpose(dst, src, ident[0:n, 0:n])

            def keep_warm(n, spare=5):
                for i in range(n):
                    mm(bank[spare][:, 0:P], ident[:, :], ident[:, :])

            def gain_0():
                pe.wait_ge(sem.ident, me.seen("ident"))
                pe.wait_ge(sem.gain_in, 16)
                turn(bank[4][:, 0:KD], vec_rows[0:KD, :]).then_inc(sem.gain_turned, 1)
                keep_warm(WARM[0])
                pe.wait_ge(sem.vec_out, me.seen("vec_out"))

            def vectors():
                pe.wait_ge(sem.vec_in, 16 * (len(VEC_A) - 1))
                turn(bank[4][:, 0:VEC_ROWS], vec_rows[0:VEC_ROWS, :]).then_inc(sem.vec_turned, 1)
                pe.wait_ge(sem.dw_in, me.seen("dw_in", 16))
                turn(bank[4][:, P:P + DW_ROWS], dw_rows[0:DW_ROWS, :]).then_inc(sem.vec_turned, 1)

            def turn_merged(c):
                pe.wait_ge(sem.merged, 2 * c + 2)
                pe.wait_ge(sem.y_c, 1)
                for q in (2 * c, 2 * c + 1):
                    for k in range(2):
                        for t in range(TT):
                            kt = 2 * q + k
                            ins = turn(bank[4 + q][:, k * T + t * P:k * T + (t + 1) * P], xn[:, t, kt * P:(kt + 1) * P])
                    ins.then_inc(sem.turned, 1)

            def norm(src=x):
                for t in range(TT):
                    pe.wait_ge(sem.diag, me.seen("diag"))
                    for kt in range(KD):
                        o = (kt % 2) * T + t * P
                        ins = mm(bank[4 + kt // 2][:, o:o + P], src[:, t, kt * P:(kt + 1) * P], diag[:, t, :])
                        if t == 1 and kt % 2:
                            ins.then_inc(sem.turned, 1)

            def if_rows():
                pe.wait_ge(sem.ifsv_in, 2)
                for k in range(2):
                    for t in range(TT):
                        ins = turn(bank[6][0:4, k * T + t * P:k * T + (t + 1) * P], if_tok[:, t, 4 * k:4 * k + 4])
                ins.then_inc(sem.if_turned, 1)

            def lru_gates():
                pe.wait_ge(sem.lru_conv, me.seen("lru_conv", 2))
                pe.wait_ge(sem.gate_w, me.seen("gate_w", 16 * 8))
                for i in range(2):
                    for c in range(2):
                        ins = mm(bank[4 + i][:, c * T:(c + 1) * T], gate_w[i][:, c, :], xa[:, c, :])
                ins.then_inc(sem.lru_z, 1)

            def mlstm_cols():
                pe.wait_ge(sem.exp_m, me.seen("exp_m"))
                for k, r in enumerate((1, 5)):
                    for t in range(TT):
                        o = 8 * k + 4 * t
                        ins = turn(bank[7][:, o:o + 4], rows[0:4, r, t * P:(t + 1) * P])
                ins.then_inc(sem.cols_turned, 1)
                pe.wait_ge(sem.consts, me.seen("consts", 5))
                pe.wait_ge(sem.lru_t, 2)
                for h in range(4):
                    ins = mm(bank[4 + h // 2][:, (h % 2) * T:(h % 2 + 1) * T], head_row[0:4, h, :], rows[0:4, 4, :])
                    if h % 2:
                        ins.then_inc(sem.m_bc, 1)

            def scores(dst, q, k, h):
                p_ = slice(64 * (h % 2), 64 * (h % 2) + 64)
                mm(dst[:, 0:T], k[p_, h // 2, 0:P], q[p_, h // 2, :])
                return mm(dst[:, T:DIAG], k[p_, h // 2, P:T], q[p_, h // 2, P:T], start=False)

            def mlstm_scores():
                pe.wait_ge(sem.m_qk, me.seen("m_qk"))
                pe.wait_ge(sem.m_e, me.seen("m_e", 8))
                pe.wait_ge(sem.cols, me.seen("cols"))
                for h in range(4):
                    scores(bank[(6, 7, 4, 5)[h]], m_qk[:, 0], m_qk[:, 1], h).then_inc(sem.m_s, 1)

            def mlstm_out():
                pe.wait_ge(sem.m_p, me.seen("m_p", 4))
                pe.wait_ge(sem.vo_in, 2)
                for h in range(4):
                    o = slice(65 * h, 65 * h + 65)
                    mm(bank[6][:, o], m_e[:, h, 0:P], m_v[:, 0, h, :], start=h == 0)
                    mm(bank[7][:, o], m_e[:, h, P:T], m_v[:, 0, h, :], start=h == 0, stop=False)
                    ins = mm(bank[7][:, o], m_e[:, h, T:DIAG], m_v[:, 1, h, :], start=False)
                ins.then_inc(sem.m_y, 1)

            def turn_256(dst, src):
                for c in range(2):
                    for t in range(TT):
                        ins = turn(dst[:, c * T + t * P:c * T + (t + 1) * P], src[:, t, c * P:(c + 1) * P])
                return ins

            def mlstm_turn():
                pe.wait_ge(sem.m_yb, me.seen("m_yb", 2))
                turn_256(bank[4], m_tmp).then_inc(sem.m_turned, 1)

            def sb_scores():
                pe.wait_ge(sem.sqk_in, 2)
                for h in (1, 2, 3, 0):
                    if h == 0:
                        pe.wait_ge(sem.y_b, me.seen("y_b"))
                    scores(bank[4 + h], s_q, s_k, h).then_inc(sem.sb_z, 1)

            def sb_sums():
                pe.wait_ge(sem.sb_masked, me.seen("sb_masked", 2))
                pe.wait_ge(sem.sb_sp, me.seen("sb_sp", 4))
                for h in range(4):
                    b, a = bank[4 + h], sb_a[:, h, :]
                    mm(b[:, 0:T], neg_tri, a[:, 0:T], start=False)
                    mm(b[:, P:T], neg_one, a[:, T:DIAG], start=False)
                    mm(b[:, T:DIAG], neg_tri, a[:, T:DIAG], start=False).then_inc(sem.sb_sum, 1)

            def weighted(dst, v, p, h, hh, start):
                q = slice(64 * (h % 2), 64 * (h % 2) + 64)
                d = slice(64 * h, 64 * h + 64)
                mm(dst[q, 0:T], v[:, 0, d], p[:, hh, 0:T], start=start, stop=False)
                return mm(dst[q, P:T], v[:, 1, d], p[:, hh, T:DIAG], start=False)

            def sb_out():
                pe.wait_ge(sem.sb_a_masked, me.seen("sb_a_masked", 2))
                pe.wait_ge(sem.sb_a, me.seen("sb_a", 4))
                for h in (0, 1, 2, 3):
                    ins = weighted(bank[4][:, (h // 2) * T:(h // 2 + 1) * T], s_v, sb_a, h, h, h < 2)
                ins.then_inc(sem.sb_o, 1)


            def spatial_w_turn():
                pe.wait_ge(sem.ws_masked, me.seen("ws_masked"))
                for h in range(4):
                    ins = turn(bank[7][:, h * P:(h + 1) * P], spatial_w[:, h, :])
                ins.then_inc(sem.ws_turned, 1)

            def moba_scores(i):
                if i == 1:
                    pe.wait_ge(sem.mo_sc, me.seen("mo_sc", 4))
                for h in range(4 * i, 4 * i + 4):
                    if h == 3:
                        pe.wait_ge(sem.ws_out, me.seen("ws_out"))
                    q = slice(64 * (h % 2), 64 * (h % 2) + 64)
                    b = bank[4 + h % 4]
                    mm(b[:, 0:P], q2[q, h // 2, 0:P], k2[q, h // 2, 0:P])
                    mm(b[:, P:DIAG], q2[q, h // 2, P:T], k2[q, h // 2, :], start=False).then_inc(sem.mo_s, 1)

            def moba_turn(i, heads=range(4)):
                for h in heads:
                    pe.wait_ge(sem.mo_n, me.seen("mo_n"))
                    for k in range(3):
                        ins = turn(bank[TURN_BANK[i][h]][:, k * P:(k + 1) * P], sc[:, 4 * i + h, k * P:(k + 1) * P])
                    ins.then_inc(sem.mo_turned, 1)

            def moba_values(i, b):
                for h in range(4):
                    ins = weighted(b[:, (h // 2) * T:(h // 2 + 1) * T], v2, pt, 4 * i + h, h, h < 2)
                ins.then_inc(sem.mo_o, 1)

            def spatial():
                pe.wait_ge(sem.vn, me.seen("vn", 2))
                for t in range(TT):
                    for h in range(4):
                        o = t * T + h * 64
                        ins = mm(bank[5][:, o:o + 64], spatial_t[:, h, :], vn[:, t, h * 64:h * 64 + 64])
                ins.then_inc(sem.mixed, 1)

            def group_mean():
                pe.wait_ge(sem.conv_done, me.seen("conv_done", 2))
                mm(bank[6][:, :], block_mean[:, :], flat(cv)).then_inc(sem.gn_mean, 1)

            def group_var():
                mm(bank[4][:, :], block_mean[:, :], cs).then_inc(sem.gn_var, 1)

            def x_scores(i):
                for h in (2 * i, 2 * i + 1):
                    pe.wait_ge(sem.xq_in, 2 + 2 * (h // 2))
                    for t in range(TT):
                        for k in range(2):
                            ins = mm(bank[4 + h][:, t * T:(t + 1) * T], x_q[:, 2 * h + k, t * P:(t + 1) * P],
                                     k_mem[:, 2 * h + k, :], start=k == 0, stop=k == 1)
                    ins.then_inc(sem.x_s, 1)

            def x_turn(i):
                for h in (2 * i, 2 * i + 1):
                    pe.wait_ge(sem.x_n, me.seen("x_n"))
                    for m in range(2):
                        for t in range(TT):
                            ins = turn(bank[4 + h][:, m * T + t * P:m * T + (t + 1) * P],
                                       x_p[:, h, t, m * P:(m + 1) * P])
                    ins.then_inc(sem.x_turned, 1)

            def x_out(i):
                pe.wait_ge(sem.x_t, me.seen("x_t", 2))
                for h in (2 * i, 2 * i + 1):
                    for c in range(2):
                        for m in range(2):
                            ch = slice((2 * h + c) * P, (2 * h + c + 1) * P)
                            ins = mm(bank[4 + h][:, c * T:(c + 1) * T], v_mem[:, m, ch], x_pt[:, h, m, :],
                                     start=m == 0, stop=m == 1)
                    ins.then_inc(sem.x_o, 1)

            gain_0()
            norm()
            keep_warm(WARM[0], 0)
            products("lru", "C", fresh=True)
            vectors()
            products("qk", "C")
            pe.wait_ge(sem.lru_in, 2)
            products("ifsv", "T", width=264)
            if_rows()
            pe.wait_ge(sem.qk_in, 2)
            products("vo", "T")
            lru_gates()
            pe.wait_ge(sem.ifsv_in, 2)
            products("sqk", "C")
            mlstm_cols()
            pe.wait_ge(sem.vo_in, 2)
            products(("gate", 0), "T")
            mlstm_scores()
            pe.wait_ge(sem.sqk_in, 2)
            products(("gate", 1), "T")
            mlstm_out()
            pe.wait_ge(sem.gate_in, 2)
            products(("gate", 2), "T")
            mlstm_turn()
            sb_scores()
            pe.wait_ge(sem.gate_in, 4)
            products(("gate", 3), "T")
            sb_sums()
            pe.wait_ge(sem.gate_in, 6)
            products(("gate", 4), "T")
            pe.wait_ge(sem.sb_a, 4)
            norm(mem)
            pe.wait_ge(sem.act_hl, me.seen("act_hl", 3))
            sb_out()
            pe.wait_ge(sem.gate_in, 8)
            products(("gate", 5), "T")
            for b in range(3):
                if b == 2:
                    pe.wait_ge(sem.act_hl, me.seen("act_hl", 4))
                branch_products(b)
            for c in range(2):
                turn_merged(c)
                pe.wait_ge(sem.merge, 10 + 2 * c)
                products(("wo_top", c), "T", fresh=c == 0, last=False)
            for c in range(2):
                products(("wo_bottom", c), "T", kt0=4, fresh=c == 0, tile0=c == 1, first=False)
            norm()
            n1 = F1 // 256
            for c in range(n1 + 1):
                if c < n1:
                    if c >= 2:
                        pe.wait_ge(sem.hid_a, c - 1)
                    products(("up1", c), "C", fresh=c == 0)
                if c >= 1:
                    pe.wait_ge(sem.hid_hl, c)
                    products(("down1", c - 1), "F", c - 1, tile0=c == n1, first=c == 1, last=c == n1)
            products(("kv", 0), "C", is_mem=True)
            norm()
            products("zc", "C", fresh=True)
            pe.wait_ge(sem.kv_in, 2)
            products("q2", "C")
            pe.wait_ge(sem.zc_in, 1)
            products("k2", "C")
            spatial_w_turn()
            pe.wait_ge(sem.qk2_in, 3)
            moba_scores(0)
            products("za", "T")
            pe.wait_ge(sem.qk2_in, 4)
            moba_scores(1)
            products("v2", "T")
            pe.wait_ge(sem.mo_sc, me.seen("mo_sc", 4))
            moba_turn(0)
            pe.wait_ge(sem.za_in, 2)
            products(("kv", 1), "C", is_mem=True)
            pe.wait_ge(sem.v2_in, 2)
            pe.wait_ge(sem.mo_t, me.seen("mo_t", 4))
            moba_values(0, bank[4])
            spatial()
            group_mean()
            products(("kv", 2), "T", is_mem=True)
            pe.wait_ge(sem.ya2_tok, me.seen("ya2_tok", 2))
            turn_256(bank[7], vn).then_inc(sem.ya2_turned, 1)
            pe.wait_ge(sem.gn_sq, me.seen("gn_sq"))
            pe.wait_ge(sem.act_hl, me.seen("act_hl"))
            group_var()
            moba_turn(1, (0, 1))
            pe.wait_ge(sem.act_hl, me.seen("act_hl"))
            pe.wait_ge(sem.kv_in, 4)
            products(("mix_top", 0), "T", last=False)
            pe.wait_ge(sem.gn_sd, 1)
            moba_turn(1, (2, 3))
            pe.wait_ge(sem.kv_in, 6)
            products(("mix_top", 1), "T", last=False)
            pe.wait_ge(sem.mo_t, me.seen("mo_t", 4))
            moba_values(1, bank[5])
            for c in range(2):
                products(("mix_bottom", c), "T", kt0=4, fresh=c == 0, tile0=c == 1, first=False, back_first=c == 0)
            pe.wait_ge(sem.zg, 2)
            products(("kv", 3), "T", is_mem=True)
            norm()
            products(("xq", 0), "C", fresh=True)
            pe.wait_ge(sem.kv_in, 8)
            products(("xq", 1), "C", between=lambda: x_scores(0))
            x_turn(0)
            x_scores(1)
            x_out(0)
            x_turn(1)
            x_out(1)
            for c in range(2):
                products(("xo", c), "T", fresh=c == 0, tile0=c == 1)
            keep_warm(WARM[1])
            norm()
            n2 = F2 // NB
            for c in range(n2 + 1):
                if c < n2:
                    if c >= 2:
                        pe.wait_ge(sem.hid_a, F1 // 256 + 2 * (c - 1))
                    products(("up2", c), "C", fresh=c == 0)
                if c >= 1:
                    pe.wait_ge(sem.hid_hl, F1 // 256 + 2 * c)
                    products(("down2", c - 1), "F", c - 1, tile0=c == n2, first=c == 1, last=c == n2)


_INS = ["x", "norm_mix_g", "w_in", "conv_lru_w", "lru_wa", "lru_ba", "lru_wx", "lru_bx", "lru_lambda",
        "conv_mlstm_w", "mlstm_ig_b", "mlstm_fg_b", "w_out_lru", "w_out_mlstm", "w_out_sb", "w_o", "norm_ffn_g",
        "w_ffn_in", "w_ffn_out", "final_norm_g", "mem_2", "pre_mix_g_2", "w_in_2", "gate_ln_g_2", "gate_ln_b_2",
        "w_s_2", "b_s_2", "w_dw_2", "b_dw_2", "conv_gn_g_2", "conv_gn_b_2", "w_out_2", "post_mix_g_2", "pre_x_g_2",
        "mem_g_2", "w_xq_2", "w_xkv_2", "w_xo_2", "post_x_g_2", "pre_ffn_g_2", "w_ff1_2", "w_ff2_2", "post_ffn_g_2"]
_FLAT = {name for name, _ in VEC_A} | {"w_dw_2"}


def kernel(**inputs):
    import numpy as _np
    import concourse.bacc as _bacc
    from concourse.bass_utils import run_bass_kernel_spmd as _run

    nc = _bacc.Bacc("TRN2", target_bir_lowering=False, num_devices=1)
    arrays, args = {}, {}
    for name in _INS:
        a = _np.ascontiguousarray(inputs[name])
        if a.ndim > 1 and a.shape[0] == 1:
            a = a[0]
        if name in _FLAT:
            a = a.reshape(-1)
        arrays[f"in_{name}_dram"] = a
        args[name] = nc.dram_tensor(f"in_{name}_dram", a.shape, mybir.dt.from_np(a.dtype), kind="ExternalInput").ap()
    out = nc.dram_tensor("out_0_dram", (T, D), F32, kind="ExternalOutput").ap()
    two_blocks(nc, args, out)
    r = _run(nc, [arrays], core_ids=[0])
    return r.results[0]["out_0_dram"].reshape(1, T, D)
```
